# Optimizing a Trainium2 kernel written in Bass

```python
import jax, jax.numpy as jnp
from jax import lax
import numpy as np

D_MODEL = 1024
BATCH = 1
SEQ = 1024
DEPTH = 1

GLA_HEADS = 4
GLA_KEY = D_MODEL // 2
GLA_VAL = D_MODEL
GLA_DK = GLA_KEY // GLA_HEADS
GLA_DV = GLA_VAL // GLA_HEADS
GLA_GATE_RANK = 16
GLA_GATE_NORM = 16.0
GLA_CHUNK = 64
GLA_NORM_EPS = 1e-5

RWKV_HEAD = 64
RWKV_DIM = D_MODEL
RWKV_HEADS = RWKV_DIM // RWKV_HEAD
DECAY_LORA = 64
AAA_LORA = 64
GATE_LORA = 128
RWKV_GN_EPS = 64e-5

D_FF = 4 * D_MODEL
NORM_EPS = 1e-6

GLA_SIZES = (GLA_KEY, GLA_KEY, GLA_VAL, GLA_VAL, GLA_GATE_RANK)
RWKV_SIZES = (RWKV_DIM, RWKV_DIM, RWKV_DIM, DECAY_LORA, AAA_LORA, GATE_LORA)
GATE_SIZES = (D_MODEL, D_MODEL)
GLA_WIDTH = 2 * GLA_KEY + 2 * GLA_VAL + GLA_GATE_RANK
RWKV_WIDTH = 3 * RWKV_DIM + DECAY_LORA + AAA_LORA + GATE_LORA
IN_WIDTH = GLA_WIDTH + RWKV_WIDTH + 2 * D_MODEL

kernel_name = "gla_rwkv7_gated_hybrid_block"

def _split(t, sizes):
    out, off = [], 0
    for s in sizes:
        out.append(t[..., off:off + s])
        off += s
    return out

def _rmsnorm(x, g):
    xf = x.astype(jnp.float32)
    y = xf * lax.rsqrt(jnp.mean(xf * xf, axis=-1, keepdims=True) + NORM_EPS)
    return (y * g.astype(jnp.float32)).astype(x.dtype)

def _token_shift(z):
    return jnp.pad(z[:, :-1], ((0, 0), (1, 0), (0, 0)))

def _gla_chunked(q, k, v, log_a):
    B, S, H, DK = q.shape
    DV = v.shape[-1]
    C = GLA_CHUNK
    N = S // C
    q = q.reshape(B, N, C, H, DK) * (DK ** -0.5)
    k = k.reshape(B, N, C, H, DK)
    v = v.reshape(B, N, C, H, DV)
    b = jnp.cumsum(log_a.reshape(B, N, C, H, DK), axis=2)
    b_mid = b[:, :, C // 2 - 1:C // 2]
    scores = jnp.einsum('bnthk,bnshk->bnhts', q * jnp.exp(b - b_mid), k * jnp.exp(b_mid - b))
    causal = jnp.tril(jnp.ones((C, C), dtype=bool))
    scores = jnp.where(causal, scores, 0.0)
    o_intra = jnp.einsum('bnhts,bnshv->bnthv', scores, v)
    b_last = b[:, :, -1:]
    q_dec = q * jnp.exp(b)
    k_dec = k * jnp.exp(b_last - b)
    chunk_decay = jnp.exp(b_last[:, :, 0])

    def step(state, inp):
        qd, kd, vc, dec = inp
        o = jnp.einsum('bthk,bhkv->bthv', qd, state)
        state = state * dec[..., None] + jnp.einsum('bthk,bthv->bhkv', kd, vc)
        return state, o

    state0 = jnp.zeros((B, H, DK, DV), jnp.float32)
    xs = (jnp.moveaxis(q_dec, 1, 0), jnp.moveaxis(k_dec, 1, 0), jnp.moveaxis(v, 1, 0), jnp.moveaxis(chunk_decay, 1, 0))
    _, o_inter = lax.scan(step, state0, xs)
    o = o_intra + jnp.moveaxis(o_inter, 0, 1)
    return o.reshape(B, S, H, DV)

def _rwkv7_scan(r, w, k, v, a_, b_):
    B, S, H, N = r.shape

    def step(state, inp):
        rt, wt, kt, vt, at, bt = inp
        sa = jnp.einsum('bhvk,bhk->bhv', state, at)
        state = state * wt[:, :, None, :] + sa[..., None] * bt[:, :, None, :] + vt[..., None] * kt[:, :, None, :]
        y = jnp.einsum('bhvk,bhk->bhv', state, rt)
        return state, y

    state0 = jnp.zeros((B, H, N, N), jnp.float32)
    xs = tuple(jnp.moveaxis(t, 1, 0) for t in (r, w, k, v, a_, b_))
    _, y = lax.scan(step, state0, xs)
    return jnp.moveaxis(y, 0, 1)

def setup_inputs(seed: int = 0) -> dict:
    key = jax.random.key(seed)
    ks = jax.random.split(key, 32)
    f32 = jnp.float32
    L, D = DEPTH, D_MODEL

    def nrm(k, shape, scale):
        return jax.random.normal(k, shape, f32) * scale

    return {
        "x": jax.random.normal(ks[0], (BATCH, SEQ, D), f32),
        "norm_mix": 1.0 + nrm(ks[1], (L, D), 0.05),
        "w_in": nrm(ks[2], (L, D, IN_WIDTH), D ** -0.5),
        "gla_a_w2": nrm(ks[3], (L, GLA_GATE_RANK, GLA_KEY), GLA_GATE_RANK ** -0.5),
        "gla_a_b": 0.5 + nrm(ks[4], (L, GLA_KEY), 0.1),
        "gla_norm": 1.0 + nrm(ks[5], (L, GLA_DV), 0.05),
        "rwkv_mu": jax.random.uniform(ks[6], (L, RWKV_WIDTH), f32, 0.0, 1.0),
        "rwkv_w0": -1.0 + nrm(ks[7], (L, RWKV_DIM), 0.5),
        "rwkv_w_w2": nrm(ks[8], (L, DECAY_LORA, RWKV_DIM), 0.5 * DECAY_LORA ** -0.5),
        "rwkv_a0": nrm(ks[9], (L, RWKV_DIM), 0.3),
        "rwkv_a_w2": nrm(ks[10], (L, AAA_LORA, RWKV_DIM), AAA_LORA ** -0.5),
        "rwkv_g_w2": nrm(ks[11], (L, GATE_LORA, RWKV_DIM), GATE_LORA ** -0.5),
        "rwkv_k_k": 0.85 + nrm(ks[12], (L, RWKV_DIM), 0.05),
        "rwkv_k_a": 1.0 + nrm(ks[13], (L, RWKV_DIM), 0.05),
        "rwkv_r_k": nrm(ks[14], (L, RWKV_HEADS, RWKV_HEAD), 0.1),
        "rwkv_ln_w": 1.0 + nrm(ks[15], (L, RWKV_DIM), 0.05),
        "rwkv_ln_b": nrm(ks[16], (L, RWKV_DIM), 0.02),
        "w_branch_gla": nrm(ks[17], (L, GLA_VAL, D), GLA_VAL ** -0.5),
        "w_branch_rwkv": nrm(ks[18], (L, RWKV_DIM, D), RWKV_DIM ** -0.5),
        "w_out": nrm(ks[19], (L, D, D), D ** -0.5),
        "norm_mlp": 1.0 + nrm(ks[20], (L, D), 0.05),
        "w_up": nrm(ks[21], (L, D, D_FF), D ** -0.5),
        "w_down": nrm(ks[22], (L, D_FF, D), D_FF ** -0.5),
        "norm_final": 1.0 + nrm(ks[23], (D,), 0.05),
    }

def reference(x, norm_mix, w_in, gla_a_w2, gla_a_b, gla_norm, rwkv_mu, rwkv_w0, rwkv_w_w2,
              rwkv_a0, rwkv_a_w2, rwkv_g_w2, rwkv_k_k, rwkv_k_a, rwkv_r_k, rwkv_ln_w, rwkv_ln_b,
              w_branch_gla, w_branch_rwkv, w_out, norm_mlp, w_up, w_down, norm_final):
    f32 = jnp.float32
    B, S, _ = x.shape
    for l in range(DEPTH):
        h = _rmsnorm(x, norm_mix[l])
        proj = h @ w_in[l]
        gla_p, rwkv_p, gate_p = _split(proj, (GLA_WIDTH, RWKV_WIDTH, 2 * D_MODEL))

        g_q, g_k, g_v, g_og, g_al = _split(gla_p.astype(f32), GLA_SIZES)
        log_a = jax.nn.log_sigmoid(g_al @ gla_a_w2[l].astype(f32) + gla_a_b[l].astype(f32)) / GLA_GATE_NORM
        o = _gla_chunked(g_q.reshape(B, S, GLA_HEADS, GLA_DK),
                         g_k.reshape(B, S, GLA_HEADS, GLA_DK),
                         g_v.reshape(B, S, GLA_HEADS, GLA_DV),
                         log_a.reshape(B, S, GLA_HEADS, GLA_DK))
        o = o * lax.rsqrt(jnp.mean(o * o, axis=-1, keepdims=True) + GLA_NORM_EPS) * gla_norm[l].astype(f32)
        y_gla = (o.reshape(B, S, GLA_VAL) * jax.nn.silu(g_og)).astype(x.dtype)

        z = rwkv_p.astype(f32)
        z = z + (_token_shift(z) - z) * rwkv_mu[l].astype(f32)
        r, k, v, wl, al, gl = _split(z, RWKV_SIZES)
        w = -jax.nn.softplus(-(rwkv_w0[l].astype(f32) + jnp.tanh(wl) @ rwkv_w_w2[l].astype(f32))) - 0.5
        decay = jnp.exp(-jnp.exp(w))
        a = jax.nn.sigmoid(rwkv_a0[l].astype(f32) + al @ rwkv_a_w2[l].astype(f32))
        gate = jax.nn.sigmoid(gl) @ rwkv_g_w2[l].astype(f32)
        hs = (B, S, RWKV_HEADS, RWKV_HEAD)
        kk = (k * rwkv_k_k[l].astype(f32)).reshape(hs)
        kk = kk / jnp.maximum(jnp.linalg.norm(kk, axis=-1, keepdims=True), 1e-12)
        k = k * (1.0 + (a - 1.0) * rwkv_k_a[l].astype(f32))
        r4, k4, v4 = r.reshape(hs), k.reshape(hs), v.reshape(hs)
        a4 = a.reshape(hs)
        y = _rwkv7_scan(r4, decay.reshape(hs), k4, v4, -kk, kk * a4)
        mu = jnp.mean(y, axis=-1, keepdims=True)
        var = jnp.mean(jnp.square(y - mu), axis=-1, keepdims=True)
        y = ((y - mu) * lax.rsqrt(var + RWKV_GN_EPS)).reshape(B, S, RWKV_DIM)
        y = y * rwkv_ln_w[l].astype(f32) + rwkv_ln_b[l].astype(f32)
        bonus = jnp.sum(r4 * k4 * rwkv_r_k[l].astype(f32), axis=-1, keepdims=True) * v4
        y_rwkv = ((y + bonus.reshape(B, S, RWKV_DIM)) * gate).astype(x.dtype)

        ga, gb = _split(gate_p, GATE_SIZES)
        mixed = jax.nn.sigmoid(ga) * (y_gla @ w_branch_gla[l]) + jax.nn.sigmoid(gb) * (y_rwkv @ w_branch_rwkv[l])
        x = x + (mixed @ w_out[l]).astype(x.dtype)

        h2 = _rmsnorm(x, norm_mlp[l])
        x = x + (jnp.square(jax.nn.relu(h2 @ w_up[l])) @ w_down[l]).astype(x.dtype)
    return _rmsnorm(x, norm_final)


_drawn_inputs = setup_inputs


def setup_inputs(seed=0):
    import zlib

    import numpy as np

    out = dict(_drawn_inputs(seed))
    spreads = {}
    factors = {'gla_a_b': 3.564,
     'gla_norm': 3.329,
     'rwkv_w_w2': 3.047,
     'rwkv_k_k': 8.0,
     'rwkv_k_a': 3.264,
     'rwkv_ln_w': 3.95,
     'rwkv_ln_b': 8.0}
    for name, (base, spread) in spreads.items():
        noise = np.random.default_rng([zlib.crc32(name.encode()), seed]).standard_normal(out[name].shape)
        drawn = base * np.exp(spread * noise) if base else spread * noise
        out[name] = __import__('jax').numpy.asarray(drawn.astype(out[name].dtype))
    for name, factor in factors.items():
        out[name] = (out[name] * factor).astype(out[name].dtype)
    return out
```

```python
from contextlib import ExitStack

import concourse.bass as bass
from concourse import mybir

P = 128
F32 = mybir.dt.float32
U32 = mybir.dt.uint32
ALU = mybir.AluOpType
ACT = mybir.ActivationFunctionType

D = 1024
SEQ = 1024
KT = D // P
HALF = 512
CHUNK = 128
NC = HALF // CHUNK
GLA_HEADS, GLA_DK, GLA_DV = 4, 128, 256
RANK = 16
RWKV_PAIRS = 8
HEAD = 64
LEVELS = 6
FF_GROUPS, FF_TILES = 4, 8
NORM_EPS, GLA_EPS, GN_EPS = 1e-6, 1e-5, 64e-5
DECAY = 0.6065306597126334
MU_R, MU_K, MU_V, W0, A0, K_K, K_A, R_K, LN_W, LN_B = range(10)
NPAR = 10


class Steps:

    def __init__(self, nc, sems, name, names):
        self.sem = sems.enter_context(nc.semaphore(name))
        self.names = {x: n for n, x in enumerate(names)}
        self.n = len(names)
        assert len(self.names) == self.n
        self.at = 0

    def start(self, eng):
        eng.sem_inc(self.sem, self.n)

    def done(self, ins, name):
        assert self.names[name] == self.at, (name, self.at)
        self.at = (self.at + 1) % self.n
        ins.then_inc(self.sem, 1)

    def need(self, eng, name, unit):
        eng.wait_ge(self.sem, unit * self.n + (self.n + self.names[name] + 1))

    def need_before(self, eng, name, unit):
        eng.wait_ge(self.sem, unit * self.n + (self.names[name] + 1))


def _prepare(nc, sems, d, hT, cst):
    ident = cst["ident"]
    with ExitStack() as ctx:
        sb = lambda n, s: ctx.enter_context(nc.sbuf_tensor(n, s, F32))
        x = sb("p_x", [P, KT, D])
        junk = sb("p_junk", [P, D])
        ss = sb("p_ss", [P, 8])
        rs = sb("p_rs", [P, 8])
        bank = [ctx.enter_context(nc.psum_tensor(f"p_ps{i}", [P, HALF], F32)) for i in range(4)]
        x_in = [sems.enter_context(nc.semaphore(f"x_in{t}")) for t in range(KT)]
        const_in = sems.enter_context(nc.semaphore("const_in"))
        squares = sems.enter_context(nc.semaphore("squares"))
        mean_eps = sems.enter_context(nc.semaphore("mean_eps"))
        root = sems.enter_context(nc.semaphore("root"))
        rstd = sems.enter_context(nc.semaphore("rstd"))
        scaled = sems.enter_context(nc.semaphore("scaled"))
        turned = sems.enter_context(nc.semaphore("turned"))
        evacuated = sems.enter_context(nc.semaphore("evacuated"))
        block = ctx.enter_context(nc.Block())

        @block.sync
        def _(sp):
            for t in range(KT):
                sp.dma_start(x[:, t, :], d["x"][t * P:(t + 1) * P, :]).then_inc(x_in[t], 16)
            n = 0
            for name in ("ident", "ones", "block_ones", "score_mask", "level_mask", "restart", "norms"):
                sp.dma_start(cst[name][:], d[name]).then_inc(const_in, 16)
                n += 16
            sp.wait_ge(const_in, n)

        @block.scalar
        def _(act):
            for t in range(KT):
                act.wait_ge(x_in[t], 16)
                if t:
                    act.wait_ge(squares, t)
                nc.scalar.activation(junk[:], x[:, t, :], ACT.Square, accum_out=ss[:, t:t + 1]).then_inc(squares, 1)
            act.wait_ge(mean_eps, 1)
            nc.scalar.activation(rs[:], ss[:], ACT.Sqrt).then_inc(root, 1)

        @block.vector
        def _(dve):
            dve.wait_ge(squares, KT)
            nc.vector.tensor_scalar(ss[:], ss[:], 1.0 / D, NORM_EPS, ALU.mult, ALU.add).then_inc(mean_eps, 1)
            dve.wait_ge(root, 1)
            nc.vector.reciprocal(rs[:], rs[:]).then_inc(rstd, 1)
            dve.wait_ge(rstd, 1)
            for t in range(KT):
                nc.vector.tensor_scalar(x[:, t, :], x[:, t, :], rs[:, t:t + 1], None, ALU.mult).then_inc(scaled, 1)
            dve.wait_ge(const_in, 16 * 7)
            for h in range(2):
                for k in range(KT):
                    n = h * KT + k
                    dve.wait_ge(turned, n + 1)
                    nc.vector.tensor_scalar(hT[:, k, h * HALF:(h + 1) * HALF], bank[n % 4][:],
                                            cst["norms"][:, k:k + 1], None, ALU.mult).then_inc(evacuated, 1)
            dve.wait_ge(evacuated, 2 * KT)

        @block.tensor
        def _(pe):
            pe.wait_ge(const_in, 16 * 7)
            pe.wait_ge(scaled, KT)
            for h in range(2):
                for k in range(KT):
                    n = h * KT + k
                    if n >= 4:
                        pe.wait_ge(evacuated, n - 3)
                    for j in range(4):
                        mm = pe.transpose(bank[n % 4][:, j * P:(j + 1) * P],
                                          x[:, 4 * h + j, k * P:(k + 1) * P], ident[:])
                    mm.then_inc(turned, 1)


def _low_rank(nc, sems, d, hT, lora_wa, lora_g, gla_al, norms):
    with ExitStack() as ctx:
        sb = lambda n, s: ctx.enter_context(nc.sbuf_tensor(n, s, F32))
        w = sb("l_w", [P, KT, 272])
        raw = [sb(f"l_raw{i}", [P, 1 + SEQ]) for i in range(2)]
        diff = sb("l_diff", [P, SEQ])
        bank = [ctx.enter_context(nc.psum_tensor(f"l_ps{i}", [P, HALF], F32)) for i in range(6)]
        sem = lambda n: sems.enter_context(nc.semaphore(n))
        w_in, product, copied, zeroed, shifted, gated = map(sem, ("l_w_in", "l_product", "l_copied", "l_zeroed", "l_shifted", "l_gated"))
        block = ctx.enter_context(nc.Block())

        @block.sync
        def _(sp):
            sp.dma_start(w[:], d["w_lora"]).then_inc(w_in, 16)

        @block.tensor
        def _(pe):
            pe.wait_ge(w_in, 16)
            for n in range(6):
                q, h = n // 2, n % 2
                a, b = ((0, P), (P, 2 * P), (2 * P, 2 * P + RANK))[q]
                for k in range(KT):
                    mm = pe.matmul(bank[n][0:b - a, :], w[:, k, a:b], hT[:, k, h * HALF:(h + 1) * HALF],
                                   start=k == 0, stop=k == KT - 1)
                mm.then_inc(product, 1)

        @block.scalar
        def _(act):
            for n in range(6):
                q, h = n // 2, n % 2
                act.wait_ge(product, n + 1)
                if q < 2:
                    out, src = raw[q][:, 1 + h * HALF:1 + (h + 1) * HALF], bank[n][:]
                else:
                    out, src = gla_al[0:RANK, h * HALF:(h + 1) * HALF], bank[n][0:RANK, :]
                nc.scalar.activation(out, src, ACT.Copy).then_inc(copied, 1)
            act.wait_ge(shifted, 4)
            nc.scalar.activation(lora_wa[0:HEAD, :], lora_wa[0:HEAD, :], ACT.Tanh).then_inc(gated, 1)
            nc.scalar.activation(lora_g[:], lora_g[:], ACT.Tanh, scale=0.5).then_inc(gated, 1)

        @block.vector
        def _(dve):
            for q in range(2):
                nc.vector.memset(raw[q][:, 0:1], 0.0).then_inc(zeroed, 1)
            dve.wait_ge(zeroed, 2)
            for q, out in enumerate((lora_wa, lora_g)):
                dve.wait_ge(copied, 2 * q + 2)
                if q:
                    dve.wait_ge(shifted, 2)
                nc.vector.tensor_tensor(diff[:], raw[q][:, 0:SEQ], raw[q][:, 1:1 + SEQ], ALU.subtract).then_inc(shifted, 1)
                dve.wait_ge(shifted, 2 * q + 1)
                nc.vector.scalar_tensor_tensor(out[:], diff[:], norms[:, 16 + q:17 + q], raw[q][:, 1:1 + SEQ],
                                               ALU.mult, ALU.add).then_inc(shifted, 1)
            dve.wait_ge(gated, 2)
            nc.vector.tensor_scalar(lora_g[:], lora_g[:], 0.5, 0.5, ALU.mult, ALU.add).then_inc(gated, 1)
            dve.wait_ge(gated, 3)


def _gla(nc, sems, d, hT, gla_al, yT, cst):
    ident, ones = cst["ident"], cst["ones"]
    causal = cst["score_mask"][:, P:2 * P]
    with ExitStack() as ctx:
        sb = lambda n, s: ctx.enter_context(nc.sbuf_tensor(n, s, F32))
        w = sb("g_w", [P, KT, 768])
        aw = sb("g_aw", [RANK, P])
        par = sb("g_par", [P, 3])
        q, k, silu_t, silu_x = sb("g_q", [P, HALF]), sb("g_k", [P, HALF]), sb("g_st", [P, 2, HALF]), sb("g_sx", [P, 2, HALF])
        v = sb("g_v", [P, NC, GLA_DV])
        az, mz, la, cum = (sb(n, [P, HALF]) for n in ("g_az", "g_mz", "g_la", "g_cum"))
        up, down, k_tok = (sb(n, [P, HALF]) for n in ("g_up", "g_down", "g_kt"))
        scores = sb("g_scores", [P, NC, CHUNK])
        small = sb("g_small", [P, 4 * NC])
        state = [sb(f"g_state{i}", [P, GLA_DV]) for i in range(2)]
        o, sq = sb("g_o", [P, 2, HALF]), sb("g_sq", [P, 2, HALF])
        rs = sb("g_rs", [P, HALF])
        bank = [ctx.enter_context(nc.psum_tensor(f"g_ps{i}", [P, HALF], F32)) for i in range(8)]
        touch = sb("g_touch", [P, 1])
        w_in = sems.enter_context(nc.semaphore("g_w_in"))
        zeroed = sems.enter_context(nc.semaphore("g_zeroed"))
        pe_s = Steps(nc, sems, "g_pe", ["q", "k", "z", "og0", "og1", "v0", "v1", "k_tok", "scores"]
                     + [f"{x}{c}" for c in range(NC) for x in ("state", "o")] + ["mean"])
        act_s = Steps(nc, sems, "g_act", ["q", "k", "abs_z", "og0", "og1", "x0", "x1", "v0", "v1", "exp_z", "log_z",
                                         "up", "down", "mid", "decay", "k_tok"]
                      + [f"state{c}" for c in range(NC)] + ["o0", "o1", "sq0", "sq1", "root"])
        dve_s = Steps(nc, sems, "g_dve", ["min_z", "log_a", "cum", "mid", "from_mid", "to_end", "to_next", "q", "k", "half0", "half1", "silu0", "silu1",
                                         "scores", "start", "var", "rstd", "n0", "n1", "y0", "y1"])
        block = ctx.enter_context(nc.Block())

        @block.sync
        def _(sp):
            with sp.Fori(0, GLA_HEADS) as g:
                pe_s.need_before(sp, "v1", g * 2)
                dve_s.need_before(sp, "n1", g * 2)
                sp.dma_start(w[:], d["w_gla"][bass.ds(g, 1)].rearrange("o p k n -> p (o k) n")).then_inc(w_in, 16)
                sp.dma_start(aw[:], d["gla_a_w2"][bass.ds(g, 1)].rearrange("o p n -> p (o n)")).then_inc(w_in, 16)
                sp.dma_start(par[:], d["gla_par"][bass.ds(g, 1)].rearrange("o p n -> p (o n)")).then_inc(w_in, 16)

        @block.tensor
        def _(pe):
            pe_s.start(pe)
            with pe.Fori(0, GLA_HEADS) as g:
                pe.wait_ge(w_in, g * 48 + 48)
                for h in range(2):
                    u = g * 2 + h
                    tok = slice(h * HALF, (h + 1) * HALF)
                    act_s.need_before(pe, "v0", u)
                    dve_s.need_before(pe, "y1", u)
                    for n, (name, a, evac) in enumerate((("q", 0, None), ("k", 128, None), ("z", None, None),
                                                         ("og0", 256, "q"), ("og1", 384, "k"))):
                        if n == 3:
                            act_s.need(pe, "q", u)
                        if n == 4:
                            act_s.need(pe, "k", u)
                        b = bank[(0, 1, 2, 0, 1)[n]]
                        if a is None:
                            mm = pe.matmul(b[:], aw[:], gla_al[0:RANK, tok], start=True, stop=True)
                        else:
                            for kk in range(KT):
                                mm = pe.matmul(b[:], w[:, kk, a:a + P], hT[:, kk, tok], start=kk == 0, stop=kk == KT - 1)
                        pe_s.done(mm, name)
                    for j in range(2):
                        for c in range(2):
                            t0 = h * HALF + (2 * j + c) * P
                            for kk in range(KT):
                                mm = pe.matmul(bank[3 + j][:, c * GLA_DV:(c + 1) * GLA_DV], hT[:, kk, t0:t0 + P],
                                               w[:, kk, 512:768], start=kk == 0, stop=kk == KT - 1)
                        pe_s.done(mm, f"v{j}")
                    dve_s.need(pe, "k", u)
                    for c in range(NC):
                        mm = pe.transpose(bank[5][:, c * P:(c + 1) * P], k[:, c * P:(c + 1) * P], ident[:])
                    pe_s.done(mm, "k_tok")
                    for c in range(NC):
                        s = slice(c * P, (c + 1) * P)
                        mm = pe.matmul(bank[6][:, s], k[:, s], q[:, s], start=True, stop=True)
                    pe_s.done(mm, "scores")
                    act_s.need(pe, "k_tok", u)
                    act_s.need(pe, "v1", u)
                    for c in range(NC):
                        s = slice(c * P, (c + 1) * P)
                        if c:
                            act_s.need(pe, f"state{c - 1}", u)
                        else:
                            dve_s.need(pe, "start", u)
                        sb_ = bank[7]
                        pe.matmul(sb_[:, 0:GLA_DV], k_tok[:, s], v[:, c, :], start=True, stop=False)
                        mm = pe.matmul(sb_[:, 0:GLA_DV], ident[:], state[c % 2][:], start=False, stop=True)
                        pe_s.done(mm, f"state{c}")
                        if c == 0:
                            dve_s.need(pe, "scores", u)
                        for x in range(2):
                            vs = slice(x * P, (x + 1) * P)
                            pe.matmul(bank[3 + x][:, s], v[:, c, vs], scores[:, c, :], start=True, stop=False)
                            mm = pe.matmul(bank[3 + x][:, s], state[c % 2][:, vs], q[:, s], start=False, stop=True)
                        pe_s.done(mm, f"o{c}")
                    act_s.need(pe, "sq1", u)
                    pe.matmul(bank[2][:], ones[:], sq[:, 0, :], start=True, stop=False)
                    mm = pe.matmul(bank[2][:], ones[:], sq[:, 1, :], start=False, stop=True)
                    pe_s.done(mm, "mean")

        @block.scalar
        def _(act):
            act_s.start(act)
            with act.Fori(0, GLA_HEADS) as g:
                for h in range(2):
                    u = g * 2 + h
                    pe_s.need(act, "q", u)
                    act_s.done(nc.scalar.activation(q[:], bank[0][:], ACT.Copy, scale=GLA_DK ** -0.5), "q")
                    pe_s.need(act, "k", u)
                    act_s.done(nc.scalar.activation(k[:], bank[1][:], ACT.Copy), "k")
                    pe_s.need(act, "z", u)
                    act_s.done(nc.scalar.activation(az[:], bank[2][:], ACT.Abs, bias=par[:, 0:1]), "abs_z")
                    for x in range(2):
                        pe_s.need(act, f"og{x}", u)
                        act_s.done(nc.scalar.activation(silu_t[:, x, :], bank[x][:], ACT.Tanh, scale=0.5), f"og{x}")
                    for x in range(2):
                        act_s.done(nc.scalar.activation(silu_x[:, x, :], bank[x][:], ACT.Copy), f"x{x}")
                    for x in range(2):
                        pe_s.need(act, f"v{x}", u)
                        act_s.done(nc.scalar.activation(v[:, 2 * x:2 * x + 2, :].rearrange("p a b -> p (a b)"), bank[3 + x][:], ACT.Copy), f"v{x}")
                    act_s.need(act, "abs_z", u)
                    act_s.done(nc.scalar.activation(az[:], az[:], ACT.Exp, scale=-1.0), "exp_z")
                    act_s.need(act, "exp_z", u)
                    act_s.done(nc.scalar.activation(az[:], az[:], ACT.Ln, bias=1.0), "log_z")
                    dve_s.need(act, "from_mid", u)
                    act_s.done(nc.scalar.activation(up[:], la[:], ACT.Exp, scale=1 / 16), "up")
                    act_s.done(nc.scalar.activation(down[:], la[:], ACT.Exp, scale=-1 / 16), "down")
                    dve_s.need(act, "to_next", u)
                    act_s.done(nc.scalar.activation(small[:, 2 * NC:3 * NC], small[:, 0:NC], ACT.Exp, scale=1 / 16), "mid")
                    act_s.done(nc.scalar.activation(small[:, 3 * NC:4 * NC], small[:, NC:2 * NC], ACT.Exp, scale=1 / 16), "decay")
                    pe_s.need(act, "k_tok", u)
                    act_s.done(nc.scalar.activation(k_tok[:], bank[5][:], ACT.Copy), "k_tok")
                    act_s.need(act, "decay", u)
                    for c in range(NC):
                        pe_s.need(act, f"state{c}", u)
                        if c:
                            pe_s.need(act, f"o{c - 1}", u)
                        act_s.done(nc.scalar.activation(state[(c + 1) % 2][:], bank[7][:, 0:GLA_DV], ACT.Copy,
                                                        scale=small[:, 3 * NC + c:3 * NC + c + 1]), f"state{c}")
                    pe_s.need(act, f"o{NC - 1}", u)
                    dve_s.need_before(act, "y1", u)
                    for x in range(2):
                        act_s.done(nc.scalar.activation(o[:, x, :], bank[3 + x][:], ACT.Copy), f"o{x}")
                    for x in range(2):
                        act_s.done(nc.scalar.activation(sq[:, x, :], bank[3 + x][:], ACT.Square, scale=GLA_DV ** -0.5), f"sq{x}")
                    dve_s.need(act, "var", u)
                    act_s.done(nc.scalar.activation(rs[:], rs[:], ACT.Sqrt), "root")

        @block.vector
        def _(dve):
            dve_s.start(dve)
            nc.vector.memset(scores[:], 0.0).then_inc(zeroed, 1)
            with dve.Fori(0, GLA_HEADS) as g:
                for h in range(2):
                    u = g * 2 + h
                    tok = slice(h * HALF, (h + 1) * HALF)
                    pe_s.need(dve, "z", u)
                    act_s.need(dve, "abs_z", u)
                    dve_s.done(nc.vector.tensor_scalar(mz[:], bank[2][:], par[:, 0:1], 0.0, ALU.add, ALU.min), "min_z")
                    dve_s.need(dve, "min_z", u)
                    act_s.need(dve, "log_z", u)
                    dve_s.done(nc.vector.tensor_tensor(la[:], mz[:], az[:], ALU.subtract), "log_a")
                    dve_s.need(dve, "log_a", u)
                    dve_s.done(nc.vector.tensor_tensor_scan(cum[:], cst["restart"][:], la[:], 0.0, ALU.mult, ALU.add), "cum")
                    dve_s.need(dve, "cum", u)
                    _chunk_small(nc, dve, dve_s, u, cum, la, None, small)
                    act_s.need(dve, "up", u)
                    act_s.need(dve, "q", u)
                    dve_s.done(nc.vector.tensor_tensor(q[:], q[:], up[:], ALU.mult), "q")
                    act_s.need(dve, "down", u)
                    dve_s.done(nc.vector.tensor_tensor(k[:], k[:], down[:], ALU.mult), "k")
                    act_s.need(dve, "x1", u)
                    for x in range(2):
                        dve_s.done(nc.vector.tensor_scalar(silu_t[:, x, :], silu_t[:, x, :], 0.5, 0.5, ALU.mult, ALU.add), f"half{x}")
                    for x in range(2):
                        dve_s.need(dve, f"half{x}", u)
                        dve_s.done(nc.vector.tensor_tensor(silu_x[:, x, :], silu_x[:, x, :], silu_t[:, x, :], ALU.mult), f"silu{x}")
                    pe_s.need(dve, "scores", u)
                    nc.vector.memset(touch[:], 0.0)
                    dve.wait_ge(zeroed, 1)
                    dve_s.done(nc.vector.copy_predicated(
                        scores[:], _over(causal, NC),
                        bank[6][:].rearrange("p (c t) -> p c t", c=NC)), "scores")
                    act_s.need(dve, "decay", u)
                    if h == 0:
                        pe_s.need_before(dve, f"o{NC - 1}", u)
                        dve_s.done(nc.vector.memset(state[0][:], 0.0), "start")
                    else:
                        act_s.need_before(dve, f"state{NC - 1}", u)
                        dve_s.done(nc.vector.tensor_scalar(state[0][:], state[0][:], small[:, 2 * NC:2 * NC + 1], None, ALU.mult), "start")
                    pe_s.need(dve, "mean", u)
                    dve_s.done(nc.vector.tensor_scalar(rs[:], bank[2][:], GLA_EPS, None, ALU.add), "var")
                    act_s.need(dve, "root", u)
                    dve_s.done(nc.vector.reciprocal(rs[:], rs[:]), "rstd")
                    dve_s.need(dve, "rstd", u)
                    for x in range(2):
                        dve_s.done(nc.vector.scalar_tensor_tensor(o[:, x, :], o[:, x, :], par[:, 1 + x:2 + x], rs[:], ALU.mult, ALU.mult), f"n{x}")
                    for x in range(2):
                        dve_s.need(dve, f"n{x}", u)
                        dve_s.done(nc.vector.tensor_tensor(
                            yT[:, bass.ds(g * 2 + x, 1), tok].rearrange("p o t -> p (o t)"),
                            o[:, x, :], silu_x[:, x, :], ALU.mult), f"y{x}")


def _over(mask, n):
    return mask.rearrange("p (o t) -> p o t", o=1).to_broadcast([P, n, CHUNK])


def _chunk_small(nc, dve, dve_s, u, cum, out, less, small):
    c3 = cum[:].rearrange("p (c t) -> p c t", c=NC)
    mid, end = c3[:, :, CHUNK // 2 - 1:CHUNK // 2], c3[:, :, CHUNK - 1:CHUNK]
    s3 = small[:].rearrange("p (k c o) -> p k c o", k=4, o=1)
    dve_s.need(dve, "cum", u)
    dve_s.done(nc.vector.tensor_copy(s3[:, 0], mid), "mid")
    dve_s.need(dve, "mid", u)
    dve_s.done(nc.vector.tensor_tensor(out[:].rearrange("p (c t) -> p c t", c=NC), c3,
                                       s3[:, 0].to_broadcast([P, NC, CHUNK]), ALU.subtract), "from_mid")
    dve_s.done(nc.vector.tensor_tensor(s3[:, 1], end, s3[:, 0], ALU.subtract), "to_end")
    dve_s.need(dve, "to_end", u)
    dve_s.done(nc.vector.tensor_tensor(s3[:, 1, 0:NC - 1], s3[:, 1, 0:NC - 1], s3[:, 0, 1:NC], ALU.add), "to_next")


def _rwkv(nc, sems, d, hT, lora_wa, lora_g, y_dram, cst):
    ident, block_ones = cst["ident"], cst["block_ones"]
    with ExitStack() as ctx:
        sb = lambda n, s: ctx.enter_context(nc.sbuf_tensor(n, s, F32))
        t = lambda n: sb(n, [P, HALF])
        w = sb("r_w", [P, KT, 3 * P])
        pack = sb("r_pack", [P, 2 * P + NPAR])
        par = lambda i: pack[:, 2 * P + i:2 * P + i + 1]
        half_par = sb("r_half_par", [P, 2])
        raw = [sb(f"r_raw{i}", [P, 1 + SEQ]) for i in range(3)]
        diff = [t("r_diff0"), t("r_diff1")]
        r, k, v, log_w, cum, from_mid, a, kk, sq, norm = map(t, ("r_r", "r_k", "r_v", "r_lw", "r_cum", "r_fm", "r_a", "r_kk", "r_sq", "r_norm"))
        up, down, prev, k_bar, b_bar, gate, bonus = map(t, ("r_up", "r_down", "r_prev", "r_kbar", "r_bbar", "r_gate", "r_bonus"))
        ar = sb("r_ar", [P, NC, 2, CHUNK])
        small = sb("r_small", [P, 4 * NC])
        k_tok, b_tok, v_tok = map(t, ("r_kt", "r_bt", "r_vt"))
        scores = sb("r_scores", [P, 2 * NC, 4, CHUNK])
        invT = [sb(f"r_invT{b}", [P, 4, CHUNK]) for b in range(2)]
        inv = [sb(f"r_inv{b}", [P, 4, CHUNK]) for b in range(2)]
        prod = [sb(f"r_prod{b}", [P, 4, CHUNK]) for b in range(2)]
        z, uu = sb("r_z", [P, P]), sb("r_u", [P, P])
        state = [sb(f"r_state{i}", [P, P]) for i in range(2)]
        y, ysq = t("r_y"), t("r_ysq")
        y_out = [t("r_yout0"), t("r_yout1")]
        stored = [sems.enter_context(nc.semaphore(f"r_stored{h}")) for h in range(2)]
        bank = [ctx.enter_context(nc.psum_tensor(f"r_ps{i}", [P, HALF], F32)) for i in range(8)]
        touch = sb("r_touch", [P, 2 * NC])
        w_in = sems.enter_context(nc.semaphore("r_w_in"))
        zeroed = sems.enter_context(nc.semaphore("r_zeroed"))
        lv = [f"{l}.{b}" for l in range(1, LEVELS + 1) for b in range(2)]
        last = f"{LEVELS}.1"
        pf = Steps(nc, sems, "pe_front", ["r", "k", "v", "w", "a", "gate", "norm", "bonus"])
        af = Steps(nc, sems, "act_front", ["r", "k", "v", "w", "a", "gate", "kk_sq", "up", "down", "prev", "mid", "decay", "norm"])
        df = Steps(nc, sems, "dve_front", ["half_par", "r_diff", "r", "k_diff", "k", "kk", "v_diff", "v", "log_w", "cum", "mid", "from_mid",
                                           "to_end", "to_next", "from_prev", "a", "k_gain", "k_mod", "r_up", "k_bar", "rk", "norm_floor",
                                           "norm_inv", "kk_unit", "b", "b_bar", "a_prev", "bonus"])
        pb = Steps(nc, sems, "pe_back", ["k_tok", "b_tok", "v_tok"] + [f"scores{j}" for j in range(2 * NC)] + ["inv0", "inv1"]
                   + [f"{x}{l}.{b}" for l in range(1, LEVELS + 1) for x in ("prod", "inv") for b in range(2)]
                   + [f"{x}{c}" for c in range(NC) for x in ("z", "u", "s", "y")] + ["mean", "var"])
        ab = Steps(nc, sems, "act_back", ["k_tok", "b_tok", "v_tok"] + [f"{x}{c}" for c in range(NC) for x in ("z", "s")] + ["y", "y_sq", "std"])
        db = Steps(nc, sems, "dve_back", [f"scores{j}" for j in range(2 * NC)] + [f"{x}{b}" for b in range(2) for x in ("invT_mask", "invT")]
                   + ["inv0", "inv1"]
                   + [x for l in range(1, LEVELS + 1) for x in [f"prod{l}.{b}" for b in range(2)]
                      + [f"{i}{l}.{b}" for b in range(2) for i in (("invT", "inv") if l < LEVELS else ("invT",))]]
                   + ["start0", "start1"] + [f"{x}{c}" for c in range(NC) for x in ("u", "s")]
                   + ["centred", "var", "rstd", "n", "affine", "plus", "out"])
        block = ctx.enter_context(nc.Block())
        end = f"y{NC - 1}"

        @block.sync
        def _(sp):
            with sp.Fori(0, RWKV_PAIRS) as p:
                pf.need_before(sp, "gate", p * 2)
                sp.dma_start(w[:], d["w_rwkv"][bass.ds(p, 1)].rearrange("o p k n -> p (o k) n")).then_inc(w_in, 16)
                df.need_before(sp, "bonus", p * 2)
                db.need_before(sp, "affine", p * 2)
                af.need_before(sp, "norm", p * 2)
                sp.dma_start(pack[:], d["rwkv_pack"][bass.ds(p, 1)].rearrange("o p n -> p (o n)")).then_inc(w_in, 16)
                for h in range(2):
                    db.need(sp, "out", p * 2 + h)
                    sp.dma_start(y_dram[bass.ds(p, 1), :, h * HALF:(h + 1) * HALF].rearrange("o p t -> p (o t)"), y_out[h][:]).then_inc(stored[h], 16)
            for h in range(2):
                sp.wait_ge(stored[h], 16 * RWKV_PAIRS + 16)

        @block.tensor
        def _(pe):
            pf.start(pe)
            pb.start(pe)

            def front(p, h):
                u = p * 2 + h
                tok = slice(h * HALF, (h + 1) * HALF)
                free = ((df, "norm_floor"), (df, "bonus"), (af, "r"), (af, "k"), (af, "v"), (af, "w"))
                for n, name in enumerate(("r", "k", "v", "w", "a", "gate")):
                    who, step = free[n]
                    (who.need_before if n < 2 else who.need)(pe, step, u)
                    b = bank[n % 2]
                    if n < 3:
                        for kk_ in range(KT):
                            mm = pe.matmul(b[:], w[:, kk_, n * P:(n + 1) * P], hT[:, kk_, tok], start=kk_ == 0, stop=kk_ == KT - 1)
                    elif n == 3:
                        mm = pe.matmul(b[:], pack[0:HEAD, 0:P], lora_wa[0:HEAD, tok], start=True, stop=True)
                    elif n == 4:
                        mm = pe.matmul(b[:], pack[HEAD:P, 0:P], lora_wa[HEAD:P, tok], start=True, stop=True)
                    else:
                        mm = pe.matmul(b[:], pack[:, P:2 * P], lora_g[:, tok], start=True, stop=True)
                    pf.done(mm, name)
                af.need(pe, "a", u)
                af.need(pe, "kk_sq", u)
                pf.done(pe.matmul(bank[0][:], block_ones[:], sq[:], start=True, stop=True), "norm")
                af.need(pe, "gate", u)
                df.need(pe, "rk", u)
                pf.done(pe.matmul(bank[1][:], block_ones[:], diff[0][:], start=True, stop=True), "bonus")

            def back(p, h):
                u = p * 2 + h
                ab.need_before(pe, "y", u)
                db.need_before(pe, "var", u)
                df.need(pe, "bonus", u)
                for n, (src, name) in enumerate(((k_bar, "k_tok"), (b_bar, "b_tok"), (v, "v_tok"))):
                    for c in range(NC):
                        s = slice(c * P, (c + 1) * P)
                        mm = pe.transpose(bank[4 + n][:, s], src[:, s], ident[:])
                    pb.done(mm, name)
                for j in range(2 * NC):
                    c, hd = j // 2, j % 2
                    rows = slice(hd * HEAD, (hd + 1) * HEAD)
                    b = bank[(2, 3, 7)[j % 3]]
                    if j >= 3:
                        db.need(pe, f"scores{j - 3}", u)
                    rhs = ar[rows, c, :, :].rearrange("p k t -> p (k t)")
                    pe.matmul(b[:, 0:2 * P], b_bar[rows, c * P:(c + 1) * P], rhs, start=True, stop=True)
                    mm = pe.matmul(b[:, 2 * P:4 * P], k_bar[rows, c * P:(c + 1) * P], rhs, start=True, stop=True)
                    pb.done(mm, f"scores{j}")
                ab.need(pe, "v_tok", u)
                for b in range(2):
                    db.need(pe, f"invT{b}", u)
                    for i in range(4):
                        mm = pe.transpose(bank[4 + b][:, i * P:(i + 1) * P], invT[b][:, i, :], ident[:])
                    pb.done(mm, f"inv{b}")
                for l in range(1, LEVELS + 1):
                    for b in range(2):
                        db.need(pe, f"inv{b}" if l == 1 else f"inv{l - 1}.{b}", u)
                        for i in range(4):
                            mm = pe.matmul(bank[2 + b][:, i * P:(i + 1) * P], scores[:, 4 * b + i, 0, :], inv[b][:, i, :], start=True, stop=True)
                        pb.done(mm, f"prod{l}.{b}")
                    for b in range(2):
                        db.need(pe, f"prod{l}.{b}", u)
                        for i in range(4):
                            mm = pe.matmul(bank[4 + 2 * b][:, i * P:(i + 1) * P], prod[b][:, i, :], invT[b][:, i, :], start=True, stop=True)
                        if l < LEVELS:
                            for i in range(4):
                                mm = pe.matmul(bank[5 + 2 * b][:, i * P:(i + 1) * P], invT[b][:, i, :], prod[b][:, i, :], start=True, stop=True)
                        pb.done(mm, f"inv{l}.{b}")
                db.need(pe, f"invT{last}", u)
                for c in range(NC):
                    s = slice(c * P, (c + 1) * P)
                    now = state[c % 2]
                    for hd in range(2):
                        hs = slice(hd * HEAD, (hd + 1) * HEAD)
                        pe.matmul(bank[4][:, hs], scores[:, 2 * c + hd, 2, :], v_tok[:, c * P + hd * HEAD:c * P + (hd + 1) * HEAD],
                                  start=hd == 0, stop=False, skip_group_check=True)
                    pe.matmul(bank[(6, 3)[c % 2]][:, 0:P], k_tok[:, s], v_tok[:, s], start=True, stop=False)
                    if c:
                        ab.need(pe, f"s{c - 1}", u)
                        db.need(pe, f"s{c - 1}", u)
                    else:
                        db.need(pe, "start1", u)
                    pb.done(pe.matmul(bank[4][:, 0:P], ar[:, c, 0, :], now[:], start=False, stop=True, skip_group_check=True), f"z{c}")
                    pe.matmul(bank[(6, 3)[c % 2]][:, 0:P], ident[:], now[:], start=False, stop=False)
                    ab.need(pe, f"z{c}", u)
                    for hd in range(2):
                        hs = slice(hd * HEAD, (hd + 1) * HEAD)
                        mm = pe.matmul(bank[5][:, hs], invT[c // 2][:, 2 * (c % 2) + hd, :], z[:, hs], start=True, stop=True)
                    pb.done(mm, f"u{c}")
                    pe.matmul(bank[7][:, s], now[:], ar[:, c, 1, :], start=True, stop=False, skip_group_check=True)
                    db.need(pe, f"u{c}", u)
                    pb.done(pe.matmul(bank[(6, 3)[c % 2]][:, 0:P], b_tok[:, s], uu[:], start=False, stop=True), f"s{c}")
                    for hd in range(2):
                        hs = slice(hd * HEAD, (hd + 1) * HEAD)
                        pe.matmul(bank[7][hs, s], v_tok[:, c * P + hd * HEAD:c * P + (hd + 1) * HEAD], scores[:, 2 * c + hd, 3, :],
                                  start=False, stop=False, skip_group_check=True)
                        mm = pe.matmul(bank[7][hs, s], uu[:, hs], scores[:, 2 * c + hd, 1, :], start=False, stop=True, skip_group_check=True)
                    pb.done(mm, f"y{c}")
                ab.need(pe, "y", u)
                pb.done(pe.matmul(bank[2][:], block_ones[:], y[:], start=True, stop=True), "mean")
                ab.need(pe, "y_sq", u)
                pb.done(pe.matmul(bank[3][:], block_ones[:], ysq[:], start=True, stop=True), "var")

            with pe.Fori(0, RWKV_PAIRS) as p:
                pe.wait_ge(w_in, p * 32 + 32)
                for h in range(2):
                    front(p, h)
                    back(p, h)

        @block.scalar
        def _(act):
            af.start(act)
            ab.start(act)
            A = nc.scalar.activation

            def front(p, h):
                u = p * 2 + h
                df.need_before(act, "bonus", u)
                db.need_before(act, "out", u)
                for n, name in enumerate(("r", "k", "v")):
                    pf.need(act, name, u)
                    af.done(A(raw[n][:, 1 + h * HALF:1 + (h + 1) * HALF], bank[n % 2][:], ACT.Copy), name)
                df.need(act, "half_par", u)
                pf.need(act, "w", u)
                af.done(A(log_w[:], bank[1][:], ACT.Tanh, scale=0.5, bias=half_par[:, 0:1]), "w")
                pf.need(act, "a", u)
                af.done(A(a[:], bank[0][:], ACT.Tanh, scale=0.5, bias=half_par[:, 1:2]), "a")
                pf.need(act, "gate", u)
                af.done(A(gate[:], bank[1][:], ACT.Copy), "gate")
                df.need(act, "kk", u)
                af.done(A(sq[:], kk[:], ACT.Square), "kk_sq")
                df.need(act, "from_mid", u)
                af.done(A(up[:], from_mid[:], ACT.Exp), "up")
                af.done(A(down[:], from_mid[:], ACT.Exp, scale=-1.0), "down")
                df.need(act, "from_prev", u)
                af.done(A(prev[:], cum[:], ACT.Exp), "prev")
                af.done(A(small[:, 2 * NC:3 * NC], small[:, 0:NC], ACT.Exp), "mid")
                af.done(A(small[:, 3 * NC:4 * NC], small[:, NC:2 * NC], ACT.Exp), "decay")
                df.need(act, "norm_floor", u)
                af.done(A(norm[:], norm[:], ACT.Sqrt), "norm")

            def back(p, h):
                u = p * 2 + h
                for n, (out, name) in enumerate(((k_tok, "k_tok"), (b_tok, "b_tok"), (v_tok, "v_tok"))):
                    pb.need(act, name, u)
                    ab.done(A(out[:], bank[4 + n][:], ACT.Copy), name)
                af.need(act, "decay", u)
                for c in range(NC):
                    pb.need(act, f"z{c}", u)
                    ab.done(A(z[:], bank[4][:, 0:P], ACT.Copy), f"z{c}")
                    pb.need(act, f"s{c}", u)
                    ab.done(A(state[(c + 1) % 2][0:HEAD, 0:HEAD], bank[(6, 3)[c % 2]][0:HEAD, 0:HEAD], ACT.Copy,
                              scale=small[0:HEAD, 3 * NC + c:3 * NC + c + 1]), f"s{c}")
                pb.need(act, end, u)
                ab.done(A(y[:], bank[7][:], ACT.Copy), "y")
                db.need(act, "centred", u)
                ab.done(A(ysq[:], y[:], ACT.Square, scale=0.125), "y_sq")
                db.need(act, "var", u)
                ab.done(A(ysq[:], ysq[:], ACT.Sqrt), "std")

            with act.Fori(0, RWKV_PAIRS) as p:
                for h in range(2):
                    front(p, h)
                    back(p, h)

        @block.vector
        def _(dve):
            V = nc.vector
            for x in stored:
                dve.sem_inc(x, 16)
            df.start(dve)
            db.start(dve)
            for i, x in enumerate(raw):
                V.memset(x[:, 0:1], 0.0).then_inc(zeroed, 1)
            for x in state:
                V.memset(x[:], 0.0).then_inc(zeroed, 1)
            V.memset(scores[:], 0.0).then_inc(zeroed, 1)
            dve.wait_ge(zeroed, 6)

            def front(p, h):
                u = p * 2 + h
                pb.need_before(dve, end, u)
                ab.need_before(dve, f"s{NC - 1}", u)
                dve.wait_ge(w_in, p * 32 + 32)
                df.done(V.tensor_scalar(half_par[:], pack[:, 2 * P + W0:2 * P + A0 + 1], 0.5, None, ALU.mult), "half_par")
                for n, (name, out) in enumerate((("r", r), ("k", k), ("v", v))):
                    now = raw[n][:, 1 + h * HALF:1 + (h + 1) * HALF]
                    before = raw[n][:, h * HALF:(h + 1) * HALF]
                    af.need(dve, name, u)
                    if n == 2:
                        df.need(dve, "r", u)
                    df.done(V.tensor_tensor(diff[n % 2][:], before, now, ALU.subtract), f"{name}_diff")
                    df.need(dve, f"{name}_diff", u)
                    df.done(V.scalar_tensor_tensor(out[:], diff[n % 2][:], par(MU_R + n), now, ALU.mult, ALU.add), name)
                    if n == 1:
                        df.need(dve, "k", u)
                        df.done(V.tensor_scalar(kk[:], k[:], par(K_K), None, ALU.mult), "kk")
                af.need(dve, "w", u)
                df.done(V.tensor_scalar(log_w[:], log_w[:], -0.5 * DECAY, -0.5 * DECAY, ALU.mult, ALU.add), "log_w")
                df.need(dve, "log_w", u)
                df.done(V.tensor_tensor_scan(cum[:], cst["restart"][:], log_w[:], 0.0, ALU.mult, ALU.add), "cum")
                _chunk_small(nc, dve, df, u, cum, from_mid, None, small)
                df.need(dve, "from_mid", u)
                df.done(V.tensor_tensor(cum[:], from_mid[:], log_w[:], ALU.subtract), "from_prev")
                af.need(dve, "a", u)
                df.done(V.tensor_scalar(a[:], a[:], 0.5, 0.5, ALU.mult, ALU.add), "a")
                df.need(dve, "a", u)
                df.done(V.tensor_scalar(diff[1][:], a[:], 1.0, par(K_A), ALU.subtract, ALU.mult), "k_gain")
                df.need(dve, "k_gain", u)
                df.done(V.scalar_tensor_tensor(k[:], diff[1][:], 1.0, k[:], ALU.add, ALU.mult), "k_mod")
                af.need(dve, "up", u)
                df.done(V.tensor_tensor(ar[:, :, 1, :], r[:].rearrange("p (c t) -> p c t", c=NC), up[:].rearrange("p (c t) -> p c t", c=NC), ALU.mult), "r_up")
                af.need(dve, "down", u)
                df.need(dve, "k_mod", u)
                df.done(V.tensor_tensor(k_bar[:], k[:], down[:], ALU.mult), "k_bar")
                df.need(dve, "v", u)
                df.done(V.scalar_tensor_tensor(diff[0][:], r[:], par(R_K), k[:], ALU.mult, ALU.mult), "rk")
                pf.need(dve, "norm", u)
                df.done(V.tensor_scalar(norm[:], bank[0][:], 1e-24, None, ALU.max), "norm_floor")
                af.need(dve, "norm", u)
                df.done(V.reciprocal(norm[:], norm[:]), "norm_inv")
                df.need(dve, "norm_inv", u)
                df.done(V.tensor_tensor(kk[:], kk[:], norm[:], ALU.mult), "kk_unit")
                df.need(dve, "kk_unit", u)
                df.done(V.tensor_tensor(a[:], kk[:], a[:], ALU.mult), "b")
                df.need(dve, "b", u)
                df.done(V.tensor_tensor(b_bar[:], a[:], down[:], ALU.mult), "b_bar")
                af.need(dve, "prev", u)
                df.done(V.scalar_tensor_tensor(ar[:, :, 0, :], kk[:].rearrange("p (c t) -> p c t", c=NC), -1.0,
                                               prev[:].rearrange("p (c t) -> p c t", c=NC), ALU.mult, ALU.mult), "a_prev")
                pf.need(dve, "bonus", u)
                df.done(V.tensor_tensor(bonus[:], bank[1][:], v[:], ALU.mult), "bonus")

            def back(p, h):
                u = p * 2 + h
                for j in range(2 * NC):
                    pb.need(dve, f"scores{j}", u)
                    V.memset(touch[:, j:j + 1], 0.0)
                    db.done(V.copy_predicated(scores[:, j].rearrange("p k t -> p (k t)"), cst["score_mask"][:],
                                              bank[(2, 3, 7)[j % 3]][:]), f"scores{j}")
                level = lambda l: _over(cst["level_mask"][:, l, :], 4)
                for b in range(2):
                    db.need(dve, f"scores{4 * b + 3}", u)
                    db.done(V.tensor_tensor(invT[b][:], scores[:, 4 * b:4 * b + 4, 0, :], level(0), ALU.mult), f"invT_mask{b}")
                    db.need(dve, f"invT_mask{b}", u)
                    db.done(V.tensor_tensor(invT[b][:], invT[b][:], _over(ident[:], 4), ALU.add), f"invT{b}")
                for b in range(2):
                    pb.need(dve, f"inv{b}", u)
                    db.done(V.tensor_copy(inv[b][:].rearrange("p i t -> p (i t)"), bank[4 + b][:]), f"inv{b}")
                for l in range(1, LEVELS + 1):
                    def evac_prod(b):
                        pb.need(dve, f"prod{l}.{b}", u)
                        db.done(V.tensor_tensor(prod[b][:], bank[2 + b][:].rearrange("p (i t) -> p i t", i=4), level(l), ALU.mult), f"prod{l}.{b}")

                    def evac_inv(b):
                        pb.need(dve, f"inv{l}.{b}", u)
                        db.done(V.tensor_tensor(invT[b][:], bank[4 + 2 * b][:].rearrange("p (i t) -> p i t", i=4), invT[b][:], ALU.add), f"invT{l}.{b}")
                        if l < LEVELS:
                            db.done(V.tensor_tensor(inv[b][:], bank[5 + 2 * b][:].rearrange("p (i t) -> p i t", i=4), inv[b][:], ALU.add), f"inv{l}.{b}")
                    evac_prod(0)
                    evac_prod(1)
                    evac_inv(0)
                    evac_inv(1)
                for hd in range(2):
                    hs = slice(hd * HEAD, (hd + 1) * HEAD)
                    if h == 0:
                        db.done(V.memset(state[0][hs, hs], 0.0), f"start{hd}")
                    else:
                        af.need(dve, "mid", u)
                        db.done(V.tensor_scalar(state[0][hs, hs], state[0][hs, hs], small[hs, 2 * NC:2 * NC + 1], None, ALU.mult), f"start{hd}")
                low = slice(HEAD, P)
                for c in range(NC):
                    pb.need(dve, f"u{c}", u)
                    db.done(V.tensor_copy(uu[:], bank[5][:, 0:P]), f"u{c}")
                    pb.need(dve, f"s{c}", u)
                    if c == 0:
                        af.need(dve, "decay", u)
                    db.done(V.tensor_scalar(state[(c + 1) % 2][low, low], bank[(6, 3)[c % 2]][low, low],
                                            small[low, 3 * NC + c:3 * NC + c + 1], None, ALU.mult), f"s{c}")
                pb.need(dve, "mean", u)
                db.done(V.scalar_tensor_tensor(y[:], bank[2][:], -1.0 / HEAD, y[:], ALU.mult, ALU.add), "centred")
                pb.need(dve, "var", u)
                db.done(V.tensor_scalar(ysq[:], bank[3][:], GN_EPS, None, ALU.add), "var")
                ab.need(dve, "std", u)
                db.done(V.reciprocal(ysq[:], ysq[:]), "rstd")
                db.need(dve, "rstd", u)
                db.done(V.tensor_tensor(y[:], y[:], ysq[:], ALU.mult), "n")
                db.need(dve, "n", u)
                db.done(V.tensor_scalar(y[:], y[:], par(LN_W), par(LN_B), ALU.mult, ALU.add), "affine")
                db.need(dve, "affine", u)
                db.done(V.tensor_tensor(y[:], y[:], bonus[:], ALU.add), "plus")
                db.need(dve, "plus", u)
                dve.wait_ge(stored[h], p * 16 + 16)
                db.done(V.tensor_tensor(y_out[h][:], y[:], gate[:], ALU.mult), "out")

            with dve.Fori(0, RWKV_PAIRS) as p:
                for h in range(2):
                    front(p, h)
                    back(p, h)
            db.need(dve, "out", 2 * RWKV_PAIRS - 1)


def _merge(nc, sems, d, hT, glaT, y_dram, mixT):
    with ExitStack() as ctx:
        sb = lambda n, s: ctx.enter_context(nc.sbuf_tensor(n, s, F32))
        w = [sb(f"m_w{i}", [P, KT, 4 * P]) for i in range(2)]
        rwkvT = sb("m_rwkvT", [P, KT, SEQ])
        y_in = sems.enter_context(nc.semaphore("m_y_in"))
        gate = [[sb(f"m_g{i}{x}", [P, HALF]) for x in range(2)] for i in range(2)]
        bank = [ctx.enter_context(nc.psum_tensor(f"m_ps{i}", [P, HALF], F32)) for i in range(8)]
        w_in = [sems.enter_context(nc.semaphore(f"m_w_in{i}")) for i in range(2)]
        unit = [(i, h) for i in range(2) for h in range(2)]
        pe_s = Steps(nc, sems, "m_pe", [f"{x}{i}{h}" for i, h in unit for x in ("ga", "gb", "gla", "rwkv")])
        act_s = Steps(nc, sems, "m_act", [f"{x}{i}{h}" for i, h in unit for x in ("ga", "gb")])
        dve_s = Steps(nc, sems, "m_dve", [f"{x}{i}{h}" for i, h in unit for x in ("sa", "sb", "ma", "mb", "mix")])
        block = ctx.enter_context(nc.Block())
        srcs = (("ga", hT), ("gb", hT), ("gla", glaT), ("rwkv", rwkvT))

        @block.sync
        def _(sp):
            sp.dma_start(rwkvT[:], y_dram.rearrange("k p t -> p k t")).then_inc(y_in, 16)
            with sp.Fori(0, 4) as n:
                for i in range(2):
                    pe_s.need_before(sp, f"rwkv{i}1", n)
                    sp.dma_start(w[i][:], d["w_merge"][bass.ds(n * 2 + i, 1)].rearrange("o p k n -> p (o k) n")).then_inc(w_in[i], 16)

        @block.tensor
        def _(pe):
            pe_s.start(pe)
            pe.wait_ge(y_in, 16)
            with pe.Fori(0, 4) as n:
                for i, h in unit:
                    if h == 0:
                        pe.wait_ge(w_in[i], n * 16 + 16)
                    (dve_s.need_before if i == 0 else dve_s.need)(pe, f"mb{1 - i}{h}", n)
                    for q, (name, src) in enumerate(srcs):
                        b = bank[4 * h + q]
                        for k in range(KT):
                            mm = pe.matmul(b[:], w[i][:, k, q * P:(q + 1) * P], src[:, k, h * HALF:(h + 1) * HALF],
                                           start=k == 0, stop=k == KT - 1)
                        pe_s.done(mm, f"{name}{i}{h}")

        @block.scalar
        def _(act):
            act_s.start(act)
            with act.Fori(0, 4) as n:
                for i, h in unit:
                    (dve_s.need_before if i == 0 else dve_s.need)(act, f"mix{1 - i}{h}", n)
                    for x, name in enumerate(("ga", "gb")):
                        pe_s.need(act, f"{name}{i}{h}", n)
                        act_s.done(nc.scalar.activation(gate[h][x][:], bank[4 * h + x][:], ACT.Tanh, scale=0.5), f"{name}{i}{h}")

        @block.vector
        def _(dve):
            dve_s.start(dve)
            with dve.Fori(0, 4) as n:
                for i, h in unit:
                    for x, (s, g) in enumerate((("sa", "ga"), ("sb", "gb"))):
                        act_s.need(dve, f"{g}{i}{h}", n)
                        dve_s.done(nc.vector.tensor_scalar(gate[h][x][:], gate[h][x][:], 0.5, 0.5, ALU.mult, ALU.add), f"{s}{i}{h}")
                    for x, (m, s, y) in enumerate((("ma", "sa", "gla"), ("mb", "sb", "rwkv"))):
                        dve_s.need(dve, f"{s}{i}{h}", n)
                        pe_s.need(dve, f"{y}{i}{h}", n)
                        dve_s.done(nc.vector.tensor_tensor(gate[h][x][:], bank[4 * h + 2 + x][:], gate[h][x][:], ALU.mult), f"{m}{i}{h}")
                    dve_s.need(dve, f"mb{i}{h}", n)
                    dve_s.done(nc.vector.tensor_tensor(mixT[:, bass.ds(n * 2 + i, 1), h * HALF:(h + 1) * HALF].rearrange("p o t -> p (o t)"),
                                                       gate[h][0][:], gate[h][1][:], ALU.add), f"mix{i}{h}")
            dve_s.need(dve, "mix11", 3)


def _residual(nc, sems, d, mixT, x1, h2T, cst):
    ident = cst["ident"]
    with ExitStack() as ctx:
        sb = lambda n, s: ctx.enter_context(nc.sbuf_tensor(n, s, F32))
        w = sb("o_w", [P, KT, D])
        h2 = sb("o_h2", [P, KT, D])
        ss, rs = sb("o_ss", [P, 8]), sb("o_rs", [P, 8])
        bank = [ctx.enter_context(nc.psum_tensor(f"o_ps{i}", [P, HALF], F32)) for i in range(8)]
        sem = lambda n: sems.enter_context(nc.semaphore(n))
        w_in, product, added, squares, mean_eps, root, rstd, scaled, turned, evacuated = map(
            sem, ("o_w_in", "o_product", "o_added", "o_squares", "o_mean", "o_root", "o_rstd", "o_scaled", "o_turned", "o_evac"))
        x_in = [sem(f"o_x_in{t}") for t in range(KT)]
        block = ctx.enter_context(nc.Block())

        @block.sync
        def _(sp):
            sp.dma_start(w[:], d["w_out"]).then_inc(w_in, 16)
            for t in range(KT):
                sp.dma_start(x1[:, t, :], d["x"][t * P:(t + 1) * P, :]).then_inc(x_in[t], 16)

        @block.tensor
        def _(pe):
            pe.wait_ge(w_in, 16)
            for t in range(KT):
                for e in range(2):
                    n = 2 * t + e
                    if n >= 8:
                        pe.wait_ge(added, n - 7)
                    for k in range(KT):
                        mm = pe.matmul(bank[n % 8][:], mixT[:, k, t * P:(t + 1) * P], w[:, k, e * HALF:(e + 1) * HALF],
                                       start=k == 0, stop=k == KT - 1)
                    mm.then_inc(product, 1)
            pe.wait_ge(added, 16)
            pe.wait_ge(scaled, KT)
            for h in range(2):
                for k in range(KT):
                    n = h * KT + k
                    if n >= 8:
                        pe.wait_ge(evacuated, n - 7)
                    for j in range(4):
                        mm = pe.transpose(bank[n % 8][:, j * P:(j + 1) * P], h2[:, 4 * h + j, k * P:(k + 1) * P], ident[:])
                    mm.then_inc(turned, 1)

        @block.vector
        def _(dve):
            for t in range(KT):
                dve.wait_ge(x_in[t], 16)
                for e in range(2):
                    n = 2 * t + e
                    dve.wait_ge(product, n + 1)
                    s = slice(e * HALF, (e + 1) * HALF)
                    nc.vector.tensor_tensor(x1[:, t, s], bank[n % 8][:], x1[:, t, s], ALU.add).then_inc(added, 1)
            dve.wait_ge(squares, KT)
            nc.vector.tensor_scalar(ss[:], ss[:], 1.0 / D, NORM_EPS, ALU.mult, ALU.add).then_inc(mean_eps, 1)
            dve.wait_ge(root, 1)
            nc.vector.reciprocal(rs[:], rs[:]).then_inc(rstd, 1)
            dve.wait_ge(rstd, 1)
            for t in range(KT):
                nc.vector.tensor_scalar(h2[:, t, :], x1[:, t, :], rs[:, t:t + 1], None, ALU.mult).then_inc(scaled, 1)
            for n in range(2 * KT):
                h, k = n // KT, n % KT
                dve.wait_ge(turned, n + 1)
                nc.vector.tensor_scalar(h2T[:, k, h * HALF:(h + 1) * HALF], bank[n % 8][:],
                                        cst["norms"][:, 8 + k:9 + k], None, ALU.mult).then_inc(evacuated, 1)
            dve.wait_ge(evacuated, 2 * KT)

        @block.scalar
        def _(act):
            for t in range(KT):
                act.wait_ge(added, 2 * t + 2)
                nc.scalar.activation(h2[:, t, :], x1[:, t, :], ACT.Square, accum_out=ss[:, t:t + 1]).then_inc(squares, 1)
            act.wait_ge(mean_eps, 1)
            nc.scalar.activation(rs[:], ss[:], ACT.Sqrt).then_inc(root, 1)


def _mlp(nc, sems, d, h2T, x1):
    with ExitStack() as ctx:
        sb = lambda n, s: ctx.enter_context(nc.sbuf_tensor(n, s, F32))
        w_up = [sb(f"f_up{i}", [P, KT, P]) for i in range(4)]
        w_down = sb("f_down", [P, FF_TILES, D])
        hid = sb("f_hid", [P, FF_TILES, SEQ])
        relu = [sb(f"f_relu{i}", [P, HALF]) for i in range(4)]
        bank = [ctx.enter_context(nc.psum_tensor(f"f_ps{i}", [P, HALF], F32)) for i in range(8)]
        up_in = [sems.enter_context(nc.semaphore(f"f_up_in{i}")) for i in range(4)]
        down_in = sems.enter_context(nc.semaphore("f_down_in"))
        N = 2 * FF_TILES
        pe_s = Steps(nc, sems, "f_pe", [f"up{n}" for n in range(N)] + [f"down{n}" for n in range(N)])
        act_s = Steps(nc, sems, "f_act", [f"relu{n}" for n in range(N)])
        dve_s = Steps(nc, sems, "f_dve", [f"sq{n}" for n in range(N)] + [f"add{n}" for n in range(N)])
        block = ctx.enter_context(nc.Block())

        @block.sync
        def _(sp):
            with sp.Fori(0, FF_GROUPS) as g:
                for t in range(FF_TILES):
                    (pe_s.need_before if t < 4 else pe_s.need)(sp, f"up{2 * ((t + 4) % 8) + 1}", g)
                    sp.dma_start(w_up[t % 4][:], d["w_up"][bass.ds(g * 8 + t, 1)].rearrange("o p k n -> p (o k) n")).then_inc(up_in[t % 4], 16)
                    if t == 3:
                        pe_s.need_before(sp, f"down{N - 1}", g)
                        sp.dma_start(w_down[:], d["w_down"][bass.ds(g, 1)].rearrange("o p k n -> p (o k) n")).then_inc(down_in, 16)

        @block.tensor
        def _(pe):
            pe_s.start(pe)
            with pe.Fori(0, FF_GROUPS) as g:
                for n in range(N):
                    t, h = n // 2, n % 2
                    if h == 0:
                        pe.wait_ge(up_in[t % 4], g * 32 + 16 * (t // 4 + 1))
                    if n < 8:
                        dve_s.need_before(pe, f"add{N - 8 + n}", g)
                    else:
                        act_s.need(pe, f"relu{n - 8}", g)
                    for k in range(KT):
                        mm = pe.matmul(bank[n % 8][:], w_up[t % 4][:, k, :], h2T[:, k, h * HALF:(h + 1) * HALF], start=k == 0, stop=k == KT - 1)
                    pe_s.done(mm, f"up{n}")
                pe.wait_ge(down_in, g * 16 + 16)
                dve_s.need(pe, f"sq{N - 1}", g)
                for n in range(N):
                    t, e = n // 2, n % 2
                    if n < 8:
                        act_s.need(pe, f"relu{N - 8 + n}", g)
                    else:
                        dve_s.need(pe, f"add{n - 8}", g)
                    for k in range(FF_TILES):
                        mm = pe.matmul(bank[n % 8][:], hid[:, k, t * P:(t + 1) * P], w_down[:, k, e * HALF:(e + 1) * HALF], start=k == 0, stop=k == FF_TILES - 1)
                    pe_s.done(mm, f"down{n}")

        @block.scalar
        def _(act):
            act_s.start(act)
            with act.Fori(0, FF_GROUPS) as g:
                for n in range(N):
                    pe_s.need(act, f"up{n}", g)
                    if n < 4:
                        dve_s.need_before(act, f"sq{N - 4 + n}", g)
                    else:
                        dve_s.need(act, f"sq{n - 4}", g)
                    act_s.done(nc.scalar.activation(relu[n % 4][:], bank[n % 8][:], ACT.Relu), f"relu{n}")

        @block.vector
        def _(dve):
            dve_s.start(dve)
            with dve.Fori(0, FF_GROUPS) as g:
                pe_s.need_before(dve, f"down{N - 1}", g)
                for n in range(N):
                    t, h = n // 2, n % 2
                    act_s.need(dve, f"relu{n}", g)
                    dve_s.done(nc.vector.tensor_tensor(hid[:, t, h * HALF:(h + 1) * HALF], relu[n % 4][:], relu[n % 4][:], ALU.mult), f"sq{n}")
                for n in range(N):
                    t, s = n // 2, slice((n % 2) * HALF, (n % 2 + 1) * HALF)
                    pe_s.need(dve, f"down{n}", g)
                    dve_s.done(nc.vector.tensor_tensor(x1[:, t, s], bank[n % 8][:], x1[:, t, s], ALU.add), f"add{n}")
            dve_s.need(dve, f"add{N - 1}", FF_GROUPS - 1)


def _finish(nc, sems, d, x1):
    with ExitStack() as ctx:
        sb = lambda n, s: ctx.enter_context(nc.sbuf_tensor(n, s, F32))
        gain = sb("e_gain", [P, D])
        out = sb("e_out", [P, KT, D])
        ss, rs = sb("e_ss", [P, 8]), sb("e_rs", [P, 8])
        sem = lambda n: sems.enter_context(nc.semaphore(n))
        gain_in, squares, mean_eps, root, rstd, scaled, stored = map(sem, ("e_gain_in", "e_squares", "e_mean", "e_root", "e_rstd", "e_scaled", "e_stored"))
        block = ctx.enter_context(nc.Block())

        @block.sync
        def _(sp):
            sp.dma_start(gain[:], d["norm_final"]).then_inc(gain_in, 16)
            for t in range(KT):
                sp.wait_ge(scaled, t + 1)
                sp.dma_start(d["out"][t * P:(t + 1) * P, :], out[:, t, :]).then_inc(stored, 16)
            sp.wait_ge(stored, 16 * KT)

        @block.scalar
        def _(act):
            for t in range(KT):
                nc.scalar.activation(out[:, t, :], x1[:, t, :], ACT.Square, accum_out=ss[:, t:t + 1]).then_inc(squares, 1)
            act.wait_ge(mean_eps, 1)
            nc.scalar.activation(rs[:], ss[:], ACT.Sqrt).then_inc(root, 1)

        @block.vector
        def _(dve):
            dve.wait_ge(squares, KT)
            nc.vector.tensor_scalar(ss[:], ss[:], 1.0 / D, NORM_EPS, ALU.mult, ALU.add).then_inc(mean_eps, 1)
            dve.wait_ge(root, 1)
            nc.vector.reciprocal(rs[:], rs[:]).then_inc(rstd, 1)
            dve.wait_ge(rstd, 1)
            dve.wait_ge(gain_in, 16)
            for t in range(KT):
                nc.vector.scalar_tensor_tensor(out[:, t, :], x1[:, t, :], rs[:, t:t + 1], gain[:], ALU.mult, ALU.mult).then_inc(scaled, 1)


def build(nc, d):
    with ExitStack() as outer, ExitStack() as sems:
        sb = lambda ctx, n, s, dt=F32: ctx.enter_context(nc.sbuf_tensor(n, s, dt))
        cst = {n: sb(outer, f"c_{n}", s) for n, s in (("ident", [P, P]), ("ones", [P, P]), ("block_ones", [P, P]),
                                                       ("level_mask", [P, 7, P]), ("restart", [P, HALF]), ("norms", [P, 18]))}
        cst["score_mask"] = sb(outer, "c_score_mask", [P, 4 * P], U32)
        x1 = sb(outer, "x1", [P, KT, D])
        hT = sb(outer, "hT", [P, KT, SEQ])
        _prepare(nc, sems, d, hT, cst)
        glaT = x1
        with ExitStack() as ctx:
            lora_wa, lora_g = sb(ctx, "lora_wa", [P, SEQ]), sb(ctx, "lora_g", [P, SEQ])
            with ExitStack() as low:
                gla_al = sb(low, "gla_al", [RANK, SEQ])
                _low_rank(nc, sems, d, hT, lora_wa, lora_g, gla_al, cst["norms"])
                _gla(nc, sems, d, hT, gla_al, glaT, cst)
            _rwkv(nc, sems, d, hT, lora_wa, lora_g, d["y_rwkv"], cst)
        with ExitStack() as ctx:
            mixT = sb(ctx, "mixT", [P, KT, SEQ])
            _merge(nc, sems, d, hT, glaT, d["y_rwkv"], mixT)
            _residual(nc, sems, d, mixT, x1, hT, cst)
        _mlp(nc, sems, d, hT, x1)
        _finish(nc, sems, d, x1)


def _tiles(np, w, width):
    r, c = w.shape
    return np.ascontiguousarray(w.reshape(r // P, P, c // width, width).transpose(2, 1, 0, 3))


def kernel(**inputs):
    import numpy as np
    import concourse.bacc as bacc
    from concourse.bass_utils import run_bass_kernel_spmd

    a = {k: np.asarray(v) for k, v in inputs.items()}
    w_in = a["w_in"][0]
    cols = lambda lo, n: w_in[:, lo:lo + n]
    gq, gk, gv, gog, gal = 0, 512, 1024, 2048, 3072
    rr = 3088
    rk, rv, rwl, rgl = rr + 1024, rr + 2048, rr + 3072, rr + 3200
    ga, gb = rr + 3328, rr + 4352
    group = lambda n, parts: np.concatenate([np.concatenate([cols(o + i * s, s) for o, s in parts], 1) for i in range(n)], 1)
    per_channel = lambda v: np.ascontiguousarray(v.reshape(-1, P).T)
    mu = a["rwkv_mu"][0]
    pair = np.stack([v.reshape(-1, P) for v in (mu[0:1024], mu[1024:2048], mu[2048:3072], a["rwkv_w0"][0], a["rwkv_a0"][0],
                                                a["rwkv_k_k"][0], a["rwkv_k_a"][0], a["rwkv_r_k"][0].reshape(-1),
                                                a["rwkv_ln_w"][0], a["rwkv_ln_b"][0])], -1)
    wa2 = np.concatenate([a["rwkv_w_w2"][0], a["rwkv_a_w2"][0]], 0).reshape(P, 8, P).transpose(1, 0, 2)
    g2 = a["rwkv_g_w2"][0].reshape(P, 8, P).transpose(1, 0, 2)
    i, j = np.arange(P)[:, None], np.arange(P)[None, :]
    strict, incl = (j > i), (j >= i)
    levels = [(j % 2 == 1) & (i == j - 1)] + [((i >> l) % 2 == 1) & ((j >> l) == (i >> l) - 1) for l in range(1, 7)]
    merge = np.stack([_tiles(np, m, P) for m in (cols(ga, 1024), cols(gb, 1024), a["w_branch_gla"][0], a["w_branch_rwkv"][0])], 3)
    arrays = {
        "x": a["x"][0],
        "w_gla": _tiles(np, group(4, ((gq, 128), (gk, 128), (gog, 256), (gv, 256))), 768),
        "w_rwkv": _tiles(np, group(8, ((rr, 128), (rk, 128), (rv, 128))), 384),
        "w_lora": _tiles(np, np.concatenate([cols(rwl, 256), cols(gal, 16)], 1), 272)[0],
        "w_merge": np.ascontiguousarray(merge.reshape(8, P, KT, 4 * P)),
        "w_out": _tiles(np, a["w_out"][0], D)[0],
        "w_up": _tiles(np, a["w_up"][0], P),
        "w_down": np.ascontiguousarray(a["w_down"][0].reshape(4, 8, P, D).transpose(0, 2, 1, 3)),
        "gla_a_w2": np.ascontiguousarray(a["gla_a_w2"][0].reshape(RANK, 4, P).transpose(1, 0, 2)),
        "gla_par": np.ascontiguousarray(np.concatenate([a["gla_a_b"][0].reshape(4, P, 1),
                                                        np.broadcast_to(per_channel(a["gla_norm"][0]), (4, P, 2))], 2)),
        "rwkv_pack": np.ascontiguousarray(np.concatenate([wa2, g2, pair], 2)),
        "norms": np.concatenate([per_channel(a["norm_mix"][0]), per_channel(a["norm_mlp"][0]), per_channel(mu[3072:3328])], 1),
        "norm_final": np.ascontiguousarray(np.broadcast_to(a["norm_final"], (P, D))),
        "ident": np.eye(P, dtype=np.float32),
        "ones": np.ones((P, P), np.float32),
        "block_ones": (i // HEAD == j // HEAD).astype(np.float32),
        "level_mask": np.ascontiguousarray(np.stack(levels, 1).astype(np.float32)),
        "score_mask": np.concatenate([strict, incl, strict, incl], 1).astype(np.uint32),
        "restart": np.ascontiguousarray(np.broadcast_to((np.arange(HALF) % CHUNK != 0).astype(np.float32), (P, HALF))),
    }
    nc = bacc.Bacc("TRN2", target_bir_lowering=False, num_devices=1)
    d = {n: nc.dram_tensor(f"in_{n}", v.shape, mybir.dt.from_np(v.dtype), kind="ExternalInput").ap() for n, v in arrays.items()}
    d["out"] = nc.dram_tensor("out", (SEQ, D), F32, kind="ExternalOutput").ap()
    d["y_rwkv"] = nc.dram_tensor("y_rwkv", (RWKV_PAIRS, P, SEQ), F32, kind="Internal").ap()
    build(nc, d)
    r = run_bass_kernel_spmd(nc, [{f"in_{n}": v for n, v in arrays.items()}], core_ids=[0])
    return r.results[0]["out"].reshape(1, SEQ, D)
```

```python
from contextlib import ExitStack

import concourse.bass as bass
from concourse import mybir

P = 128
F32 = mybir.dt.float32
F32R = mybir.dt.float32r
U32 = mybir.dt.uint32
ALU = mybir.AluOpType
ACT = mybir.ActivationFunctionType

D = 1024
SEQ = 1024
KT = D // P
HALF = 512
CHUNK = 128
NC = HALF // CHUNK
GLA_HEADS, GLA_DK, GLA_DV = 4, 128, 256
RANK = 16
RWKV_PAIRS = 8
HEAD = 64
LEVELS = 6
FF_GROUPS, FF_TILES = 8, 4
NORM_EPS, GLA_EPS, GN_EPS = 1e-6, 1e-5, 64e-5
DECAY = 0.6065306597126334
MU_R, MU_K, MU_V, W0, A0, K_K, K_A, R_K, LN_W, LN_B = range(10)
NPAR = 10


class Steps:

    def __init__(self, nc, sems, name, names):
        self.sem = sems.enter_context(nc.semaphore(name))
        self.names = {x: n for n, x in enumerate(names)}
        self.n = len(names)
        assert len(self.names) == self.n
        self.at = 0

    def start(self, eng):
        eng.sem_inc(self.sem, 2 * self.n)

    def done(self, ins, name):
        assert self.names[name] == self.at, (name, self.at)
        self.at = (self.at + 1) % self.n
        ins.then_inc(self.sem, 1)

    def need(self, eng, name, unit, back=0):
        eng.wait_ge(self.sem, unit * self.n + ((2 - back) * self.n + self.names[name] + 1))

    def need_before(self, eng, name, unit):
        self.need(eng, name, unit, 1)


def _prepare(nc, sems, d, hT_hi, hT_lo, cst):
    ident = cst["ident"]
    with ExitStack() as ctx:
        sb = lambda n, s: ctx.enter_context(nc.sbuf_tensor(n, s, F32))
        x = sb("p_x", [P, KT, D])
        junk = sb("p_junk", [P, D])
        ss = sb("p_ss", [P, 8])
        rs = sb("p_rs", [P, 8])
        bank = [ctx.enter_context(nc.psum_tensor(f"p_ps{i}", [P, HALF], F32)) for i in range(4)]
        x_in = [sems.enter_context(nc.semaphore(f"x_in{t}")) for t in range(KT)]
        const_in = sems.enter_context(nc.semaphore("const_in"))
        squares = sems.enter_context(nc.semaphore("squares"))
        mean_eps = sems.enter_context(nc.semaphore("mean_eps"))
        root = sems.enter_context(nc.semaphore("root"))
        rstd = sems.enter_context(nc.semaphore("rstd"))
        scaled = sems.enter_context(nc.semaphore("scaled"))
        turned = sems.enter_context(nc.semaphore("turned"))
        high = sems.enter_context(nc.semaphore("high"))
        evacuated = sems.enter_context(nc.semaphore("evacuated"))
        block = ctx.enter_context(nc.Block())

        @block.sync
        def _(sp):
            for t in range(KT):
                sp.dma_start(x[:, t, :], d["x"][t * P:(t + 1) * P, :]).then_inc(x_in[t], 16)
            n = 0
            for name in ("ident", "ones", "block_ones", "score_mask", "level_mask", "restart", "norms"):
                sp.dma_start(cst[name][:], d[name]).then_inc(const_in, 16)
                n += 16
            sp.wait_ge(const_in, n)

        @block.scalar
        def _(act):
            for t in range(KT):
                act.wait_ge(x_in[t], 16)
                if t:
                    act.wait_ge(squares, t)
                nc.scalar.activation(junk[:], x[:, t, :], ACT.Square, accum_out=ss[:, t:t + 1]).then_inc(squares, 1)
            act.wait_ge(mean_eps, 1)
            nc.scalar.activation(rs[:], ss[:], ACT.Sqrt).then_inc(root, 1)
            act.wait_ge(const_in, 16 * 7)
            for n in range(2 * KT):
                h, k = n // KT, n % KT
                act.wait_ge(turned, n + 1)
                nc.scalar.activation(hT_hi[:, k, h * HALF:(h + 1) * HALF], bank[n % 4][:], ACT.Copy,
                                     scale=cst["norms"][:, k:k + 1]).then_inc(high, 1)

        @block.vector
        def _(dve):
            dve.wait_ge(squares, KT)
            nc.vector.tensor_scalar(ss[:], ss[:], 1.0 / D, NORM_EPS, ALU.mult, ALU.add).then_inc(mean_eps, 1)
            dve.wait_ge(root, 1)
            nc.vector.reciprocal(rs[:], rs[:]).then_inc(rstd, 1)
            dve.wait_ge(rstd, 1)
            for t in range(KT):
                nc.vector.tensor_scalar(x[:, t, :], x[:, t, :], rs[:, t:t + 1], None, ALU.mult).then_inc(scaled, 1)
            dve.wait_ge(const_in, 16 * 7)
            for h in range(2):
                for k in range(KT):
                    n = h * KT + k
                    dve.wait_ge(high, n + 1)
                    s = slice(h * HALF, (h + 1) * HALF)
                    nc.vector.scalar_tensor_tensor(hT_lo[:, k, s], bank[n % 4][:], cst["norms"][:, k:k + 1],
                                                   hT_hi[:, k, s].bitcast(F32), ALU.mult, ALU.subtract).then_inc(evacuated, 1)
            dve.wait_ge(evacuated, 2 * KT)

        @block.tensor
        def _(pe):
            pe.wait_ge(const_in, 16 * 7)
            pe.wait_ge(scaled, KT)
            for h in range(2):
                for k in range(KT):
                    n = h * KT + k
                    if n >= 4:
                        pe.wait_ge(evacuated, n - 3)
                    for j in range(4):
                        mm = pe.transpose(bank[n % 4][:, j * P:(j + 1) * P],
                                          x[:, 4 * h + j, k * P:(k + 1) * P], ident[:])
                    mm.then_inc(turned, 1)


def _product(pe, out, w_hi, w_lo, x_hi, x_lo, first, last):
    pe.matmul(out, w_hi, x_hi, start=first, stop=False)
    pe.matmul(out, w_hi, x_lo, start=False, stop=False)
    return pe.matmul(out, w_lo, x_hi, start=False, stop=last)


def _whole(nc, sems, hT_hi, hT_lo, hT):
    with ExitStack() as ctx:
        summed, summed_pool = (sems.enter_context(nc.semaphore(n)) for n in ("h_summed", "h_summed_pool"))
        block = ctx.enter_context(nc.Block())
        cut = 6

        def add(eng, lo, hi, sem):
            for k in range(lo, hi):
                eng.tensor_tensor(hT[:, k, :], hT_hi[:, k, :].bitcast(F32), hT_lo[:, k, :].bitcast(F32), ALU.add).then_inc(sem, 1)

        @block.vector
        def _(dve):
            add(nc.vector, 0, cut, summed)
            dve.wait_ge(summed, cut)

        @block.gpsimd
        def _(pool):
            add(nc.gpsimd, cut, KT, summed_pool)
            pool.wait_ge(summed_pool, KT - cut)


def _low_rank(nc, sems, d, hT_hi, hT_lo, lora_wa, lora_g, gla_al, norms):
    with ExitStack() as ctx:
        sb = lambda n, s: ctx.enter_context(nc.sbuf_tensor(n, s, F32))
        w = sb("l_w", [P, KT, 272])
        w_hi, w_lo = (ctx.enter_context(nc.sbuf_tensor(f"l_w_{x}", [P, KT, 272], F32R)) for x in ("hi", "lo"))
        raw = [sb(f"l_raw{i}", [P, 1 + SEQ]) for i in range(2)]
        diff = sb("l_diff", [P, SEQ])
        bank = [ctx.enter_context(nc.psum_tensor(f"l_ps{i}", [P, HALF], F32)) for i in range(6)]
        sem = lambda n: sems.enter_context(nc.semaphore(n))
        w_split = sem("l_w_split")
        w_in, product, copied, zeroed, shifted, gated = map(sem, ("l_w_in", "l_product", "l_copied", "l_zeroed", "l_shifted", "l_gated"))
        block = ctx.enter_context(nc.Block())

        @block.sync
        def _(sp):
            sp.dma_start(w[:], d["w_lora"]).then_inc(w_in, 16)

        @block.tensor
        def _(pe):
            pe.wait_ge(w_split, 2)
            for n in range(6):
                q, h = n // 2, n % 2
                a, b = ((0, P), (P, 2 * P), (2 * P, 2 * P + RANK))[q]
                for k in range(KT):
                    mm = _product(pe, bank[n][0:b - a, :], w_hi[:, k, a:b], w_lo[:, k, a:b], hT_hi[:, k, h * HALF:(h + 1) * HALF],
                                  hT_lo[:, k, h * HALF:(h + 1) * HALF], k == 0, k == KT - 1)
                mm.then_inc(product, 1)

        @block.scalar
        def _(act):
            act.wait_ge(w_in, 16)
            nc.scalar.activation(w_hi[:], w[:], ACT.Copy).then_inc(w_split, 1)
            for n in range(6):
                q, h = n // 2, n % 2
                act.wait_ge(product, n + 1)
                if q < 2:
                    out, src = raw[q][:, 1 + h * HALF:1 + (h + 1) * HALF], bank[n][:]
                else:
                    out, src = gla_al[0:RANK, h * HALF:(h + 1) * HALF], bank[n][0:RANK, :]
                nc.scalar.activation(out, src, ACT.Copy).then_inc(copied, 1)
            act.wait_ge(shifted, 4)
            nc.scalar.activation(lora_wa[0:HEAD, :], lora_wa[0:HEAD, :], ACT.Tanh).then_inc(gated, 1)
            nc.scalar.activation(lora_g[:], lora_g[:], ACT.Tanh, scale=0.5).then_inc(gated, 1)

        @block.vector
        def _(dve):
            for q in range(2):
                nc.vector.memset(raw[q][:, 0:1], 0.0).then_inc(zeroed, 1)
            dve.wait_ge(w_split, 1)
            nc.vector.tensor_tensor(w_lo[:], w[:], w_hi[:].bitcast(F32), ALU.subtract).then_inc(w_split, 1)
            dve.wait_ge(zeroed, 2)
            for q, out in enumerate((lora_wa, lora_g)):
                dve.wait_ge(copied, 2 * q + 2)
                if q:
                    dve.wait_ge(shifted, 2)
                nc.vector.tensor_tensor(diff[:], raw[q][:, 0:SEQ], raw[q][:, 1:1 + SEQ], ALU.subtract).then_inc(shifted, 1)
                dve.wait_ge(shifted, 2 * q + 1)
                nc.vector.scalar_tensor_tensor(out[:], diff[:], norms[:, 16 + q:17 + q], raw[q][:, 1:1 + SEQ],
                                               ALU.mult, ALU.add).then_inc(shifted, 1)
            dve.wait_ge(gated, 2)
            nc.vector.tensor_scalar(lora_g[:], lora_g[:], 0.5, 0.5, ALU.mult, ALU.add).then_inc(gated, 1)
            dve.wait_ge(gated, 3)


def _gla(nc, sems, d, hT_hi, hT_lo, gla_al, y_dram, cst):
    ident, ones = cst["ident"], cst["ones"]
    causal = cst["score_mask"][:, P:2 * P]
    with ExitStack() as ctx:
        sb = lambda n, s, dt=F32: ctx.enter_context(nc.sbuf_tensor(n, s, dt))
        t = lambda n: sb(n, [P, HALF])
        two = lambda n, s=(P, HALF): [sb(f"{n}{h}", list(s)) for h in range(2)]
        PROJ = ("k", "q", "og0", "og1")
        raw = [sb(f"g_raw{i}", [P, D]) for i in range(2)]
        w_hi, w_lo = ([sb(f"g_w_{n}_{x}", [P, D], F32R) for n in PROJ] for x in ("hi", "lo"))
        wv_hi, wv_lo = (sb(f"g_w_v_{x}", [P, KT * GLA_DV], F32R) for x in ("hi", "lo"))
        aw = sb("g_aw", [RANK, P])
        par_all, par_now = sb("g_par_all", [P, GLA_HEADS, 3]), two("g_par", (P, 3))
        az, mz, la, cum, up, down = map(t, ("g_az", "g_mz", "g_la", "g_cum", "g_up", "g_down"))
        silu_t = [t(f"g_silu_t{x}") for x in range(2)]
        q, k = two("g_q"), two("g_k")
        v, silu, small = two("g_v", (P, NC, GLA_DV)), two("g_silu", (P, 2, HALF)), two("g_small", (P, 4 * NC))
        k_tok, scores = t("g_kt"), sb("g_scores", [P, NC, CHUNK])
        state = [sb(f"g_state{i}", [P, GLA_DV]) for i in range(2)]
        o, sq, rs = sb("g_o", [P, 2, HALF]), sb("g_sq", [P, 2, HALF]), t("g_rs")
        y_out = two("g_yout", (P, 2, HALF))
        touch, eps = sb("g_touch", [P, 1]), sb("g_eps", [P, 1])
        bank = [ctx.enter_context(nc.psum_tensor(f"g_ps{i}", [P, HALF], F32)) for i in range(8)]
        sem = lambda n: sems.enter_context(nc.semaphore(n))
        stored = [sem(f"g_stored{h}") for h in range(2)]
        raw_in = [sem(f"g_raw_in{n}") for n in range(2)]
        aw_in, par_in, zeroed = map(sem, ("g_aw_in", "g_par_in", "g_zeroed"))
        pf = Steps(nc, sems, "g_pe_front", ["z", "k", "q", "og0", "og1", "v0", "v1"])
        af = Steps(nc, sems, "g_act_front", ["abs_z", "exp_z", "log_z", "k", "up", "down", "mid", "decay", "q", "og0", "og1", "v0", "v1"])
        df = Steps(nc, sems, "g_dve_front", ["par", "min_z", "log_a", "cum", "mid", "from_mid", "to_end", "to_next", "k", "q",
                                             "half0", "silu0", "half1", "silu1"])
        pb = Steps(nc, sems, "g_pe_back", ["k_tok", "scores"] + [f"{x}{c}" for c in range(NC) for x in ("state", "o")] + ["mean"])
        ab = Steps(nc, sems, "g_act_back", ["k_tok"] + [f"state{c}" for c in range(NC)] + ["o0", "o1", "sq0", "sq1", "var_log", "rstd"])
        db = Steps(nc, sems, "g_dve_back", ["scores", "start", "n0", "n1", "y0", "y1"])
        WEIGHTS = PROJ + ("v_low", "v_high")
        sa, sd = Steps(nc, sems, "g_act_split", WEIGHTS), Steps(nc, sems, "g_dve_split", WEIGHTS)
        block = ctx.enter_context(nc.Block())
        last = GLA_HEADS - 1

        def parts(name):
            n = WEIGHTS.index(name)
            if n < 4:
                return w_hi[n][:], w_lo[n][:]
            s = slice((n - 4) * D, (n - 3) * D)
            return wv_hi[:, s], wv_lo[:, s]

        def act_split(act, name, g):
            n = WEIGHTS.index(name)
            pf.need(act, name if n < 4 else "v1", g * 2, 1)
            act.wait_ge(raw_in[n % 2], g * 48 + 16 * (n // 2 + 1))
            sa.done(nc.scalar.activation(parts(name)[0], raw[n % 2][:], ACT.Copy), name)

        def dve_split(dve, name, g):
            hi, lo = parts(name)
            sa.need(dve, name, g)
            sd.done(nc.vector.tensor_tensor(lo, raw[WEIGHTS.index(name) % 2][:], hi.bitcast(F32), ALU.subtract), name)

        def walk(eng, front, back, split=lambda g: None):
            split(0)
            for _ in front(0, 0):
                pass
            back(0, 0, front(0, 1))
            with eng.Fori(0, last) as g:
                split(g + 1)
                back(g, 1, front(g + 1, 0))
                back(g + 1, 0, front(g + 1, 1))
            back(last, 1, None)

        @block.sync
        def _(sp):
            sp.dma_start(par_all[:], d["gla_par"]).then_inc(par_in, 16)

            def load(g):
                pf.need(sp, "z", g * 2, 1)
                sp.dma_start(aw[:], d["gla_a_w2"][bass.ds(g, 1)].rearrange("o p n -> p (o n)")).then_inc(aw_in, 16)
                for n, name in enumerate(WEIGHTS):
                    if n < 2:
                        sd.need_before(sp, WEIGHTS[n - 2], g)
                    else:
                        sd.need(sp, WEIGHTS[n - 2], g)
                    if n < 4:
                        src = d["w_gla"][bass.ds(g * 4 + n, 1)].rearrange("o p k n -> p (o k n)")
                    else:
                        src = d["w_gla_v"][bass.ds(g, 1), :, (n - 4) * 4:(n - 3) * 4].rearrange("o p k n -> p (o k n)")
                    sp.dma_start(raw[n % 2][:], src).then_inc(raw_in[n % 2], 16)

            def store(g):
                for h in range(2):
                    db.need(sp, "y1", g * 2 + h)
                    sp.dma_start(y_dram[bass.ds(g, 1), :, :, h * HALF:(h + 1) * HALF].rearrange("o x p t -> p (o x) t"), y_out[h][:]).then_inc(stored[h], 16)

            load(0)
            with sp.Fori(0, last) as g:
                load(g + 1)
                store(g)
            store(last)
            for h in range(2):
                sp.wait_ge(stored[h], 16 * GLA_HEADS + 16)

        @block.tensor
        def _(pe):
            pf.start(pe)
            pb.start(pe)

            def front(g, h):
                u = g * 2 + h
                tok = slice(h * HALF, (h + 1) * HALF)
                af.need(pe, "v0", u, 1)
                pe.wait_ge(aw_in, g * 16 + 16)
                pf.done(pe.matmul(bank[2][:], aw[:], gla_al[0:RANK, tok], start=True, stop=True), "z")
                yield
                free = (lambda: af.need(pe, "v1", u, 1), lambda: df.need(pe, "silu1", u, 1),
                        lambda: af.need(pe, "k", u), lambda: af.need(pe, "q", u))
                for n, name in enumerate(PROJ):
                    free[n]()
                    if h == 0:
                        sd.need(pe, name, g)
                    for kt in range(KT):
                        cols = slice(kt * P, (kt + 1) * P)
                        mm = _product(pe, bank[n % 2][:], w_hi[n][:, cols], w_lo[n][:, cols], hT_hi[:, kt, tok], hT_lo[:, kt, tok],
                                      kt == 0, kt == KT - 1)
                        if kt == KT - 1:
                            pf.done(mm, name)
                        yield
                df.need(pe, "min_z", u)
                if h == 0:
                    sd.need(pe, "v_high", g)
                for j in range(2):
                    if j:
                        df.need(pe, "silu0", u)
                    for c in range(2):
                        t0 = h * HALF + (2 * j + c) * P
                        for kt in range(KT):
                            cols = slice(kt * GLA_DV, (kt + 1) * GLA_DV)
                            mm = _product(pe, bank[(2, 0)[j]][:, c * GLA_DV:(c + 1) * GLA_DV], hT_hi[:, kt, t0:t0 + P], hT_lo[:, kt, t0:t0 + P],
                                          wv_hi[:, cols], wv_lo[:, cols], kt == 0, kt == KT - 1)
                            if c == 1 and kt == KT - 1:
                                pf.done(mm, f"v{j}")
                            if kt % 2:
                                yield

            def back(g, h, fill):
                u = g * 2 + h
                df.need(pe, "k", u)
                ab.need(pe, "var_log", u, 1)
                for c in range(NC):
                    s = slice(c * P, (c + 1) * P)
                    mm = pe.transpose(bank[5][:, s], k[h][:, s], ident[:])
                pb.done(mm, "k_tok")
                df.need(pe, "q", u)
                for c in range(NC):
                    s = slice(c * P, (c + 1) * P)
                    mm = pe.matmul(bank[6][:, s], k[h][:, s], q[h][:, s], start=True, stop=True)
                pb.done(mm, "scores")
                _advance(fill, 5)
                ab.need(pe, "k_tok", u)
                af.need(pe, "v1", u)
                for c in range(NC):
                    s = slice(c * P, (c + 1) * P)
                    if c:
                        ab.need(pe, f"state{c - 1}", u)
                    else:
                        db.need(pe, "start", u)
                    pe.matmul(bank[7][:, 0:GLA_DV], k_tok[:, s], v[h][:, c, :], start=True, stop=False)
                    mm = pe.matmul(bank[7][:, 0:GLA_DV], ident[:], state[c % 2][:], start=False, stop=True)
                    pb.done(mm, f"state{c}")
                    if c == 0:
                        db.need(pe, "scores", u)
                        ab.need(pe, "sq1", u, 1)
                    for x in range(2):
                        vs = slice(x * P, (x + 1) * P)
                        pe.matmul(bank[3 + x][:, s], v[h][:, c, vs], scores[:, c, :], start=True, stop=False)
                        mm = pe.matmul(bank[3 + x][:, s], state[c % 2][:, vs], q[h][:, s], start=False, stop=True)
                    pb.done(mm, f"o{c}")
                    _advance(fill, (7, 7, 7, 6)[c])
                ab.need(pe, "sq1", u)
                pe.matmul(bank[5][:], ones[:], sq[:, 0, :], start=True, stop=False)
                pb.done(pe.matmul(bank[5][:], ones[:], sq[:, 1, :], start=False, stop=True), "mean")
                _advance(fill, 100)

            walk(pe, front, back)

        @block.scalar
        def _(act):
            af.start(act)
            ab.start(act)
            A = nc.scalar.activation
            sa.start(act)
            act.wait_ge(zeroed, 2)

            def front(g, h):
                u = g * 2 + h
                sm = small[h]
                split = (lambda name: act_split(act, name, g)) if h == 0 else lambda name: None
                split("q")
                pf.need(act, "z", u)
                df.need(act, "par", u)
                df.need(act, "log_a", u, 1)
                af.done(A(az[:], bank[2][:], ACT.Abs, bias=par_now[h][:, 0:1]), "abs_z")
                af.need(act, "abs_z", u)
                af.done(A(az[:], az[:], ACT.Exp, scale=-1.0), "exp_z")
                af.need(act, "exp_z", u)
                af.done(A(az[:], az[:], ACT.Ln, bias=1.0), "log_z")
                split("og0")
                yield
                pf.need(act, "k", u)
                af.done(A(k[h][:], bank[0][:], ACT.Copy), "k")
                split("og1")
                yield
                df.need(act, "q", u, 1)
                df.need(act, "to_next", u)
                af.done(A(up[:], la[:], ACT.Exp, scale=1 / 16), "up")
                af.done(A(down[:], la[:], ACT.Exp, scale=-1 / 16), "down")
                af.done(A(sm[:, 2 * NC:3 * NC], sm[:, 0:NC], ACT.Exp, scale=1 / 16), "mid")
                af.done(A(sm[:, 3 * NC:4 * NC], sm[:, NC:2 * NC], ACT.Exp, scale=1 / 16), "decay")
                split("v_low")
                yield
                pf.need(act, "q", u)
                af.done(A(q[h][:], bank[1][:], ACT.Copy, scale=GLA_DK ** -0.5), "q")
                split("v_high")
                yield
                for x in range(2):
                    pf.need(act, f"og{x}", u)
                    df.need(act, f"silu{x}", u, 1)
                    af.done(A(silu_t[x][:], bank[x][:], ACT.Tanh, scale=0.5), f"og{x}")
                    yield
                for x in range(2):
                    pf.need(act, f"v{x}", u)
                    af.done(A(v[h][:, 2 * x:2 * x + 2, :].rearrange("p a b -> p (a b)"), bank[(2, 0)[x]][:], ACT.Copy), f"v{x}")
                    yield

            def back(g, h, fill):
                u = g * 2 + h
                pb.need(act, "k_tok", u)
                ab.done(A(k_tok[:], bank[5][:], ACT.Copy), "k_tok")
                _advance(fill, 1)
                af.need(act, "decay", u)
                for c in range(NC):
                    pb.need(act, f"state{c}", u)
                    if c:
                        pb.need(act, f"o{c - 1}", u)
                    ab.done(A(state[(c + 1) % 2][:], bank[7][:, 0:GLA_DV], ACT.Copy,
                              scale=small[h][:, 3 * NC + c:3 * NC + c + 1]), f"state{c}")
                    _advance(fill, 1)
                pb.need(act, f"o{NC - 1}", u)
                db.need(act, "y1", u, 1)
                for x in range(2):
                    ab.done(A(o[:, x, :], bank[3 + x][:], ACT.Copy), f"o{x}")
                for x in range(2):
                    ab.done(A(sq[:, x, :], bank[3 + x][:], ACT.Square, scale=GLA_DV ** -0.5), f"sq{x}")
                _advance(fill, 1)
                pb.need(act, "mean", u)
                ab.done(A(rs[:], bank[5][:], ACT.Ln, bias=eps[:, 0:1]), "var_log")
                ab.need(act, "var_log", u)
                ab.done(A(rs[:], rs[:], ACT.Exp, scale=-0.5), "rstd")
                _advance(fill, 100)

            walk(act, front, back, lambda g: act_split(act, "k", g))

        @block.vector
        def _(dve):
            V = nc.vector
            for x in stored:
                dve.sem_inc(x, 16)
            V.memset(scores[:], 0.0).then_inc(zeroed, 1)
            V.memset(eps[:], GLA_EPS).then_inc(zeroed, 1)
            dve.wait_ge(zeroed, 2)
            dve.wait_ge(par_in, 16)
            df.start(dve)
            db.start(dve)
            sd.start(dve)

            def front(g, h):
                u = g * 2 + h
                split = (lambda name: dve_split(dve, name, g)) if h == 0 else lambda name: None
                split("q")
                ab.need(dve, f"state{NC - 1}", u, 2)
                df.done(V.tensor_scalar(par_now[h][:], par_all[:, bass.ds(g, 1), :].rearrange("p o n -> p (o n)"), 1.0, None, ALU.mult), "par")
                df.need(dve, "par", u)
                af.need(dve, "abs_z", u)
                df.done(V.tensor_scalar(mz[:], bank[2][:], par_now[h][:, 0:1], 0.0, ALU.add, ALU.min), "min_z")
                df.need(dve, "min_z", u)
                af.need(dve, "log_z", u)
                df.done(V.tensor_tensor(la[:], mz[:], az[:], ALU.subtract), "log_a")
                df.need(dve, "log_a", u)
                df.done(V.tensor_tensor_scan(cum[:], cst["restart"][:], la[:], 0.0, ALU.mult, ALU.add), "cum")
                _chunk_small(nc, dve, df, u, cum, la, small[h])
                split("og0")
                split("og1")
                yield
                for name, x, factor in (("k", k, down), ("q", q, up)):
                    af.need(dve, name, u)
                    af.need(dve, "down", u)
                    df.done(V.tensor_tensor(x[h][:], x[h][:], factor[:], ALU.mult), name)
                    split("v_low" if name == "k" else "v_high")
                    yield
                for x in range(2):
                    af.need(dve, f"og{x}", u)
                    df.done(V.tensor_scalar(silu_t[x][:], silu_t[x][:], 0.5, 0.5, ALU.mult, ALU.add), f"half{x}")
                    df.need(dve, f"half{x}", u)
                    df.done(V.tensor_tensor(silu[h][:, x, :], bank[x][:], silu_t[x][:], ALU.mult), f"silu{x}")
                    yield

            def back(g, h, fill):
                u = g * 2 + h
                pb.need(dve, "scores", u)
                V.memset(touch[:], 0.0)
                db.done(V.copy_predicated(scores[:], _over(causal, NC), bank[6][:].rearrange("p (c t) -> p c t", c=NC)), "scores")
                ab.need(dve, f"state{NC - 1}", u, 1)
                if h == 0:
                    db.done(V.memset(state[0][:], 0.0), "start")
                else:
                    af.need(dve, "mid", u)
                    db.done(V.tensor_scalar(state[0][:], state[0][:], small[h][:, 2 * NC:2 * NC + 1], None, ALU.mult), "start")
                _advance(fill, 100)
                ab.need(dve, "rstd", u)
                for x in range(2):
                    db.done(V.scalar_tensor_tensor(o[:, x, :], o[:, x, :], par_now[h][:, 1 + x:2 + x], rs[:], ALU.mult, ALU.mult), f"n{x}")
                for x in range(2):
                    db.need(dve, f"n{x}", u)
                    if x == 0:
                        dve.wait_ge(stored[h], g * 16 + 16)
                    db.done(V.tensor_tensor(y_out[h][:, x, :], o[:, x, :], silu[h][:, x, :], ALU.mult), f"y{x}")

            walk(dve, front, back, lambda g: dve_split(dve, "k", g))


def _over(mask, n):
    return mask.rearrange("p (o t) -> p o t", o=1).to_broadcast([P, n, CHUNK])


def _chunk_small(nc, dve, dve_s, u, cum, out, small):
    c3 = cum[:].rearrange("p (c t) -> p c t", c=NC)
    mid, end = c3[:, :, CHUNK // 2 - 1:CHUNK // 2], c3[:, :, CHUNK - 1:CHUNK]
    s3 = small[:].rearrange("p (k c o) -> p k c o", k=4, o=1)
    dve_s.need(dve, "cum", u)
    dve_s.done(nc.vector.tensor_copy(s3[:, 0], mid), "mid")
    dve_s.need(dve, "mid", u)
    dve_s.done(nc.vector.tensor_tensor(out[:].rearrange("p (c t) -> p c t", c=NC), c3,
                                       s3[:, 0].to_broadcast([P, NC, CHUNK]), ALU.subtract), "from_mid")
    dve_s.done(nc.vector.tensor_tensor(s3[:, 1], end, s3[:, 0], ALU.subtract), "to_end")
    dve_s.need(dve, "to_end", u)
    dve_s.done(nc.vector.tensor_tensor(s3[:, 1, 0:NC - 1], s3[:, 1, 0:NC - 1], s3[:, 0, 1:NC], ALU.add), "to_next")


def _advance(steps, n):
    for _ in range(n if steps else 0):
        next(steps, None)


def _rwkv(nc, sems, d, hT, lora_wa, lora_g, y_dram, cst):
    ident, block_ones = cst["ident"], cst["block_ones"]
    with ExitStack() as ctx:
        sb = lambda n, s, dt=F32: ctx.enter_context(nc.sbuf_tensor(n, s, dt))
        t = lambda n: sb(n, [P, HALF])
        two = lambda n, s=(P, HALF): [sb(f"{n}{h}", list(s)) for h in range(2)]
        w = [sb(f"r_w{n}", [P, KT, P]) for n in range(3)]
        lora2, gate2 = sb("r_lora2", [P, P]), sb("r_gate2", [P, P])
        par_all, par_now = sb("r_par_all", [P, RWKV_PAIRS, NPAR]), two("r_par", (P, NPAR))
        half_par = sb("r_half_par", [P, 2])
        raw = [sb(f"r_raw{i}", [P, 1 + SEQ]) for i in range(3)]
        diff = [t(f"r_diff{n}") for n in range(3)]
        r, k, log_w, cum, from_mid, a, kk, sq, norm = map(t, ("r_r", "r_k", "r_lw", "r_cum", "r_fm", "r_a", "r_kk", "r_sq", "r_norm"))
        up, down, prev = map(t, ("r_up", "r_down", "r_prev"))
        gain = sq
        rk = from_mid
        v, k_bar, b_bar, gate, bonus = map(two, ("r_v", "r_kbar", "r_bbar", "r_gate", "r_bonus"))
        ar, small = two("r_ar", (P, NC, 2, CHUNK)), two("r_small", (P, 4 * NC))
        k_tok, b_tok, v_tok = map(t, ("r_kt", "r_bt", "r_vt"))
        scores = sb("r_scores", [P, 2 * NC, 4, CHUNK])
        tiles = lambda n: [sb(f"{n}{b}", [P, 4, CHUNK], F32R) for b in range(2)]
        a_hi, a_lo, invT, inv, prod = map(tiles, ("r_ahi", "r_alo", "r_invT", "r_inv", "r_prod"))
        inverseT = [sb(f"r_inverseT{b}", [P, 4, CHUNK]) for b in range(2)]
        ident_r, minus_r = sb("r_ident", [P, P], F32R), sb("r_minus", [P, P], F32R)
        z, uu = sb("r_z", [P, P]), sb("r_u", [P, P])
        state = [sb(f"r_state{i}", [P, P]) for i in range(2)]
        y, ysq, ln = two("r_y"), t("r_ysq"), two("r_ln", (P, 2))
        y_out = two("r_yout")
        touch, eps = sb("r_touch", [P, 2 * NC]), sb("r_eps", [P, 1])
        bank = [ctx.enter_context(nc.psum_tensor(f"r_ps{i}", [P, HALF], F32)) for i in range(8)]
        sem = lambda n: sems.enter_context(nc.semaphore(n))
        w_in = [sem(f"r_w_in{n}") for n in range(3)]
        lora2_in, gate2_in, par_in, zeroed = map(sem, ("r_lora2_in", "r_gate2_in", "r_par_in", "r_zeroed"))
        stored = [sem(f"r_stored{h}") for h in range(2)]
        ab2, levels = range(2), range(1, LEVELS + 1)
        PROJ = ("k", "r", "v")
        pf = Steps(nc, sems, "pe_front", ["w", "a", "k", "norm", "r", "v", "gate", "bonus"])
        af = Steps(nc, sems, "act_front", ["w", "a", "up", "down", "k", "prev", "kk_sq", "mid", "decay",
                                           "norm_log", "norm_inv", "r", "v", "gate"])
        gf = Steps(nc, sems, "pool_front", ["k_diff", "r_diff", "v_diff"])
        df = Steps(nc, sems, "dve_front", ["par", "half_par", "log_w", "cum", "mid", "from_mid", "to_end", "to_next", "from_prev",
                                           "a", "k_gain", "k", "kk", "k_mod", "k_bar", "norm_floor", "kk_unit", "b", "b_bar", "a_prev",
                                           "r", "r_up", "rk", "v", "bonus", "ln"])
        pb = Steps(nc, sems, "pe_back", ["k_tok", "b_tok"] + [f"scores{j}" for j in range(2 * NC)] + ["v_tok", "inv0.0", "inv0.1"]
                   + [f"{x}{l}.{b}" for l in levels for x in ("prod", "inv") for b in ab2]
                   + [f"{x}{b}" for x in ("res", "inverse") for b in ab2]
                   + [f"{x}{c}" for c in range(NC) for x in ("z", "u", "s", "y")])
        ab = Steps(nc, sems, "act_back", ["k_tok", "b_tok", "v_tok", "a_hi0", "a_hi1"] + [f"invT{l}.{b}" for l in levels for b in ab2]
                   + ["res0", "res1"] + [f"{x}{c}" for c in range(NC) for x in ("z", "s")] + ["y"])
        gb = Steps(nc, sems, "pool_back", ["a_lo0", "a_lo1"])
        db = Steps(nc, sems, "dve_back", [f"scores{j}" for j in range(2 * NC)] + [f"{x}{b}" for b in ab2 for x in ("invT_mask", "invT0.")]
                   + ["inv0.0", "inv0.1"] + [f"{x}{l}.{b}" for l in levels for x in ("prod", "inv") for b in ab2]
                   + ["inverse0", "inverse1", "start0", "start1"] + [f"{x}{c}" for c in range(NC) for x in ("u", "s")])
        pn = Steps(nc, sems, "pe_norm", ["mean", "var"])
        an = Steps(nc, sems, "act_norm", ["y_sq", "var", "var_log", "rstd"])
        dn = Steps(nc, sems, "dve_norm", ["centred", "n", "affine", "plus", "out"])
        block = ctx.enter_context(nc.Block())
        end, last = f"y{NC - 1}", RWKV_PAIRS - 1

        def walk(eng, front, back):
            for _ in front(0, 0, False):
                pass
            back(0, 0, front(0, 1, False))
            with eng.Fori(0, last) as p:
                back(p, 1, front(p + 1, 0, True))
                back(p + 1, 0, front(p + 1, 1, True))
            back(last, 1, front(RWKV_PAIRS, 0, True, False))
            for _ in front(RWKV_PAIRS, 1, True, False):
                pass

        @block.sync
        def _(sp):
            sp.dma_start(par_all[:], d["rwkv_par"]).then_inc(par_in, 16)

            def load(p):
                pf.need(sp, "a", p * 2, 1)
                sp.dma_start(lora2[:], d["rwkv_lora2"][bass.ds(p, 1)].rearrange("o p n -> p (o n)")).then_inc(lora2_in, 16)
                for n, name in enumerate(PROJ):
                    pf.need(sp, name, p * 2, 1)
                    sp.dma_start(w[n][:], d["w_rwkv"][bass.ds(p * 3 + n, 1)].rearrange("o p k n -> p (o k) n")).then_inc(w_in[n], 16)
                pf.need(sp, "gate", p * 2, 1)
                sp.dma_start(gate2[:], d["rwkv_g2"][bass.ds(p, 1)].rearrange("o p n -> p (o n)")).then_inc(gate2_in, 16)

            def store(p):
                for h in range(2):
                    dn.need(sp, "out", p * 2 + h)
                    sp.dma_start(y_dram[bass.ds(p, 1), :, h * HALF:(h + 1) * HALF].rearrange("o p t -> p (o t)"), y_out[h][:]).then_inc(stored[h], 16)

            load(0)
            with sp.Fori(0, last) as p:
                load(p + 1)
                store(p)
            store(last)
            for h in range(2):
                sp.wait_ge(stored[h], 16 * RWKV_PAIRS + 16)

        @block.tensor
        def _(pe):
            pf.start(pe)
            pb.start(pe)
            pn.start(pe)

            def front(p, h, norm_, next_=True):
                u = p * 2 + h
                tok = slice(h * HALF, (h + 1) * HALF)

                def low_rank(b, name, lhsT, rhs):
                    return pf.done(pe.matmul(bank[b][:], lhsT, rhs, start=True, stop=True), name)

                def project(name, free, first, end_):
                    n = PROJ.index(name)
                    if first == 0:
                        free()
                        pe.wait_ge(w_in[n], p * 16 + 16)
                    for kt in range(first, end_):
                        mm = pe.matmul(bank[0][:], w[n][:, kt, :], hT[:, kt, tok], start=kt == 0, stop=kt == KT - 1)
                        if kt == KT - 1:
                            pf.done(mm, name)
                        yield

                def var():
                    if norm_:
                        an.need(pe, "y_sq", u - 2)
                        if next_:
                            af.need(pe, "a", u)
                        elif h == 0:
                            af.need(pe, "gate", u, 1)
                        pn.done(pe.matmul(bank[1][:], block_ones[:], ysq[:], start=True, stop=True), "var")
                if norm_:
                    if next_ or h == 0:
                        df.need(pe, "bonus", u, 1)
                    else:
                        dn.need(pe, "centred", u - 3)
                    ab.need(pe, "y", u - 2)
                    pn.done(pe.matmul(bank[0][:], block_ones[:], y[h][:], start=True, stop=True), "mean")
                yield
                if not next_:
                    yield from (None,) * 4
                    var()
                    return
                af.need(pe, "gate", u, 1)
                pe.wait_ge(lora2_in, p * 16 + 16)
                low_rank(1, "w", lora2[0:HEAD, :], lora_wa[0:HEAD, tok])
                yield
                free_k = lambda: dn.need(pe, "centred", u - 2) if norm_ else df.need(pe, "bonus", u, 1)
                yield from project("k", free_k, 0, 1)
                af.need(pe, "w", u)
                low_rank(1, "a", lora2[HEAD:P, :], lora_wa[HEAD:P, tok])
                yield
                yield from project("k", None, 1, KT)
                var()
                yield
                yield from project("r", lambda: af.need(pe, "k", u), 0, 3)
                if norm_:
                    an.need(pe, "var", u - 2)
                else:
                    af.need(pe, "a", u)
                af.need(pe, "kk_sq", u)
                low_rank(1, "norm", block_ones[:], sq[:])
                yield
                yield from project("r", None, 3, KT)
                yield from project("v", lambda: af.need(pe, "r", u), 0, KT)
                df.need(pe, "norm_floor", u)
                pe.wait_ge(gate2_in, p * 16 + 16)
                low_rank(1, "gate", gate2[:], lora_g[:, tok])
                yield
                af.need(pe, "v", u)
                df.need(pe, "rk", u)
                low_rank(0, "bonus", block_ones[:], rk[:])
                yield

            def back(p, h, fill):
                u = p * 2 + h
                ab.need(pe, f"s{NC - 1}", u, 1)
                db.need(pe, f"s{NC - 1}", u, 1)
                for n, (src, name, ready) in enumerate(((k_bar[h], "k_tok", "k_bar"), (b_bar[h], "b_tok", "b_bar"))):
                    df.need(pe, ready, u)
                    for c in range(NC):
                        s = slice(c * P, (c + 1) * P)
                        mm = pe.transpose(bank[4 + n][:, s], src[:, s], ident[:])
                    pb.done(mm, name)
                df.need(pe, "r_up", u)
                for j in range(2 * NC):
                    c, hd = j // 2, j % 2
                    rows = slice(hd * HEAD, (hd + 1) * HEAD)
                    b = bank[(2, 6, 3)[j % 3]]
                    if j >= 3:
                        db.need(pe, f"scores{j - 3}", u)
                    rhs = ar[h][rows, c, :, :].rearrange("p k t -> p (k t)")
                    pe.matmul(b[:, 0:2 * P], b_bar[h][rows, c * P:(c + 1) * P], rhs, start=True, stop=True)
                    mm = pe.matmul(b[:, 2 * P:4 * P], k_bar[h][rows, c * P:(c + 1) * P], rhs, start=True, stop=True)
                    pb.done(mm, f"scores{j}")
                df.need(pe, "v", u)
                ab.need(pe, "y", u, 1)
                for c in range(NC):
                    s = slice(c * P, (c + 1) * P)
                    mm = pe.transpose(bank[7][:, s], v[h][:, s], ident[:])
                pb.done(mm, "v_tok")
                _advance(fill, 2)
                ab.need(pe, "b_tok", u)
                for b in ab2:
                    db.need(pe, f"invT0.{b}", u)
                    for i in range(4):
                        mm = pe.matmul(bank[4 + b][:, i * P:(i + 1) * P], invT[b][:, i, :], ident_r[:], start=True, stop=True)
                    pb.done(mm, f"inv0.{b}")
                ab.need(pe, "v_tok", u)
                for l in levels:
                    for b in ab2:
                        db.need(pe, f"inv{l - 1}.{b}", u)
                        if l == 1:
                            ab.need(pe, f"a_hi{b}", u)
                        for i in range(4):
                            mm = pe.matmul(bank[2 + b][:, i * P:(i + 1) * P], a_hi[b][:, i, :], inv[b][:, i, :], start=True, stop=True)
                        pb.done(mm, f"prod{l}.{b}")
                    _advance(fill, 2 if l <= 3 else 1)
                    for b in ab2:
                        db.need(pe, f"prod{l}.{b}", u)
                        if l > 1:
                            ab.need(pe, f"invT{l - 1}.{b}", u)
                        low, high = bank[4 + 2 * b], bank[5 + 2 * b]
                        pe.matmul(low[:], ident_r[:], invT[b][:].rearrange("p i t -> p (i t)"), start=True, stop=False, skip_group_check=True)
                        for i in range(4):
                            s = slice(i * P, (i + 1) * P)
                            pe.matmul(low[:, s], prod[b][:, i, :], invT[b][:, i, :], start=False, stop=True, skip_group_check=True)
                            mm = pe.matmul(high[:, s], invT[b][:, i, :], prod[b][:, i, :], start=True, stop=True, skip_group_check=True)
                        pb.done(mm, f"inv{l}.{b}")
                    _advance(fill, 1)
                for b in ab2:
                    db.need(pe, f"inv{LEVELS}.{b}", u)
                    gb.need(pe, f"a_lo{b}", u)
                    pe.matmul(bank[2 + b][:], minus_r[:], inv[b][:].rearrange("p i t -> p (i t)"), start=True, stop=False, skip_group_check=True)
                    for i in range(4):
                        s = slice(i * P, (i + 1) * P)
                        for q, (x, m) in enumerate(((ident_r[:], ident_r[:]), (a_hi[b][:, i, :], inv[b][:, i, :]), (a_lo[b][:, i, :], inv[b][:, i, :]))):
                            mm = pe.matmul(bank[2 + b][:, s], x, m, start=False, stop=q == 2, skip_group_check=True)
                    pb.done(mm, f"res{b}")
                _advance(fill, 1)
                for b in ab2:
                    ab.need(pe, f"res{b}", u)
                    pe.matmul(bank[4 + 2 * b][:], ident_r[:], invT[b][:].rearrange("p i t -> p (i t)"), start=True, stop=False, skip_group_check=True)
                    for i in range(4):
                        mm = pe.matmul(bank[4 + 2 * b][:, i * P:(i + 1) * P], prod[b][:, i, :], invT[b][:, i, :], start=False, stop=True, skip_group_check=True)
                    pb.done(mm, f"inverse{b}")
                _advance(fill, 1)
                db.need(pe, "inverse1", u)
                for c in range(NC):
                    s = slice(c * P, (c + 1) * P)
                    now = state[c % 2]
                    new = bank[(6, 3)[c % 2]]
                    for hd in range(2):
                        hs = slice(hd * HEAD, (hd + 1) * HEAD)
                        pe.matmul(bank[4][:, hs], scores[:, 2 * c + hd, 2, :], v_tok[:, c * P + hd * HEAD:c * P + (hd + 1) * HEAD],
                                  start=hd == 0, stop=False, skip_group_check=True)
                    pe.matmul(new[:, 0:P], k_tok[:, s], v_tok[:, s], start=True, stop=False)
                    _advance(fill, 1)
                    if c:
                        ab.need(pe, f"s{c - 1}", u)
                        db.need(pe, f"s{c - 1}", u)
                    else:
                        db.need(pe, "start1", u)
                    pb.done(pe.matmul(bank[4][:, 0:P], ar[h][:, c, 0, :], now[:], start=False, stop=True, skip_group_check=True), f"z{c}")
                    pe.matmul(new[:, 0:P], ident[:], now[:], start=False, stop=False)
                    pe.matmul(bank[7][:, s], now[:], ar[h][:, c, 1, :], start=True, stop=False, skip_group_check=True)
                    _advance(fill, 1)
                    ab.need(pe, f"z{c}", u)
                    for hd in range(2):
                        hs = slice(hd * HEAD, (hd + 1) * HEAD)
                        mm = pe.matmul(bank[5][:, hs], inverseT[c // 2][:, 2 * (c % 2) + hd, :], z[:, hs], start=True, stop=True)
                    pb.done(mm, f"u{c}")
                    for hd in range(2):
                        hs = slice(hd * HEAD, (hd + 1) * HEAD)
                        pe.matmul(bank[7][hs, s], v_tok[:, c * P + hd * HEAD:c * P + (hd + 1) * HEAD], scores[:, 2 * c + hd, 3, :],
                                  start=False, stop=False, skip_group_check=True)
                    _advance(fill, 1 if c < 3 else 0)
                    db.need(pe, f"u{c}", u)
                    pb.done(pe.matmul(new[:, 0:P], b_tok[:, s], uu[:], start=False, stop=True), f"s{c}")
                    for hd in range(2):
                        hs = slice(hd * HEAD, (hd + 1) * HEAD)
                        mm = pe.matmul(bank[7][hs, s], uu[:, hs], scores[:, 2 * c + hd, 1, :], start=False, stop=True, skip_group_check=True)
                    pb.done(mm, f"y{c}")
                _advance(fill, 100)

            walk(pe, front, back)

        @block.gpsimd
        def _(pool):
            gf.start(pool)
            gb.start(pool)

            def front(p, h, norm_, next_=True):
                u = p * 2 + h
                if not next_:
                    return
                df.need(pool, "bonus", u, 1)
                for n, name in enumerate(PROJ):
                    af.need(pool, name, u)
                    gf.done(nc.gpsimd.tensor_tensor(diff[n][:], raw[n][:, h * HALF:(h + 1) * HALF],
                                                    raw[n][:, 1 + h * HALF:1 + (h + 1) * HALF], ALU.subtract), f"{name}_diff")
                    yield

            def back(p, h, fill):
                u = p * 2 + h
                pb.need(pool, "res1", u, 1)
                for b in ab2:
                    ab.need(pool, f"a_hi{b}", u)
                    db.need(pool, f"scores{4 * b + 3}", u)
                    gb.done(nc.gpsimd.tensor_tensor(a_lo[b][:], scores[:, 4 * b:4 * b + 4, 0, :], a_hi[b][:].bitcast(F32), ALU.subtract), f"a_lo{b}")
                _advance(fill, 100)

            walk(pool, front, back)

        @block.scalar
        def _(act):
            af.start(act)
            ab.start(act)
            an.start(act)
            A = nc.scalar.activation

            def front(p, h, norm_, next_=True):
                u = p * 2 + h
                sm = small[h]

                def var_log():
                    an.need(act, "var", u - 2)
                    an.done(A(ysq[:], ysq[:], ACT.Ln, bias=eps[:, 0:1]), "var_log")

                def rstd():
                    an.need(act, "var_log", u - 2)
                    an.done(A(ysq[:], ysq[:], ACT.Exp, scale=-0.5), "rstd")

                def square():
                    dn.need(act, "centred", u - 2)
                    dn.need(act, "n", u - 2, 1)
                    an.done(A(ysq[:], y[h][:], ACT.Square, scale=0.125), "y_sq")

                def variance():
                    pn.need(act, "var", u - 2)
                    an.done(A(ysq[:], bank[1][:], ACT.Copy), "var")
                if not next_:
                    square()
                    yield from (None,) * 4
                    variance()
                    var_log()
                    rstd()
                    return
                df.need(act, "bonus", u, 1)
                df.need(act, "half_par", u)
                pf.need(act, "w", u)
                af.done(A(log_w[:], bank[1][:], ACT.Tanh, scale=0.5, bias=half_par[:, 0:1]), "w")
                yield
                pf.need(act, "a", u)
                af.done(A(a[:], bank[1][:], ACT.Tanh, scale=0.5, bias=half_par[:, 1:2]), "a")
                yield
                if norm_:
                    square()
                yield

                def evac(name):
                    pf.need(act, name, u)
                    af.done(A(raw[PROJ.index(name)][:, 1 + h * HALF:1 + (h + 1) * HALF], bank[0][:], ACT.Copy), name)
                df.need(act, "from_mid", u)
                af.done(A(up[:], from_mid[:], ACT.Exp), "up")
                yield
                af.done(A(down[:], from_mid[:], ACT.Exp, scale=-1.0), "down")
                yield
                evac("k")
                yield
                df.need(act, "from_prev", u)
                af.done(A(prev[:], cum[:], ACT.Exp), "prev")
                yield
                if norm_:
                    variance()
                yield
                df.need(act, "k_mod", u)
                af.done(A(sq[:], kk[:], ACT.Square), "kk_sq")
                yield
                ab.need(act, f"s{NC - 1}", u, 2)
                af.done(A(sm[:, 2 * NC:3 * NC], sm[:, 0:NC], ACT.Exp), "mid")
                af.done(A(sm[:, 3 * NC:4 * NC], sm[:, NC:2 * NC], ACT.Exp), "decay")
                yield
                df.need(act, "norm_floor", u)
                af.done(A(norm[:], norm[:], ACT.Ln), "norm_log")
                if norm_:
                    var_log()
                yield
                af.need(act, "norm_log", u)
                af.done(A(norm[:], norm[:], ACT.Exp, scale=-0.5), "norm_inv")
                if norm_:
                    rstd()
                yield
                evac("r")
                yield
                evac("v")
                yield
                pf.need(act, "gate", u)
                dn.need(act, "out", u, 2)
                af.done(A(gate[h][:], bank[1][:], ACT.Copy), "gate")
                yield

            def back(p, h, fill):
                u = p * 2 + h
                for n, (out, name) in enumerate(((k_tok, "k_tok"), (b_tok, "b_tok"), (v_tok, "v_tok"))):
                    pb.need(act, name, u)
                    ab.done(A(out[:], bank[(4, 5, 7)[n]][:], ACT.Copy), name)
                gb.need(act, "a_lo1", u, 1)
                for b in ab2:
                    db.need(act, f"scores{4 * b + 3}", u)
                    ab.done(A(a_hi[b][:], scores[:, 4 * b:4 * b + 4, 0, :], ACT.Copy), f"a_hi{b}")
                _advance(fill, 1)
                for l in levels:
                    for b in ab2:
                        pb.need(act, f"inv{l}.{b}", u)
                        ab.done(A(invT[b][:].rearrange("p i t -> p (i t)"), bank[4 + 2 * b][:], ACT.Copy), f"invT{l}.{b}")
                    _advance(fill, (1, 1, 2, 2, 2, 2)[l - 1])
                for b in ab2:
                    pb.need(act, f"res{b}", u)
                    ab.done(A(prod[b][:].rearrange("p i t -> p (i t)"), bank[2 + b][:], ACT.Copy), f"res{b}")
                _advance(fill, 1)
                af.need(act, "decay", u)
                for c in range(NC):
                    pb.need(act, f"z{c}", u)
                    ab.done(A(z[:], bank[4][:, 0:P], ACT.Copy), f"z{c}")
                    _advance(fill, (1, 0, 0, 0)[c])
                    pb.need(act, f"s{c}", u)
                    ab.done(A(state[(c + 1) % 2][0:HEAD, 0:HEAD], bank[(6, 3)[c % 2]][0:HEAD, 0:HEAD], ACT.Copy,
                              scale=small[h][0:HEAD, 3 * NC + c:3 * NC + c + 1]), f"s{c}")
                pb.need(act, end, u)
                dn.need(act, "plus", u, 2)
                ab.done(A(y[h][:], bank[7][:], ACT.Copy), "y")
                _advance(fill, 100)

            walk(act, front, back)

        @block.vector
        def _(dve):
            V = nc.vector
            for x in stored:
                dve.sem_inc(x, 16)
            V.memset(eps[:], GN_EPS).then_inc(zeroed, 1)
            V.tensor_scalar(ident_r[:], ident[:], 1.0, None, ALU.mult).then_inc(zeroed, 1)
            V.tensor_scalar(minus_r[:], ident[:], -1.0, None, ALU.mult).then_inc(zeroed, 1)
            for x in raw:
                V.memset(x[:, 0:1], 0.0).then_inc(zeroed, 1)
            for x in state:
                V.memset(x[:], 0.0).then_inc(zeroed, 1)
            V.memset(scores[:], 0.0).then_inc(zeroed, 1)
            dve.wait_ge(zeroed, 9)
            dve.wait_ge(par_in, 16)
            df.start(dve)
            db.start(dve)
            dn.start(dve)
            ch = lambda x: x.rearrange("p (c t) -> p c t", c=NC)

            def front(p, h, norm_, next_=True):
                u = p * 2 + h
                par = lambda i: par_now[h][:, i:i + 1]

                def centre():
                    pn.need(dve, "mean", u - 2)
                    dn.done(V.scalar_tensor_tensor(y[h][:], bank[0][:], -1.0 / HEAD, y[h][:], ALU.mult, ALU.add), "centred")

                def norm_ends():
                    an.need(dve, "rstd", u - 2)
                    dn.done(V.tensor_tensor(y[h][:], y[h][:], ysq[:], ALU.mult), "n")
                    dn.need(dve, "n", u - 2)
                    dn.done(V.tensor_scalar(y[h][:], y[h][:], ln[h][:, 0:1], ln[h][:, 1:2], ALU.mult, ALU.add), "affine")
                    dn.need(dve, "affine", u - 2)
                    dn.done(V.tensor_tensor(y[h][:], y[h][:], bonus[h][:], ALU.add), "plus")
                    dn.need(dve, "plus", u - 2)
                    dve.wait_ge(stored[h], p * 16)
                    dn.done(V.tensor_tensor(y_out[h][:], y[h][:], gate[h][:], ALU.mult), "out")
                if not next_:
                    centre()
                    yield from (None,) * 8
                    norm_ends()
                    return
                pb.need(dve, end, u, 2)
                ab.need(dve, f"s{NC - 1}", u, 2)
                df.done(V.tensor_scalar(par_now[h][:], par_all[:, bass.ds(p, 1), :].rearrange("p o n -> p (o n)"), 1.0, None, ALU.mult), "par")
                af.need(dve, "a", u, 1)
                df.need(dve, "par", u)
                df.done(V.tensor_scalar(half_par[:], par_now[h][:, W0:A0 + 1], 0.5, None, ALU.mult), "half_par")
                yield
                if norm_:
                    centre()
                yield
                af.need(dve, "w", u)
                df.done(V.tensor_scalar(log_w[:], log_w[:], -0.5 * DECAY, -0.5 * DECAY, ALU.mult, ALU.add), "log_w")
                yield
                df.need(dve, "log_w", u)
                df.done(V.tensor_tensor_scan(cum[:], cst["restart"][:], log_w[:], 0.0, ALU.mult, ALU.add), "cum")
                yield
                pf.need(dve, "bonus", u, 1)
                _chunk_small(nc, dve, df, u, cum, from_mid, small[h])
                yield
                df.need(dve, "from_mid", u)
                df.done(V.tensor_tensor(cum[:], from_mid[:], log_w[:], ALU.subtract), "from_prev")
                yield
                af.need(dve, "a", u)
                df.done(V.tensor_scalar(a[:], a[:], 0.5, 0.5, ALU.mult, ALU.add), "a")
                df.need(dve, "a", u)
                df.done(V.tensor_scalar(gain[:], a[:], 1.0, par(K_A), ALU.subtract, ALU.mult), "k_gain")
                yield

                def shift(n, name, out):
                    gf.need(dve, f"{name}_diff", u)
                    df.done(V.scalar_tensor_tensor(out[:], diff[n][:], par((MU_K, MU_R, MU_V)[n]), raw[n][:, 1 + h * HALF:1 + (h + 1) * HALF],
                                                   ALU.mult, ALU.add), name)
                shift(0, "k", k)
                df.need(dve, "k", u)
                df.done(V.tensor_scalar(kk[:], k[:], par(K_K), None, ALU.mult), "kk")
                yield
                df.done(V.scalar_tensor_tensor(k[:], gain[:], 1.0, k[:], ALU.add, ALU.mult), "k_mod")
                yield
                af.need(dve, "down", u)
                df.need(dve, "k_mod", u)
                df.done(V.tensor_tensor(k_bar[h][:], k[:], down[:], ALU.mult), "k_bar")
                yield
                pf.need(dve, "norm", u)
                df.done(V.tensor_scalar(norm[:], bank[1][:], 1e-24, None, ALU.max), "norm_floor")
                yield
                af.need(dve, "norm_inv", u)
                df.done(V.tensor_tensor(kk[:], kk[:], norm[:], ALU.mult), "kk_unit")
                yield
                df.need(dve, "kk_unit", u)
                df.done(V.tensor_tensor(a[:], kk[:], a[:], ALU.mult), "b")
                df.need(dve, "b", u)
                df.done(V.tensor_tensor(b_bar[h][:], a[:], down[:], ALU.mult), "b_bar")
                yield
                if norm_:
                    norm_ends()
                yield
                af.need(dve, "prev", u)
                df.done(V.scalar_tensor_tensor(ar[h][:, :, 0, :], ch(kk[:]), -1.0, ch(prev[:]), ALU.mult, ALU.mult), "a_prev")
                yield
                shift(1, "r", r)
                yield
                df.need(dve, "r", u)
                af.need(dve, "up", u)
                df.done(V.tensor_tensor(ar[h][:, :, 1, :], ch(r[:]), ch(up[:]), ALU.mult), "r_up")
                yield
                df.done(V.scalar_tensor_tensor(rk[:], r[:], par(R_K), k[:], ALU.mult, ALU.mult), "rk")
                yield
                shift(2, "v", v[h])
                yield
                df.need(dve, "v", u)
                pf.need(dve, "bonus", u)
                df.done(V.tensor_tensor(bonus[h][:], bank[0][:], v[h][:], ALU.mult), "bonus")
                df.done(V.tensor_scalar(ln[h][:], par_now[h][:, LN_W:LN_B + 1], 1.0, None, ALU.mult), "ln")
                yield

            def back(p, h, fill):
                u = p * 2 + h
                level = lambda l: _over(cst["level_mask"][:, l, :], 4)
                tiled = lambda x: x.rearrange("p (i t) -> p i t", i=4)
                gb.need(dve, "a_lo1", u, 1)
                for j in range(2 * NC):
                    pb.need(dve, f"scores{j}", u)
                    V.memset(touch[:, j:j + 1], 0.0)
                    db.done(V.copy_predicated(scores[:, j].rearrange("p k t -> p (k t)"), cst["score_mask"][:],
                                              bank[(2, 6, 3)[j % 3]][:]), f"scores{j}")
                for b in ab2:
                    db.need(dve, f"scores{4 * b + 3}", u)
                    db.done(V.tensor_tensor(invT[b][:], scores[:, 4 * b:4 * b + 4, 0, :], level(0), ALU.mult), f"invT_mask{b}")
                    db.need(dve, f"invT_mask{b}", u)
                    db.done(V.tensor_tensor(invT[b][:], invT[b][:].bitcast(F32), _over(ident[:], 4), ALU.add), f"invT0.{b}")
                for b in ab2:
                    pb.need(dve, f"inv0.{b}", u)
                    db.done(V.tensor_copy(inv[b][:].rearrange("p i t -> p (i t)"), bank[4 + b][:]), f"inv0.{b}")
                _advance(fill, 2)
                for l in levels:
                    for b in ab2:
                        pb.need(dve, f"prod{l}.{b}", u)
                        db.done(V.tensor_tensor(prod[b][:], tiled(bank[2 + b][:]), level(l), ALU.mult), f"prod{l}.{b}")
                    _advance(fill, (1, 1, 1, 0, 1, 1)[l - 1])
                    for b in ab2:
                        pb.need(dve, f"inv{l}.{b}", u)
                        db.done(V.tensor_tensor(inv[b][:], tiled(bank[5 + 2 * b][:]), inv[b][:].bitcast(F32), ALU.add), f"inv{l}.{b}")
                    _advance(fill, (1, 1, 0, 0, 1, 1)[l - 1])
                for b in ab2:
                    pb.need(dve, f"inverse{b}", u)
                    db.done(V.tensor_copy(inverseT[b][:].rearrange("p i t -> p (i t)"), bank[4 + 2 * b][:]), f"inverse{b}")
                for hd in range(2):
                    hs = slice(hd * HEAD, (hd + 1) * HEAD)
                    if h == 0:
                        db.done(V.memset(state[0][hs, hs], 0.0), f"start{hd}")
                    else:
                        af.need(dve, "mid", u)
                        db.done(V.tensor_scalar(state[0][hs, hs], state[0][hs, hs], small[h][hs, 2 * NC:2 * NC + 1], None, ALU.mult), f"start{hd}")
                low = slice(HEAD, P)
                for c in range(NC):
                    pb.need(dve, f"u{c}", u)
                    db.done(V.tensor_copy(uu[:], bank[5][:, 0:P]), f"u{c}")
                    pb.need(dve, f"s{c}", u)
                    if c == 0:
                        af.need(dve, "decay", u)
                    db.done(V.tensor_scalar(state[(c + 1) % 2][low, low], bank[(6, 3)[c % 2]][low, low],
                                            small[h][low, 3 * NC + c:3 * NC + c + 1], None, ALU.mult), f"s{c}")
                    _advance(fill, (2, 2, 2, 1)[c])
                _advance(fill, 100)

            walk(dve, front, back)


def _merge(nc, sems, d, hT, glaT, mixT, w_out, w_out_in):
    with ExitStack() as ctx:
        sb = lambda n, s: ctx.enter_context(nc.sbuf_tensor(n, s, F32))
        w = [sb(f"m_w{i}", [P, KT, 4 * P]) for i in range(2)]
        rwkvT = sb("m_rwkvT", [P, KT, SEQ])
        y_in = [sems.enter_context(nc.semaphore(f"m_y_in{i}")) for i in range(2)]
        gate = [[sb(f"m_g{i}{x}", [P, HALF]) for x in range(2)] for i in range(2)]
        bank = [ctx.enter_context(nc.psum_tensor(f"m_ps{i}", [P, HALF], F32)) for i in range(8)]
        w_in = [sems.enter_context(nc.semaphore(f"m_w_in{i}")) for i in range(2)]
        unit = [(i, h) for i in range(2) for h in range(2)]
        order = [(i, h, q) for i in range(2) for qs in ((0, 1), (2, 3)) for h in range(2) for q in qs]
        src_names = ("ga", "gb", "gla", "rwkv")
        pe_s = Steps(nc, sems, "m_pe", [f"{src_names[q]}{i}{h}" for i, h, q in order])
        act_s = Steps(nc, sems, "m_act", [f"{x}{i}{h}" for i, h in unit for x in ("ga", "gb")])
        dve_s = Steps(nc, sems, "m_dve", [f"{x}{i}{h}" for i, h in unit for x in ("sa", "sb", "ma", "mb", "mix")])
        block = ctx.enter_context(nc.Block())
        srcs = (("ga", hT), ("gb", hT), ("gla", glaT), ("rwkv", rwkvT))

        @block.sync
        def _(sp):
            def weights(n, i):
                pe_s.need_before(sp, f"rwkv{i}1", n)
                sp.dma_start(w[i][:], d["w_merge"][bass.ds(n * 2 + i, 1)].rearrange("o p k n -> p (o k) n")).then_inc(w_in[i], 16)
            weights(0, 0)
            sp.dma_start(glaT[:], d["y_gla"].rearrange("g x p t -> p (g x) t")).then_inc(y_in[0], 16)
            sp.dma_start(rwkvT[:], d["y_rwkv"].rearrange("k p t -> p k t")).then_inc(y_in[1], 16)
            weights(0, 1)
            with sp.Fori(1, 4) as n:
                for i in range(2):
                    weights(n, i)
            sp.dma_start(w_out[:], d["w_out"]).then_inc(w_out_in, 16)

        @block.tensor
        def _(pe):
            pe_s.start(pe)

            def group(n, first):
                for i, h, q in order:
                    if q == 0 and h == 0:
                        pe.wait_ge(w_in[i], n * 16 + 16)
                    if q == 0:
                        (dve_s.need_before if i == 0 else dve_s.need)(pe, f"mb{1 - i}{h}", n)
                    if first and i == 0 and h == 0 and q >= 2:
                        pe.wait_ge(y_in[q - 2], 16)
                    name, src = srcs[q]
                    for k in range(KT):
                        mm = pe.matmul(bank[4 * h + q][:], w[i][:, k, q * P:(q + 1) * P], src[:, k, h * HALF:(h + 1) * HALF],
                                       start=k == 0, stop=k == KT - 1)
                    pe_s.done(mm, f"{name}{i}{h}")
            group(0, True)
            with pe.Fori(1, 4) as n:
                group(n, False)

        @block.scalar
        def _(act):
            act_s.start(act)
            with act.Fori(0, 4) as n:
                for i, h in unit:
                    (dve_s.need_before if i == 0 else dve_s.need)(act, f"mix{1 - i}{h}", n)
                    for x, name in enumerate(("ga", "gb")):
                        pe_s.need(act, f"{name}{i}{h}", n)
                        act_s.done(nc.scalar.activation(gate[h][x][:], bank[4 * h + x][:], ACT.Tanh, scale=0.5), f"{name}{i}{h}")

        @block.vector
        def _(dve):
            dve_s.start(dve)
            with dve.Fori(0, 4) as n:
                for i, h in unit:
                    for x, (s, g) in enumerate((("sa", "ga"), ("sb", "gb"))):
                        act_s.need(dve, f"{g}{i}{h}", n)
                        dve_s.done(nc.vector.tensor_scalar(gate[h][x][:], gate[h][x][:], 0.5, 0.5, ALU.mult, ALU.add), f"{s}{i}{h}")
                    for x, (m, s, y) in enumerate((("ma", "sa", "gla"), ("mb", "sb", "rwkv"))):
                        dve_s.need(dve, f"{s}{i}{h}", n)
                        pe_s.need(dve, f"{y}{i}{h}", n)
                        dve_s.done(nc.vector.tensor_tensor(gate[h][x][:], bank[4 * h + 2 + x][:], gate[h][x][:], ALU.mult), f"{m}{i}{h}")
                    dve_s.need(dve, f"mb{i}{h}", n)
                    dve_s.done(nc.vector.tensor_tensor(mixT[:, bass.ds(n * 2 + i, 1), h * HALF:(h + 1) * HALF].rearrange("p o t -> p (o t)"),
                                                       gate[h][0][:], gate[h][1][:], ALU.add), f"mix{i}{h}")
            dve_s.need(dve, "mix11", 3)


def _residual(nc, sems, d, mixT, w, w_in, x1, h2T_hi, h2T_lo, cst):
    ident = cst["ident"]
    with ExitStack() as ctx:
        sb = lambda n, s: ctx.enter_context(nc.sbuf_tensor(n, s, F32))
        h2 = sb("o_h2", [P, KT, D])
        ss, rs = sb("o_ss", [P, 8]), sb("o_rs", [P, 8])
        bank = [ctx.enter_context(nc.psum_tensor(f"o_ps{i}", [P, HALF], F32)) for i in range(8)]
        sem = lambda n: sems.enter_context(nc.semaphore(n))
        product, added, squares, mean_eps, root, rstd, scaled, turned, evacuated, high = map(
            sem, ("o_product", "o_added", "o_squares", "o_mean", "o_root", "o_rstd", "o_scaled", "o_turned", "o_evac", "o_high"))
        x_in = [sem(f"o_x_in{t}") for t in range(KT)]
        block = ctx.enter_context(nc.Block())

        @block.sync
        def _(sp):
            for t in range(KT):
                sp.dma_start(x1[:, t, :], d["x"][t * P:(t + 1) * P, :]).then_inc(x_in[t], 16)

        @block.tensor
        def _(pe):
            pe.wait_ge(w_in, 16)
            for t in range(KT):
                for e in range(2):
                    n = 2 * t + e
                    if n >= 8:
                        pe.wait_ge(added, n - 7)
                    for k in range(KT):
                        mm = pe.matmul(bank[n % 8][:], mixT[:, k, t * P:(t + 1) * P], w[:, k, e * HALF:(e + 1) * HALF],
                                       start=k == 0, stop=k == KT - 1)
                    mm.then_inc(product, 1)
            pe.wait_ge(added, 16)
            pe.wait_ge(scaled, KT)
            for h in range(2):
                for k in range(KT):
                    n = h * KT + k
                    if n >= 8:
                        pe.wait_ge(evacuated, n - 7)
                    for j in range(4):
                        mm = pe.transpose(bank[n % 8][:, j * P:(j + 1) * P], h2[:, 4 * h + j, k * P:(k + 1) * P], ident[:])
                    mm.then_inc(turned, 1)

        @block.vector
        def _(dve):
            for t in range(KT):
                dve.wait_ge(x_in[t], 16)
                for e in range(2):
                    n = 2 * t + e
                    dve.wait_ge(product, n + 1)
                    s = slice(e * HALF, (e + 1) * HALF)
                    nc.vector.tensor_tensor(x1[:, t, s], bank[n % 8][:], x1[:, t, s], ALU.add).then_inc(added, 1)
            dve.wait_ge(squares, KT)
            nc.vector.tensor_scalar(ss[:], ss[:], 1.0 / D, NORM_EPS, ALU.mult, ALU.add).then_inc(mean_eps, 1)
            dve.wait_ge(root, 1)
            nc.vector.reciprocal(rs[:], rs[:]).then_inc(rstd, 1)
            dve.wait_ge(rstd, 1)
            for t in range(KT):
                nc.vector.tensor_scalar(h2[:, t, :], x1[:, t, :], rs[:, t:t + 1], None, ALU.mult).then_inc(scaled, 1)
            for n in range(2 * KT):
                h, k = n // KT, n % KT
                dve.wait_ge(high, n + 1)
                s = slice(h * HALF, (h + 1) * HALF)
                nc.vector.scalar_tensor_tensor(h2T_lo[:, k, s], bank[n % 8][:], cst["norms"][:, 8 + k:9 + k],
                                               h2T_hi[:, k, s].bitcast(F32), ALU.mult, ALU.subtract).then_inc(evacuated, 1)
            dve.wait_ge(evacuated, 2 * KT)

        @block.scalar
        def _(act):
            for t in range(KT):
                act.wait_ge(added, 2 * t + 2)
                nc.scalar.activation(h2[:, t, :], x1[:, t, :], ACT.Square, accum_out=ss[:, t:t + 1]).then_inc(squares, 1)
            act.wait_ge(mean_eps, 1)
            nc.scalar.activation(rs[:], ss[:], ACT.Sqrt).then_inc(root, 1)
            for n in range(2 * KT):
                h, k = n // KT, n % KT
                act.wait_ge(turned, n + 1)
                nc.scalar.activation(h2T_hi[:, k, h * HALF:(h + 1) * HALF], bank[n % 8][:], ACT.Copy,
                                     scale=cst["norms"][:, 8 + k:9 + k]).then_inc(high, 1)


def _mlp(nc, sems, d, h2T_hi, h2T_lo, x1):
    with ExitStack() as ctx:
        sb = lambda n, s, dt=F32: ctx.enter_context(nc.sbuf_tensor(n, s, dt))
        raw = [sb(f"f_raw{i}", [P, D]) for i in range(4)]
        up_hi, up_lo = ([sb(f"f_up_{x}{i}", [P, D], F32R) for i in range(2)] for x in ("hi", "lo"))
        down_hi, down_lo = (sb(f"f_down_{x}", [P, FF_TILES, D], F32R) for x in ("hi", "lo"))
        hid_hi, hid_lo = (sb(f"f_hid_{x}", [P, FF_TILES, SEQ], F32R) for x in ("hi", "lo"))
        relu = [sb(f"f_relu{i}", [P, HALF]) for i in range(2)]
        bank = [ctx.enter_context(nc.psum_tensor(f"f_ps{i}", [P, HALF], F32)) for i in range(8)]
        raw_in = [sems.enter_context(nc.semaphore(f"f_raw_in{i}")) for i in range(4)]
        NU, ND, last = 2 * FF_TILES, 2 * KT, FF_GROUPS - 1
        after = [([f"u{t + 2}"] if t < 2 else []) + [f"d{t}"] for t in range(FF_TILES)]
        slot = {"u2": (0, 0), "d0": (1, 0), "u3": (2, 1), "d1": (3, 1), "d2": (0, 1), "d3": (1, 1), "u0": (2, 0), "u1": (3, 0)}
        steps = lambda *x: [n for t in range(FF_TILES) for n in [f"{y}{2 * t + h}" for h in range(2) for y in x] + after[t]]
        pe_s = Steps(nc, sems, "f_pe", [f"up{n}" for n in range(NU)] + [f"down{n}" for n in range(ND)])
        act_s = Steps(nc, sems, "f_act", steps("relu", "hid"))
        dve_s = Steps(nc, sems, "f_dve", steps("sq", "hid") + [f"add{n}" for n in range(ND)])
        act_n = Steps(nc, sems, "f_act_next", ["u0", "u1"])
        dve_n = Steps(nc, sems, "f_dve_next", ["u0", "u1"])
        block = ctx.enter_context(nc.Block())

        def parts(name):
            i = int(name[1])
            return (up_hi[i % 2][:], up_lo[i % 2][:]) if name[0] == "u" else (down_hi[:, i, :], down_lo[:, i, :])

        def act_split(act, s, name, g):
            b, before = slot[name]
            act.wait_ge(raw_in[b], g * 32 + 16 * (before + 1))
            s.done(nc.scalar.activation(parts(name)[0], raw[b][:], ACT.Copy), name)

        def dve_split(dve, s, other, name, g):
            hi, lo = parts(name)
            other.need(dve, name, g)
            s.done(nc.vector.tensor_tensor(lo, raw[slot[name][0]][:], hi.bitcast(F32), ALU.subtract), name)

        @block.sync
        def _(sp):
            def load(name, g):
                i = int(name[1])
                src = d["w_up"][bass.ds(g * FF_TILES + i, 1)].rearrange("o p k n -> p (o k n)") if name[0] == "u" \
                    else d["w_down"][bass.ds(g * FF_TILES + i, 1)].rearrange("o p n -> p (o n)")
                b = slot[name][0]
                sp.dma_start(raw[b][:], src).then_inc(raw_in[b], 16)

            def group(g, next_):
                dve_s.need_before(sp, "d2", g)
                load("u2", g)
                dve_s.need_before(sp, "d3", g)
                load("d0", g)
                dve_n.need(sp, "u0", g)
                load("u3", g)
                dve_n.need(sp, "u1", g)
                load("d1", g)
                dve_s.need(sp, "u2", g)
                load("d2", g)
                dve_s.need(sp, "d0", g)
                load("d3", g)
                if next_:
                    dve_s.need(sp, "u3", g)
                    load("u0", g + 1)
                    dve_s.need(sp, "d1", g)
                    load("u1", g + 1)
            load("u0", 0)
            load("u1", 0)
            with sp.Fori(0, last) as g:
                group(g, True)
            group(last, False)

        @block.tensor
        def _(pe):
            pe_s.start(pe)
            with pe.Fori(0, FF_GROUPS) as g:
                for n in range(NU):
                    t, h = n // 2, n % 2
                    tok = slice(h * HALF, (h + 1) * HALF)
                    if h == 0:
                        (dve_n if t < 2 else dve_s).need(pe, f"u{t}", g)
                    dve_s.need_before(pe, f"add{ND - 8 + n}", g)
                    for k in range(KT):
                        cols = slice(k * P, (k + 1) * P)
                        hi, lo = up_hi[t % 2][:, cols], up_lo[t % 2][:, cols]
                        mm = _product(pe, bank[n][:], hi, lo, h2T_hi[:, k, tok], h2T_lo[:, k, tok], k == 0, k == KT - 1)
                    pe_s.done(mm, f"up{n}")
                dve_s.need(pe, f"d{FF_TILES - 2}", g)
                for n in range(ND):
                    t, e = n // 2, n % 2
                    if n < 8:
                        act_s.need(pe, f"relu{n}", g)
                    else:
                        dve_s.need(pe, f"add{n - 8}", g)
                    for k in range(FF_TILES):
                        if n == 0 and k == FF_TILES - 1:
                            dve_s.need(pe, f"d{k}", g)
                        hi, lo = hid_hi[:, k, t * P:(t + 1) * P], hid_lo[:, k, t * P:(t + 1) * P]
                        w = slice(e * HALF, (e + 1) * HALF)
                        mm = _product(pe, bank[n % 8][:], hi, lo, down_hi[:, k, w], down_lo[:, k, w], k == 0, k == FF_TILES - 1)
                    pe_s.done(mm, f"down{n}")

        @block.scalar
        def _(act):
            act_s.start(act)
            act_n.start(act)

            def first_tiles(g):
                for name in ("u0", "u1"):
                    act_split(act, act_n, name, g)

            def group(g):
                for n in range(NU):
                    t, h = n // 2, n % 2
                    pe_s.need(act, f"up{n}", g)
                    if n < 2:
                        dve_s.need_before(act, f"hid{NU - 2 + n}", g)
                    else:
                        dve_s.need(act, f"hid{n - 2}", g)
                    act_s.done(nc.scalar.activation(relu[n % 2][:], bank[n][:], ACT.Relu), f"relu{n}")
                    dve_s.need(act, f"sq{n}", g)
                    act_s.done(nc.scalar.activation(hid_hi[:, t, h * HALF:(h + 1) * HALF], relu[n % 2][:], ACT.Copy), f"hid{n}")
                    for name in after[t] if h else ():
                        act_split(act, act_s, name, g)
            first_tiles(0)
            with act.Fori(0, last) as g:
                group(g)
                first_tiles(g + 1)
            group(last)

        @block.vector
        def _(dve):
            dve_s.start(dve)
            dve_n.start(dve)
            V = nc.vector

            def first_tiles(g):
                for name in ("u0", "u1"):
                    dve_split(dve, dve_n, act_n, name, g)

            def group(g, next_):
                for n in range(NU):
                    t, h = n // 2, n % 2
                    act_s.need(dve, f"relu{n}", g)
                    dve_s.done(V.tensor_tensor(relu[n % 2][:], relu[n % 2][:], relu[n % 2][:], ALU.mult), f"sq{n}")
                    act_s.need(dve, f"hid{n}", g)
                    dve_s.done(V.tensor_tensor(hid_lo[:, t, h * HALF:(h + 1) * HALF], relu[n % 2][:],
                                               hid_hi[:, t, h * HALF:(h + 1) * HALF].bitcast(F32), ALU.subtract), f"hid{n}")
                    for name in after[t] if h else ():
                        dve_split(dve, dve_s, act_s, name, g)
                for n in range(ND):
                    t, s = n // 2, slice((n % 2) * HALF, (n % 2 + 1) * HALF)
                    pe_s.need(dve, f"down{n}", g)
                    dve_s.done(V.tensor_tensor(x1[:, t, s], bank[n % 8][:], x1[:, t, s], ALU.add), f"add{n}")
                    if n == 3 and next_:
                        first_tiles(g + 1)
            first_tiles(0)
            with dve.Fori(0, last) as g:
                group(g, True)
            group(last, False)
            dve_s.need(dve, f"add{ND - 1}", last)


def _finish(nc, sems, d, x1):
    with ExitStack() as ctx:
        sb = lambda n, s: ctx.enter_context(nc.sbuf_tensor(n, s, F32))
        gain = sb("e_gain", [P, D])
        out = sb("e_out", [P, KT, D])
        ss, rs = sb("e_ss", [P, 8]), sb("e_rs", [P, 8])
        sem = lambda n: sems.enter_context(nc.semaphore(n))
        gain_in, squares, mean_eps, root, rstd, scaled, stored = map(sem, ("e_gain_in", "e_squares", "e_mean", "e_root", "e_rstd", "e_scaled", "e_stored"))
        block = ctx.enter_context(nc.Block())

        @block.sync
        def _(sp):
            sp.dma_start(gain[:], d["norm_final"]).then_inc(gain_in, 16)
            for t in range(KT):
                sp.wait_ge(scaled, t + 1)
                sp.dma_start(d["out"][t * P:(t + 1) * P, :], out[:, t, :]).then_inc(stored, 16)
            sp.wait_ge(stored, 16 * KT)

        @block.scalar
        def _(act):
            for t in range(KT):
                nc.scalar.activation(out[:, t, :], x1[:, t, :], ACT.Square, accum_out=ss[:, t:t + 1]).then_inc(squares, 1)
            act.wait_ge(mean_eps, 1)
            nc.scalar.activation(rs[:], ss[:], ACT.Sqrt).then_inc(root, 1)

        @block.vector
        def _(dve):
            dve.wait_ge(squares, KT)
            nc.vector.tensor_scalar(ss[:], ss[:], 1.0 / D, NORM_EPS, ALU.mult, ALU.add).then_inc(mean_eps, 1)
            dve.wait_ge(root, 1)
            nc.vector.reciprocal(rs[:], rs[:]).then_inc(rstd, 1)
            dve.wait_ge(rstd, 1)
            dve.wait_ge(gain_in, 16)
            for t in range(KT):
                nc.vector.scalar_tensor_tensor(out[:, t, :], x1[:, t, :], rs[:, t:t + 1], gain[:], ALU.mult, ALU.mult).then_inc(scaled, 1)


def build(nc, d):
    with ExitStack() as outer, ExitStack() as sems:
        sb = lambda ctx, n, s, dt=F32: ctx.enter_context(nc.sbuf_tensor(n, s, dt))
        cst = {n: sb(outer, f"c_{n}", s) for n, s in (("ident", [P, P]), ("ones", [P, P]), ("norms", [P, 18]))}
        far = lambda ctx, n, dt=F32: ctx.enter_context(nc.sbuf_tensor(n, [P, KT, SEQ], dt, side="right"))
        mix_stream = ExitStack()
        with ExitStack() as mixers:
            cst.update({n: sb(mixers, f"c_{n}", s) for n, s in (("block_ones", [P, P]), ("level_mask", [P, 7, P]), ("restart", [P, HALF]))})
            cst["score_mask"] = sb(mixers, "c_score_mask", [P, 4 * P], U32)
            lora_wa, lora_g = sb(mixers, "lora_wa", [P, SEQ]), sb(mixers, "lora_g", [P, SEQ])
            with ExitStack() as low:
                hT_hi, hT_lo = (sb(low, f"hT_{x}", [P, KT, SEQ], F32R) for x in ("hi", "lo"))
                gla_al = sb(low, "gla_al", [RANK, SEQ])
                _prepare(nc, sems, d, hT_hi, hT_lo, cst)
                _low_rank(nc, sems, d, hT_hi, hT_lo, lora_wa, lora_g, gla_al, cst["norms"])
                _gla(nc, sems, d, hT_hi, hT_lo, gla_al, d["y_gla"], cst)
                hT = far(mix_stream, "hT")
                _whole(nc, sems, hT_hi, hT_lo, hT)
            _rwkv(nc, sems, d, hT, lora_wa, lora_g, d["y_rwkv"], cst)
        x1 = sb(outer, "x1", [P, KT, D])
        with ExitStack() as mlp_stream:
            with ExitStack() as ctx:
                mixT, w_out = sb(ctx, "mixT", [P, KT, SEQ]), sb(ctx, "w_out", [P, KT, D])
                w_out_in = sems.enter_context(nc.semaphore("w_out_in"))
                _merge(nc, sems, d, hT, x1, mixT, w_out, w_out_in)
                mix_stream.close()
                h2_hi, h2_lo = (far(mlp_stream, n, F32R) for n in ("h2_hi", "h2_lo"))
                _residual(nc, sems, d, mixT, w_out, w_out_in, x1, h2_hi, h2_lo, cst)
            _mlp(nc, sems, d, h2_hi, h2_lo, x1)
        _finish(nc, sems, d, x1)


def _tiles(np, w, width):
    r, c = w.shape
    return np.ascontiguousarray(w.reshape(r // P, P, c // width, width).transpose(2, 1, 0, 3))


def kernel(**inputs):
    import numpy as np
    import concourse.bacc as bacc
    from concourse.bass_utils import run_bass_kernel_spmd

    a = {k: np.asarray(v) for k, v in inputs.items()}
    w_in = a["w_in"][0]
    cols = lambda lo, n: w_in[:, lo:lo + n]
    gq, gk, gv, gog, gal = 0, 512, 1024, 2048, 3072
    rr = 3088
    rk, rv, rwl, rgl = rr + 1024, rr + 2048, rr + 3072, rr + 3200
    ga, gb = rr + 3328, rr + 4352
    group = lambda n, parts: np.concatenate([np.concatenate([cols(o + i * s, s) for o, s in parts], 1) for i in range(n)], 1)
    per_channel = lambda v: np.ascontiguousarray(v.reshape(-1, P).T)
    mu = a["rwkv_mu"][0]
    pair = np.stack([v.reshape(-1, P) for v in (mu[0:1024], mu[1024:2048], mu[2048:3072], a["rwkv_w0"][0], a["rwkv_a0"][0],
                                                a["rwkv_k_k"][0], a["rwkv_k_a"][0], a["rwkv_r_k"][0].reshape(-1),
                                                a["rwkv_ln_w"][0], a["rwkv_ln_b"][0])], -1)
    wa2 = np.concatenate([a["rwkv_w_w2"][0], a["rwkv_a_w2"][0]], 0).reshape(P, 8, P).transpose(1, 0, 2)
    g2 = a["rwkv_g_w2"][0].reshape(P, 8, P).transpose(1, 0, 2)
    i, j = np.arange(P)[:, None], np.arange(P)[None, :]
    strict, incl = (j > i), (j >= i)
    levels = [(j % 2 == 1) & (i == j - 1)] + [((i >> l) % 2 == 1) & ((j >> l) == (i >> l) - 1) for l in range(1, 7)]
    merge = np.stack([_tiles(np, m, P) for m in (cols(ga, 1024), cols(gb, 1024), a["w_branch_gla"][0], a["w_branch_rwkv"][0])], 3)
    arrays = {
        "x": a["x"][0],
        "w_gla": _tiles(np, group(4, ((gk, 128), (gq, 128), (gog, 256))), P),
        "w_gla_v": _tiles(np, cols(gv, 1024), GLA_DV),
        "w_rwkv": _tiles(np, group(8, ((rk, 128), (rr, 128), (rv, 128))), P),
        "w_lora": _tiles(np, np.concatenate([cols(rwl, 256), cols(gal, 16)], 1), 272)[0],
        "w_merge": np.ascontiguousarray(merge.reshape(8, P, KT, 4 * P)),
        "w_out": _tiles(np, a["w_out"][0], D)[0],
        "w_up": _tiles(np, a["w_up"][0], P),
        "w_down": a["w_down"][0].reshape(-1, P, D),
        "gla_a_w2": np.ascontiguousarray(a["gla_a_w2"][0].reshape(RANK, 4, P).transpose(1, 0, 2)),
        "gla_par": np.ascontiguousarray(np.concatenate([a["gla_a_b"][0].reshape(4, P, 1),
                                                        np.broadcast_to(per_channel(a["gla_norm"][0]), (4, P, 2))], 2).transpose(1, 0, 2)),
        "rwkv_lora2": np.ascontiguousarray(wa2),
        "rwkv_g2": np.ascontiguousarray(g2),
        "rwkv_par": np.ascontiguousarray(pair.transpose(1, 0, 2)),
        "norms": np.concatenate([per_channel(a["norm_mix"][0]), per_channel(a["norm_mlp"][0]), per_channel(mu[3072:3328])], 1),
        "norm_final": np.ascontiguousarray(np.broadcast_to(a["norm_final"], (P, D))),
        "ident": np.eye(P, dtype=np.float32),
        "ones": np.ones((P, P), np.float32),
        "block_ones": (i // HEAD == j // HEAD).astype(np.float32),
        "level_mask": np.ascontiguousarray(np.stack(levels, 1).astype(np.float32)),
        "score_mask": np.concatenate([strict, incl, strict, incl], 1).astype(np.uint32),
        "restart": np.ascontiguousarray(np.broadcast_to((np.arange(HALF) % CHUNK != 0).astype(np.float32), (P, HALF))),
    }
    nc = bacc.Bacc("TRN2", target_bir_lowering=False, num_devices=1)
    d = {n: nc.dram_tensor(f"in_{n}", v.shape, mybir.dt.from_np(v.dtype), kind="ExternalInput").ap() for n, v in arrays.items()}
    d["out"] = nc.dram_tensor("out", (SEQ, D), F32, kind="ExternalOutput").ap()
    d["y_gla"] = nc.dram_tensor("y_gla", (GLA_HEADS, 2, P, SEQ), F32, kind="Internal").ap()
    d["y_rwkv"] = nc.dram_tensor("y_rwkv", (RWKV_PAIRS, P, SEQ), F32, kind="Internal").ap()
    build(nc, d)
    r = run_bass_kernel_spmd(nc, [{f"in_{n}": v for n, v in arrays.items()}], core_ids=[0])
    return r.results[0]["out"].reshape(1, SEQ, D)
```

```python
from contextlib import ExitStack

import concourse.bass as bass
from concourse import mybir

P = 128
F32 = mybir.dt.float32
F32R = mybir.dt.float32r
U32 = mybir.dt.uint32
ALU = mybir.AluOpType
ACT = mybir.ActivationFunctionType

D = 1024
SEQ = 1024
KT = D // P
HALF = 512
CHUNK = 128
NC = HALF // CHUNK
GLA_HEADS, GLA_DK, GLA_DV = 4, 128, 256
RANK = 16
RWKV_PAIRS = 8
HEAD = 64
LEVELS = 6
FF_GROUPS, FF_TILES = 8, 4
NORM_EPS, GLA_EPS, GN_EPS = 1e-6, 1e-5, 64e-5
DECAY = 0.6065306597126334
MU_R, MU_K, MU_V, W0, A0, K_K, K_A, R_K, LN_W, LN_B = range(10)
NPAR = 10


class Steps:

    def __init__(self, nc, sems, name, names):
        self.sem = sems.enter_context(nc.semaphore(name))
        self.names = {x: n for n, x in enumerate(names)}
        self.n = len(names)
        assert len(self.names) == self.n
        self.at = 0

    def start(self, eng):
        eng.sem_inc(self.sem, 2 * self.n)

    def done(self, ins, name):
        assert self.names[name] == self.at, (name, self.at)
        self.at = (self.at + 1) % self.n
        ins.then_inc(self.sem, 1)

    def need(self, eng, name, unit, back=0):
        eng.wait_ge(self.sem, unit * self.n + ((2 - back) * self.n + self.names[name] + 1))

    def need_before(self, eng, name, unit):
        self.need(eng, name, unit, 1)


def _prepare(nc, sems, d, hT_hi, hT_lo, w_hi, w_lo, cst):
    ident = cst["ident"]
    with ExitStack() as ctx:
        sb = lambda n, s: ctx.enter_context(nc.sbuf_tensor(n, s, F32))
        x = sb("p_x", [P, KT, D])
        junk = sb("p_junk", [P, D])
        w_raw = sb("p_w_raw", [P, KT, 272])
        ident_in, norms_in, w_in, w_split = (sems.enter_context(nc.semaphore(n)) for n in ("ident_in", "norms_in", "lora_w_in", "lora_w_split"))
        ss = sb("p_ss", [P, 8])
        rs = sb("p_rs", [P, 8])
        bank = [ctx.enter_context(nc.psum_tensor(f"p_ps{i}", [P, HALF], F32)) for i in range(8)]
        x_in = [sems.enter_context(nc.semaphore(f"x_in{t}")) for t in range(KT)]
        const_in = sems.enter_context(nc.semaphore("const_in"))
        squares = sems.enter_context(nc.semaphore("squares"))
        mean_eps = sems.enter_context(nc.semaphore("mean_eps"))
        root = sems.enter_context(nc.semaphore("root"))
        rstd = sems.enter_context(nc.semaphore("rstd"))
        scaled = sems.enter_context(nc.semaphore("scaled"))
        turned = sems.enter_context(nc.semaphore("turned"))
        high = sems.enter_context(nc.semaphore("high"))
        evacuated = sems.enter_context(nc.semaphore("evacuated"))
        block = ctx.enter_context(nc.Block())

        @block.sync
        def _(sp):
            for t in range(KT):
                sp.dma_start(x[:, t, :], d["x"][t * P:(t + 1) * P, :]).then_inc(x_in[t], 16)
                if t == 1:
                    sp.dma_start(cst["ident"][:], d["ident"]).then_inc(ident_in, 16)
                    sp.dma_start(cst["norms"][:], d["norms"]).then_inc(norms_in, 16)
            sp.dma_start(w_raw[:], d["w_lora"]).then_inc(w_in, 16)
            n = 0
            for name in ("ones", "block_ones", "score_mask", "level_mask", "restart"):
                sp.dma_start(cst[name][:], d[name]).then_inc(const_in, 16)
                n += 16
            sp.wait_ge(const_in, n)

        @block.scalar
        def _(act):
            def high_parts(h):
                if h == 0:
                    act.wait_ge(norms_in, 16)
                for k in range(KT):
                    n = h * KT + k
                    act.wait_ge(turned, n + 1)
                    nc.scalar.activation(hT_hi[:, k, h * HALF:(h + 1) * HALF], bank[n % 8][:], ACT.Copy,
                                         scale=cst["norms"][:, k:k + 1]).then_inc(high, 1)
            for t in range(KT):
                act.wait_ge(x_in[t], 16)
                if t:
                    act.wait_ge(squares, t)
                nc.scalar.activation(junk[:], x[:, t, :], ACT.Square, accum_out=ss[:, t:t + 1]).then_inc(squares, 1)
                act.wait_ge(mean_eps, t + 1)
                nc.scalar.activation(rs[:, t:t + 1], ss[:, t:t + 1], ACT.Sqrt).then_inc(root, 1)
                if t == 5:
                    high_parts(0)
            act.wait_ge(w_in, 16)
            nc.scalar.activation(w_hi[:], w_raw[:], ACT.Copy).then_inc(w_split, 1)
            high_parts(1)

        @block.vector
        def _(dve):
            def low_parts(h):
                for k in range(KT):
                    dve.wait_ge(high, h * KT + k + 1)
                    s = slice(h * HALF, (h + 1) * HALF)
                    nc.vector.scalar_tensor_tensor(hT_lo[:, k, s], bank[(h * KT + k) % 8][:], cst["norms"][:, k:k + 1],
                                                   hT_hi[:, k, s].bitcast(F32), ALU.mult, ALU.subtract).then_inc(evacuated, 1)
            for t in range(KT):
                c = slice(t, t + 1)
                dve.wait_ge(squares, t + 1)
                nc.vector.tensor_scalar(ss[:, c], ss[:, c], 1.0 / D, NORM_EPS, ALU.mult, ALU.add).then_inc(mean_eps, 1)
                dve.wait_ge(root, t + 1)
                nc.vector.reciprocal(rs[:, c], rs[:, c]).then_inc(rstd, 1)
                dve.wait_ge(rstd, t + 1)
                nc.vector.tensor_scalar(x[:, t, :], x[:, t, :], rs[:, c], None, ALU.mult).then_inc(scaled, 1)
                if t == 5:
                    low_parts(0)
            dve.wait_ge(w_split, 1)
            nc.vector.tensor_tensor(w_lo[:], w_raw[:], w_hi[:].bitcast(F32), ALU.subtract).then_inc(w_split, 1)
            low_parts(1)
            dve.wait_ge(evacuated, 2 * KT)

        @block.tensor
        def _(pe):
            pe.wait_ge(ident_in, 16)
            for h in range(2):
                pe.wait_ge(scaled, 4 * h + 4)
                for k in range(KT):
                    n = h * KT + k
                    if n >= 8:
                        pe.wait_ge(evacuated, n - 7)
                    for j in range(4):
                        mm = pe.transpose(bank[n % 8][:, j * P:(j + 1) * P],
                                          x[:, 4 * h + j, k * P:(k + 1) * P], ident[:])
                    mm.then_inc(turned, 1)


def _product(pe, out, w_hi, w_lo, x_hi, x_lo, first, last):
    pe.matmul(out, w_hi, x_hi, start=first, stop=False)
    pe.matmul(out, w_hi, x_lo, start=False, stop=False)
    return pe.matmul(out, w_lo, x_hi, start=False, stop=last)


def _whole(nc, sems, hT_hi, hT_lo, hT):
    with ExitStack() as ctx:
        summed, summed_pool = (sems.enter_context(nc.semaphore(n)) for n in ("h_summed", "h_summed_pool"))
        block = ctx.enter_context(nc.Block())
        cut = 6

        def add(eng, lo, hi, sem):
            for k in range(lo, hi):
                eng.tensor_tensor(hT[:, k, :], hT_hi[:, k, :].bitcast(F32), hT_lo[:, k, :].bitcast(F32), ALU.add).then_inc(sem, 1)

        @block.vector
        def _(dve):
            add(nc.vector, 0, cut, summed)
            dve.wait_ge(summed, cut)

        @block.gpsimd
        def _(pool):
            add(nc.gpsimd, cut, KT, summed_pool)
            pool.wait_ge(summed_pool, KT - cut)


def _low_rank(nc, sems, hT_hi, hT_lo, w_hi, w_lo, lora_wa, lora_g, gla_al, norms):
    with ExitStack() as ctx:
        sb = lambda n, s: ctx.enter_context(nc.sbuf_tensor(n, s, F32))
        raw = [sb(f"l_raw{i}", [P, 1 + SEQ]) for i in range(2)]
        diff = sb("l_diff", [P, SEQ])
        bank = [ctx.enter_context(nc.psum_tensor(f"l_ps{i}", [P, HALF], F32)) for i in range(6)]
        sem = lambda n: sems.enter_context(nc.semaphore(n))
        product, copied, zeroed, shifted, gated = map(sem, ("l_product", "l_copied", "l_zeroed", "l_shifted", "l_gated"))
        block = ctx.enter_context(nc.Block())

        @block.tensor
        def _(pe):
            for n in range(6):
                q, h = n // 2, n % 2
                a, b = ((0, P), (P, 2 * P), (2 * P, 2 * P + RANK))[q]
                for k in range(KT):
                    mm = _product(pe, bank[n][0:b - a, :], w_hi[:, k, a:b], w_lo[:, k, a:b], hT_hi[:, k, h * HALF:(h + 1) * HALF],
                                  hT_lo[:, k, h * HALF:(h + 1) * HALF], k == 0, k == KT - 1)
                mm.then_inc(product, 1)

        @block.scalar
        def _(act):
            for n in range(6):
                q, h = n // 2, n % 2
                act.wait_ge(product, n + 1)
                if q < 2:
                    out, src = raw[q][:, 1 + h * HALF:1 + (h + 1) * HALF], bank[n][:]
                else:
                    out, src = gla_al[0:RANK, h * HALF:(h + 1) * HALF], bank[n][0:RANK, :]
                nc.scalar.activation(out, src, ACT.Copy).then_inc(copied, 1)
            act.wait_ge(shifted, 4)
            nc.scalar.activation(lora_wa[0:HEAD, :], lora_wa[0:HEAD, :], ACT.Tanh).then_inc(gated, 1)
            nc.scalar.activation(lora_g[:], lora_g[:], ACT.Tanh, scale=0.5).then_inc(gated, 1)

        @block.vector
        def _(dve):
            for q in range(2):
                nc.vector.memset(raw[q][:, 0:1], 0.0).then_inc(zeroed, 1)
            dve.wait_ge(zeroed, 2)
            for q, out in enumerate((lora_wa, lora_g)):
                dve.wait_ge(copied, 2 * q + 2)
                if q:
                    dve.wait_ge(shifted, 2)
                nc.vector.tensor_tensor(diff[:], raw[q][:, 0:SEQ], raw[q][:, 1:1 + SEQ], ALU.subtract).then_inc(shifted, 1)
                dve.wait_ge(shifted, 2 * q + 1)
                nc.vector.scalar_tensor_tensor(out[:], diff[:], norms[:, 16 + q:17 + q], raw[q][:, 1:1 + SEQ],
                                               ALU.mult, ALU.add).then_inc(shifted, 1)
            dve.wait_ge(gated, 2)
            nc.vector.tensor_scalar(lora_g[:], lora_g[:], 0.5, 0.5, ALU.mult, ALU.add).then_inc(gated, 1)
            dve.wait_ge(gated, 3)


def _gla(nc, sems, d, hT_hi, hT_lo, gla_al, y_dram, cst):
    ident, ones = cst["ident"], cst["ones"]
    causal = cst["score_mask"][:, P:2 * P]
    with ExitStack() as ctx:
        sb = lambda n, s, dt=F32: ctx.enter_context(nc.sbuf_tensor(n, s, dt))
        t = lambda n: sb(n, [P, HALF])
        two = lambda n, s=(P, HALF): [sb(f"{n}{h}", list(s)) for h in range(2)]
        PROJ = ("k", "q", "og0", "og1")
        raw = [sb(f"g_raw{i}", [P, D]) for i in range(2)]
        w_hi, w_lo = ([sb(f"g_w_{n}_{x}", [P, D], F32R) for n in PROJ] for x in ("hi", "lo"))
        wv_hi, wv_lo = (sb(f"g_w_v_{x}", [P, KT * GLA_DV], F32R) for x in ("hi", "lo"))
        aw = sb("g_aw", [RANK, P])
        par_all, par_now = sb("g_par_all", [P, GLA_HEADS, 3]), two("g_par", (P, 3))
        az, mz, la, cum, up, down = map(t, ("g_az", "g_mz", "g_la", "g_cum", "g_up", "g_down"))
        silu_t = [t(f"g_silu_t{x}") for x in range(2)]
        q, k = two("g_q"), two("g_k")
        v, silu, small = two("g_v", (P, NC, GLA_DV)), two("g_silu", (P, 2, HALF)), two("g_small", (P, 4 * NC))
        k_tok, scores = t("g_kt"), sb("g_scores", [P, NC, CHUNK])
        state = [sb(f"g_state{i}", [P, GLA_DV]) for i in range(2)]
        o, sq, rs = sb("g_o", [P, 2, HALF]), sb("g_sq", [P, 2, HALF]), t("g_rs")
        y_out = two("g_yout", (P, 2, HALF))
        touch, eps = sb("g_touch", [P, 1]), sb("g_eps", [P, 1])
        bank = [ctx.enter_context(nc.psum_tensor(f"g_ps{i}", [P, HALF], F32)) for i in range(8)]
        sem = lambda n: sems.enter_context(nc.semaphore(n))
        stored = [sem(f"g_stored{h}") for h in range(2)]
        raw_in = [sem(f"g_raw_in{n}") for n in range(2)]
        aw_in, par_in, zeroed = map(sem, ("g_aw_in", "g_par_in", "g_zeroed"))
        pf = Steps(nc, sems, "g_pe_front", ["z", "k", "q", "og0", "og1", "v0", "v1"])
        af = Steps(nc, sems, "g_act_front", ["abs_z", "exp_z", "log_z", "k", "up", "down", "mid", "decay", "q", "og0", "og1", "v0", "v1"])
        df = Steps(nc, sems, "g_dve_front", ["par", "min_z", "log_a", "cum", "mid", "from_mid", "to_end", "to_next", "k", "q",
                                             "half0", "silu0", "half1", "silu1"])
        pb = Steps(nc, sems, "g_pe_back", ["k_tok", "scores"] + [f"{x}{c}" for c in range(NC) for x in ("state", "o")] + ["mean"])
        ab = Steps(nc, sems, "g_act_back", ["k_tok"] + [f"state{c}" for c in range(NC)] + ["o0", "o1", "sq0", "sq1", "var_log", "rstd"])
        db = Steps(nc, sems, "g_dve_back", ["scores", "start", "n0", "n1", "y0", "y1"])
        WEIGHTS = PROJ + ("v_low", "v_high")
        sa, sd = Steps(nc, sems, "g_act_split", WEIGHTS), Steps(nc, sems, "g_dve_split", WEIGHTS)
        block = ctx.enter_context(nc.Block())
        last = GLA_HEADS - 1

        def parts(name):
            n = WEIGHTS.index(name)
            if n < 4:
                return w_hi[n][:], w_lo[n][:]
            s = slice((n - 4) * D, (n - 3) * D)
            return wv_hi[:, s], wv_lo[:, s]

        def act_split(act, name, g):
            n = WEIGHTS.index(name)
            pf.need(act, name if n < 4 else "v1", g * 2, 1)
            act.wait_ge(raw_in[n % 2], g * 48 + 16 * (n // 2 + 1))
            sa.done(nc.scalar.activation(parts(name)[0], raw[n % 2][:], ACT.Copy), name)

        def dve_split(dve, name, g):
            hi, lo = parts(name)
            sa.need(dve, name, g)
            sd.done(nc.vector.tensor_tensor(lo, raw[WEIGHTS.index(name) % 2][:], hi.bitcast(F32), ALU.subtract), name)

        def walk(eng, front, back, split=lambda g: None):
            split(0)
            for _ in front(0, 0):
                pass
            back(0, 0, front(0, 1))
            with eng.Fori(0, last) as g:
                split(g + 1)
                back(g, 1, front(g + 1, 0))
                back(g + 1, 0, front(g + 1, 1))
            back(last, 1, None)

        @block.sync
        def _(sp):
            sp.dma_start(par_all[:], d["gla_par"]).then_inc(par_in, 16)

            def load(g):
                pf.need(sp, "z", g * 2, 1)
                sp.dma_start(aw[:], d["gla_a_w2"][bass.ds(g, 1)].rearrange("o p n -> p (o n)")).then_inc(aw_in, 16)
                for n, name in enumerate(WEIGHTS):
                    if n < 2:
                        sd.need_before(sp, WEIGHTS[n - 2], g)
                    else:
                        sd.need(sp, WEIGHTS[n - 2], g)
                    if n < 4:
                        src = d["w_gla"][bass.ds(g * 4 + n, 1)].rearrange("o p k n -> p (o k n)")
                    else:
                        src = d["w_gla_v"][bass.ds(g, 1), :, (n - 4) * 4:(n - 3) * 4].rearrange("o p k n -> p (o k n)")
                    sp.dma_start(raw[n % 2][:], src).then_inc(raw_in[n % 2], 16)

            def store(g):
                for h in range(2):
                    db.need(sp, "y1", g * 2 + h)
                    sp.dma_start(y_dram[bass.ds(g * 2, 2), :, h * HALF:(h + 1) * HALF].rearrange("x p t -> p x t"), y_out[h][:]).then_inc(stored[h], 16)

            load(0)
            with sp.Fori(0, last) as g:
                load(g + 1)
                store(g)
            store(last)
            for h in range(2):
                sp.wait_ge(stored[h], 16 * GLA_HEADS + 16)

        @block.tensor
        def _(pe):
            pf.start(pe)
            pb.start(pe)

            def front(g, h):
                u = g * 2 + h
                tok = slice(h * HALF, (h + 1) * HALF)
                af.need(pe, "v0", u, 1)
                pe.wait_ge(aw_in, g * 16 + 16)
                pf.done(pe.matmul(bank[2][:], aw[:], gla_al[0:RANK, tok], start=True, stop=True), "z")
                yield
                free = (lambda: af.need(pe, "v1", u, 1), lambda: df.need(pe, "silu1", u, 1),
                        lambda: af.need(pe, "k", u), lambda: af.need(pe, "q", u))
                for n, name in enumerate(PROJ):
                    free[n]()
                    if h == 0:
                        sd.need(pe, name, g)
                    for kt in range(KT):
                        cols = slice(kt * P, (kt + 1) * P)
                        mm = _product(pe, bank[n % 2][:], w_hi[n][:, cols], w_lo[n][:, cols], hT_hi[:, kt, tok], hT_lo[:, kt, tok],
                                      kt == 0, kt == KT - 1)
                        if kt == KT - 1:
                            pf.done(mm, name)
                        yield
                df.need(pe, "min_z", u)
                if h == 0:
                    sd.need(pe, "v_high", g)
                for j in range(2):
                    if j:
                        df.need(pe, "silu0", u)
                    for c in range(2):
                        t0 = h * HALF + (2 * j + c) * P
                        for kt in range(KT):
                            cols = slice(kt * GLA_DV, (kt + 1) * GLA_DV)
                            mm = _product(pe, bank[(2, 0)[j]][:, c * GLA_DV:(c + 1) * GLA_DV], hT_hi[:, kt, t0:t0 + P], hT_lo[:, kt, t0:t0 + P],
                                          wv_hi[:, cols], wv_lo[:, cols], kt == 0, kt == KT - 1)
                            if c == 1 and kt == KT - 1:
                                pf.done(mm, f"v{j}")
                            if kt % 2:
                                yield

            def back(g, h, fill):
                u = g * 2 + h
                df.need(pe, "k", u)
                ab.need(pe, "var_log", u, 1)
                for c in range(NC):
                    s = slice(c * P, (c + 1) * P)
                    mm = pe.transpose(bank[5][:, s], k[h][:, s], ident[:])
                pb.done(mm, "k_tok")
                df.need(pe, "q", u)
                for c in range(NC):
                    s = slice(c * P, (c + 1) * P)
                    mm = pe.matmul(bank[6][:, s], k[h][:, s], q[h][:, s], start=True, stop=True)
                pb.done(mm, "scores")
                _advance(fill, 5)
                ab.need(pe, "k_tok", u)
                af.need(pe, "v1", u)
                for c in range(NC):
                    s = slice(c * P, (c + 1) * P)
                    if c:
                        ab.need(pe, f"state{c - 1}", u)
                    else:
                        db.need(pe, "start", u)
                    pe.matmul(bank[7][:, 0:GLA_DV], k_tok[:, s], v[h][:, c, :], start=True, stop=False)
                    mm = pe.matmul(bank[7][:, 0:GLA_DV], ident[:], state[c % 2][:], start=False, stop=True)
                    pb.done(mm, f"state{c}")
                    if c == 0:
                        db.need(pe, "scores", u)
                        ab.need(pe, "sq1", u, 1)
                    for x in range(2):
                        vs = slice(x * P, (x + 1) * P)
                        pe.matmul(bank[3 + x][:, s], v[h][:, c, vs], scores[:, c, :], start=True, stop=False)
                        mm = pe.matmul(bank[3 + x][:, s], state[c % 2][:, vs], q[h][:, s], start=False, stop=True)
                    pb.done(mm, f"o{c}")
                    _advance(fill, (7, 7, 7, 6)[c])
                ab.need(pe, "sq1", u)
                pe.matmul(bank[5][:], ones[:], sq[:, 0, :], start=True, stop=False)
                pb.done(pe.matmul(bank[5][:], ones[:], sq[:, 1, :], start=False, stop=True), "mean")
                _advance(fill, 100)

            walk(pe, front, back)

        @block.scalar
        def _(act):
            af.start(act)
            ab.start(act)
            A = nc.scalar.activation
            sa.start(act)
            act.wait_ge(zeroed, 2)

            def front(g, h):
                u = g * 2 + h
                sm = small[h]
                split = (lambda name: act_split(act, name, g)) if h == 0 else lambda name: None
                split("q")
                pf.need(act, "z", u)
                df.need(act, "par", u)
                df.need(act, "log_a", u, 1)
                af.done(A(az[:], bank[2][:], ACT.Abs, bias=par_now[h][:, 0:1]), "abs_z")
                af.need(act, "abs_z", u)
                af.done(A(az[:], az[:], ACT.Exp, scale=-1.0), "exp_z")
                af.need(act, "exp_z", u)
                af.done(A(az[:], az[:], ACT.Ln, bias=1.0), "log_z")
                split("og0")
                yield
                pf.need(act, "k", u)
                af.done(A(k[h][:], bank[0][:], ACT.Copy), "k")
                split("og1")
                yield
                df.need(act, "q", u, 1)
                df.need(act, "to_next", u)
                af.done(A(up[:], la[:], ACT.Exp, scale=1 / 16), "up")
                af.done(A(down[:], la[:], ACT.Exp, scale=-1 / 16), "down")
                af.done(A(sm[:, 2 * NC:3 * NC], sm[:, 0:NC], ACT.Exp, scale=1 / 16), "mid")
                af.done(A(sm[:, 3 * NC:4 * NC], sm[:, NC:2 * NC], ACT.Exp, scale=1 / 16), "decay")
                split("v_low")
                yield
                pf.need(act, "q", u)
                af.done(A(q[h][:], bank[1][:], ACT.Copy, scale=GLA_DK ** -0.5), "q")
                split("v_high")
                yield
                for x in range(2):
                    pf.need(act, f"og{x}", u)
                    df.need(act, f"silu{x}", u, 1)
                    af.done(A(silu_t[x][:], bank[x][:], ACT.Tanh, scale=0.5), f"og{x}")
                    yield
                for x in range(2):
                    pf.need(act, f"v{x}", u)
                    af.done(A(v[h][:, 2 * x:2 * x + 2, :].rearrange("p a b -> p (a b)"), bank[(2, 0)[x]][:], ACT.Copy), f"v{x}")
                    yield

            def back(g, h, fill):
                u = g * 2 + h
                pb.need(act, "k_tok", u)
                ab.done(A(k_tok[:], bank[5][:], ACT.Copy), "k_tok")
                _advance(fill, 1)
                af.need(act, "decay", u)
                for c in range(NC):
                    pb.need(act, f"state{c}", u)
                    if c:
                        pb.need(act, f"o{c - 1}", u)
                    ab.done(A(state[(c + 1) % 2][:], bank[7][:, 0:GLA_DV], ACT.Copy,
                              scale=small[h][:, 3 * NC + c:3 * NC + c + 1]), f"state{c}")
                    _advance(fill, 1)
                pb.need(act, f"o{NC - 1}", u)
                db.need(act, "y1", u, 1)
                for x in range(2):
                    ab.done(A(o[:, x, :], bank[3 + x][:], ACT.Copy), f"o{x}")
                for x in range(2):
                    ab.done(A(sq[:, x, :], bank[3 + x][:], ACT.Square, scale=GLA_DV ** -0.5), f"sq{x}")
                _advance(fill, 1)
                pb.need(act, "mean", u)
                ab.done(A(rs[:], bank[5][:], ACT.Ln, bias=eps[:, 0:1]), "var_log")
                ab.need(act, "var_log", u)
                ab.done(A(rs[:], rs[:], ACT.Exp, scale=-0.5), "rstd")
                _advance(fill, 100)

            walk(act, front, back, lambda g: act_split(act, "k", g))

        @block.vector
        def _(dve):
            V = nc.vector
            for x in stored:
                dve.sem_inc(x, 16)
            V.memset(scores[:], 0.0).then_inc(zeroed, 1)
            V.memset(eps[:], GLA_EPS).then_inc(zeroed, 1)
            dve.wait_ge(zeroed, 2)
            dve.wait_ge(par_in, 16)
            df.start(dve)
            db.start(dve)
            sd.start(dve)

            def front(g, h):
                u = g * 2 + h
                split = (lambda name: dve_split(dve, name, g)) if h == 0 else lambda name: None
                split("q")
                ab.need(dve, f"state{NC - 1}", u, 2)
                df.done(V.tensor_scalar(par_now[h][:], par_all[:, bass.ds(g, 1), :].rearrange("p o n -> p (o n)"), 1.0, None, ALU.mult), "par")
                df.need(dve, "par", u)
                af.need(dve, "abs_z", u)
                df.done(V.tensor_scalar(mz[:], bank[2][:], par_now[h][:, 0:1], 0.0, ALU.add, ALU.min), "min_z")
                df.need(dve, "min_z", u)
                af.need(dve, "log_z", u)
                df.done(V.tensor_tensor(la[:], mz[:], az[:], ALU.subtract), "log_a")
                df.need(dve, "log_a", u)
                df.done(V.tensor_tensor_scan(cum[:], cst["restart"][:], la[:], 0.0, ALU.mult, ALU.add), "cum")
                _chunk_small(nc, dve, df, u, cum, la, small[h])
                split("og0")
                split("og1")
                yield
                for name, x, factor in (("k", k, down), ("q", q, up)):
                    af.need(dve, name, u)
                    af.need(dve, "down", u)
                    df.done(V.tensor_tensor(x[h][:], x[h][:], factor[:], ALU.mult), name)
                    split("v_low" if name == "k" else "v_high")
                    yield
                for x in range(2):
                    af.need(dve, f"og{x}", u)
                    df.done(V.tensor_scalar(silu_t[x][:], silu_t[x][:], 0.5, 0.5, ALU.mult, ALU.add), f"half{x}")
                    df.need(dve, f"half{x}", u)
                    df.done(V.tensor_tensor(silu[h][:, x, :], bank[x][:], silu_t[x][:], ALU.mult), f"silu{x}")
                    yield

            def back(g, h, fill):
                u = g * 2 + h
                pb.need(dve, "scores", u)
                V.memset(touch[:], 0.0)
                db.done(V.copy_predicated(scores[:], _over(causal, NC), bank[6][:].rearrange("p (c t) -> p c t", c=NC)), "scores")
                ab.need(dve, f"state{NC - 1}", u, 1)
                if h == 0:
                    db.done(V.memset(state[0][:], 0.0), "start")
                else:
                    af.need(dve, "mid", u)
                    db.done(V.tensor_scalar(state[0][:], state[0][:], small[h][:, 2 * NC:2 * NC + 1], None, ALU.mult), "start")
                _advance(fill, 100)
                ab.need(dve, "rstd", u)
                for x in range(2):
                    db.done(V.scalar_tensor_tensor(o[:, x, :], o[:, x, :], par_now[h][:, 1 + x:2 + x], rs[:], ALU.mult, ALU.mult), f"n{x}")
                for x in range(2):
                    db.need(dve, f"n{x}", u)
                    if x == 0:
                        dve.wait_ge(stored[h], g * 16 + 16)
                    db.done(V.tensor_tensor(y_out[h][:, x, :], o[:, x, :], silu[h][:, x, :], ALU.mult), f"y{x}")

            walk(dve, front, back, lambda g: dve_split(dve, "k", g))


def _over(mask, n):
    return mask.rearrange("p (o t) -> p o t", o=1).to_broadcast([P, n, CHUNK])


def _chunk_small(nc, dve, dve_s, u, cum, out, small):
    c3 = cum[:].rearrange("p (c t) -> p c t", c=NC)
    mid, end = c3[:, :, CHUNK // 2 - 1:CHUNK // 2], c3[:, :, CHUNK - 1:CHUNK]
    s3 = small[:].rearrange("p (k c o) -> p k c o", k=4, o=1)
    dve_s.need(dve, "cum", u)
    dve_s.done(nc.vector.tensor_copy(s3[:, 0], mid), "mid")
    dve_s.need(dve, "mid", u)
    dve_s.done(nc.vector.tensor_tensor(out[:].rearrange("p (c t) -> p c t", c=NC), c3,
                                       s3[:, 0].to_broadcast([P, NC, CHUNK]), ALU.subtract), "from_mid")
    dve_s.done(nc.vector.tensor_tensor(s3[:, 1], end, s3[:, 0], ALU.subtract), "to_end")
    dve_s.need(dve, "to_end", u)
    dve_s.done(nc.vector.tensor_tensor(s3[:, 1, 0:NC - 1], s3[:, 1, 0:NC - 1], s3[:, 0, 1:NC], ALU.add), "to_next")


def _advance(steps, n):
    for _ in range(n if steps else 0):
        next(steps, None)


def _rwkv(nc, sems, d, hT, lora_wa, lora_g, y_dram, cst):
    ident, block_ones = cst["ident"], cst["block_ones"]
    with ExitStack() as ctx:
        sb = lambda n, s, dt=F32: ctx.enter_context(nc.sbuf_tensor(n, s, dt))
        t = lambda n: sb(n, [P, HALF])
        two = lambda n, s=(P, HALF): [sb(f"{n}{h}", list(s)) for h in range(2)]
        w = [sb(f"r_w{n}", [P, KT, P]) for n in range(3)]
        lora2, gate2 = sb("r_lora2", [P, P]), sb("r_gate2", [P, P])
        par_all, par_now = sb("r_par_all", [P, RWKV_PAIRS, NPAR]), two("r_par", (P, NPAR))
        half_par = sb("r_half_par", [P, 2])
        raw = [sb(f"r_raw{i}", [P, 1 + SEQ]) for i in range(3)]
        diff = [t(f"r_diff{n}") for n in range(3)]
        r, k, log_w, cum, from_mid, a, kk, sq, norm = map(t, ("r_r", "r_k", "r_lw", "r_cum", "r_fm", "r_a", "r_kk", "r_sq", "r_norm"))
        up, down, prev = map(t, ("r_up", "r_down", "r_prev"))
        gain = sq
        rk = from_mid
        v, k_bar, b_bar, gate, bonus = map(two, ("r_v", "r_kbar", "r_bbar", "r_gate", "r_bonus"))
        ar, small = two("r_ar", (P, NC, 2, CHUNK)), two("r_small", (P, 4 * NC))
        k_tok, b_tok, v_tok = map(t, ("r_kt", "r_bt", "r_vt"))
        scores = sb("r_scores", [P, 2 * NC, 4, CHUNK])
        tiles = lambda n: [sb(f"{n}{b}", [P, 4, CHUNK], F32R) for b in range(2)]
        a_hi, a_lo, invT, inv, prod = map(tiles, ("r_ahi", "r_alo", "r_invT", "r_inv", "r_prod"))
        inverseT = [sb(f"r_inverseT{b}", [P, 4, CHUNK]) for b in range(2)]
        ident_r, minus_r = sb("r_ident", [P, P], F32R), sb("r_minus", [P, P], F32R)
        z, uu = sb("r_z", [P, P]), sb("r_u", [P, P])
        state = [sb(f"r_state{i}", [P, P]) for i in range(2)]
        y, ysq, ln = two("r_y"), t("r_ysq"), two("r_ln", (P, 2))
        y_out = two("r_yout")
        touch, eps = sb("r_touch", [P, 2 * NC]), sb("r_eps", [P, 1])
        bank = [ctx.enter_context(nc.psum_tensor(f"r_ps{i}", [P, HALF], F32)) for i in range(8)]
        sem = lambda n: sems.enter_context(nc.semaphore(n))
        w_in = [sem(f"r_w_in{n}") for n in range(3)]
        lora2_in, gate2_in, par_in, zeroed = map(sem, ("r_lora2_in", "r_gate2_in", "r_par_in", "r_zeroed"))
        stored, spilled = [sem(f"r_stored{h}") for h in range(2)], sem("h_spilled")
        scores_zeroed = sem("r_scores_zeroed")
        ab2, levels = range(2), range(1, LEVELS + 1)
        PROJ = ("k", "r", "v")
        pf = Steps(nc, sems, "pe_front", ["w", "a", "k", "norm", "r", "v", "gate", "bonus"])
        af = Steps(nc, sems, "act_front", ["w", "a", "up", "down", "k", "prev", "kk_sq", "mid", "decay",
                                           "norm_log", "norm_inv", "r", "v", "gate"])
        gf = Steps(nc, sems, "pool_front", ["k_diff", "r_diff", "v_diff"])
        df = Steps(nc, sems, "dve_front", ["par", "half_par", "log_w", "cum", "mid", "from_mid", "to_end", "to_next", "from_prev",
                                           "a", "k_gain", "k", "kk", "k_mod", "k_bar", "norm_floor", "kk_unit", "b", "b_bar", "a_prev",
                                           "r", "r_up", "rk", "v", "bonus", "ln"])
        pb = Steps(nc, sems, "pe_back", ["k_tok", "b_tok"] + [f"scores{j}" for j in range(2 * NC)] + ["v_tok", "inv0.0", "inv0.1"]
                   + [f"{x}{l}.{b}" for l in levels for x in ("prod", "inv") for b in ab2]
                   + [f"{x}{b}" for x in ("res", "inverse") for b in ab2]
                   + [f"{x}{c}" for c in range(NC) for x in ("z", "u", "s", "y")])
        ab = Steps(nc, sems, "act_back", ["k_tok", "b_tok", "v_tok", "a_hi0", "a_hi1"]
                   + ["res0", "res1"] + [f"{x}{c}" for c in range(NC) for x in ("z", "s")] + ["y"])
        gb = Steps(nc, sems, "pool_back", ["a_lo0", "a_lo1"])
        db = Steps(nc, sems, "dve_back", [f"scores{j}" for j in range(2 * NC)] + [f"{x}{b}" for b in ab2 for x in ("invT_mask", "invT0.")]
                   + ["inv0.0", "inv0.1"] + [f"{x}{l}.{b}" for l in levels for x in ("prod", "inv", "invT") for b in ab2]
                   + ["inverse0", "inverse1", "start0", "start1"] + [f"{x}{c}" for c in range(NC) for x in ("u", "s")])
        pn = Steps(nc, sems, "pe_norm", ["mean", "var"])
        an = Steps(nc, sems, "act_norm", ["y_sq", "var", "var_log", "rstd"])
        dn = Steps(nc, sems, "dve_norm", ["centred", "n", "affine", "plus", "out"])
        block = ctx.enter_context(nc.Block())
        end, last = f"y{NC - 1}", RWKV_PAIRS - 1

        def walk(eng, front, back):
            for _ in front(0, 0, False):
                pass
            back(0, 0, front(0, 1, False))
            with eng.Fori(0, last) as p:
                back(p, 1, front(p + 1, 0, True))
                back(p + 1, 0, front(p + 1, 1, True))
            back(last, 1, front(RWKV_PAIRS, 0, True, False))
            for _ in front(RWKV_PAIRS, 1, True, False):
                pass

        @block.sync
        def _(sp):
            sp.dma_start(par_all[:], d["rwkv_par"]).then_inc(par_in, 16)

            def load(p):
                pf.need(sp, "a", p * 2, 1)
                sp.dma_start(lora2[:], d["rwkv_lora2"][bass.ds(p, 1)].rearrange("o p n -> p (o n)")).then_inc(lora2_in, 16)
                for n, name in enumerate(PROJ):
                    pf.need(sp, name, p * 2, 1)
                    sp.dma_start(w[n][:], d["w_rwkv"][bass.ds(p * 3 + n, 1)].rearrange("o p k n -> p (o k) n")).then_inc(w_in[n], 16)
                pf.need(sp, "gate", p * 2, 1)
                sp.dma_start(gate2[:], d["rwkv_g2"][bass.ds(p, 1)].rearrange("o p n -> p (o n)")).then_inc(gate2_in, 16)

            def store(p):
                for h in range(2):
                    dn.need(sp, "out", p * 2 + h)
                    sp.dma_start(y_dram[bass.ds(p, 1), :, h * HALF:(h + 1) * HALF].rearrange("o p t -> p (o t)"), y_out[h][:]).then_inc(stored[h], 16)

            load(0)
            sp.dma_start(d["h_spill"].rearrange("k p t -> p k t"), hT[:]).then_inc(spilled, 16)
            with sp.Fori(0, last) as p:
                load(p + 1)
                store(p)
            store(last)
            for h in range(2):
                sp.wait_ge(stored[h], 16 * RWKV_PAIRS + 16)
            sp.wait_ge(spilled, 16)

        @block.tensor
        def _(pe):
            pf.start(pe)
            pb.start(pe)
            pn.start(pe)

            def front(p, h, norm_, next_=True):
                u = p * 2 + h
                tok = slice(h * HALF, (h + 1) * HALF)

                def low_rank(b, name, lhsT, rhs):
                    return pf.done(pe.matmul(bank[b][:], lhsT, rhs, start=True, stop=True), name)

                def project(name, free, first, end_):
                    n = PROJ.index(name)
                    if first == 0:
                        free()
                        pe.wait_ge(w_in[n], p * 16 + 16)
                    for kt in range(first, end_):
                        mm = pe.matmul(bank[0][:], w[n][:, kt, :], hT[:, kt, tok], start=kt == 0, stop=kt == KT - 1)
                        if kt == KT - 1:
                            pf.done(mm, name)
                        yield

                def var():
                    if norm_:
                        an.need(pe, "y_sq", u - 2)
                        if next_:
                            af.need(pe, "a", u)
                        elif h == 0:
                            af.need(pe, "gate", u, 1)
                        pn.done(pe.matmul(bank[1][:], block_ones[:], ysq[:], start=True, stop=True), "var")
                if norm_:
                    if next_ or h == 0:
                        df.need(pe, "bonus", u, 1)
                    else:
                        dn.need(pe, "centred", u - 3)
                    ab.need(pe, "y", u - 2)
                    pn.done(pe.matmul(bank[0][:], block_ones[:], y[h][:], start=True, stop=True), "mean")
                yield
                if not next_:
                    yield from (None,) * 4
                    var()
                    return
                af.need(pe, "gate", u, 1)
                pe.wait_ge(lora2_in, p * 16 + 16)
                low_rank(1, "w", lora2[0:HEAD, :], lora_wa[0:HEAD, tok])
                yield
                free_k = lambda: dn.need(pe, "centred", u - 2) if norm_ else df.need(pe, "bonus", u, 1)
                yield from project("k", free_k, 0, 1)
                af.need(pe, "w", u)
                low_rank(1, "a", lora2[HEAD:P, :], lora_wa[HEAD:P, tok])
                yield
                yield from project("k", None, 1, KT)
                var()
                yield
                yield from project("r", lambda: af.need(pe, "k", u), 0, 3)
                if norm_:
                    an.need(pe, "var", u - 2)
                else:
                    af.need(pe, "a", u)
                af.need(pe, "kk_sq", u)
                low_rank(1, "norm", block_ones[:], sq[:])
                yield
                yield from project("r", None, 3, KT)
                yield from project("v", lambda: af.need(pe, "r", u), 0, KT)
                df.need(pe, "norm_floor", u)
                pe.wait_ge(gate2_in, p * 16 + 16)
                low_rank(1, "gate", gate2[:], lora_g[:, tok])
                yield

            def back(p, h, fill):
                u = p * 2 + h
                ab.need(pe, f"s{NC - 1}", u, 1)
                db.need(pe, f"s{NC - 1}", u, 1)
                for n, (src, name, ready) in enumerate(((k_bar[h], "k_tok", "k_bar"), (b_bar[h], "b_tok", "b_bar"))):
                    df.need(pe, ready, u)
                    for c in range(NC):
                        s = slice(c * P, (c + 1) * P)
                        mm = pe.transpose(bank[4 + n][:, s], src[:, s], ident[:])
                    pb.done(mm, name)
                af.need(pe, "v", u)
                df.need(pe, "rk", u)
                pf.done(pe.matmul(bank[0][:], block_ones[:], rk[:], start=True, stop=True), "bonus")
                df.need(pe, "r_up", u)
                for j in range(2 * NC):
                    c, hd = j // 2, j % 2
                    rows = slice(hd * HEAD, (hd + 1) * HEAD)
                    b = bank[(2, 6, 3)[j % 3]]
                    if j >= 3:
                        db.need(pe, f"scores{j - 3}", u)
                    rhs = ar[h][rows, c, :, :].rearrange("p k t -> p (k t)")
                    pe.matmul(b[:, 0:2 * P], b_bar[h][rows, c * P:(c + 1) * P], rhs, start=True, stop=True)
                    mm = pe.matmul(b[:, 2 * P:4 * P], k_bar[h][rows, c * P:(c + 1) * P], rhs, start=True, stop=True)
                    pb.done(mm, f"scores{j}")
                df.need(pe, "v", u)
                ab.need(pe, "y", u, 1)
                for c in range(NC):
                    s = slice(c * P, (c + 1) * P)
                    mm = pe.transpose(bank[7][:, s], v[h][:, s], ident[:])
                pb.done(mm, "v_tok")
                _advance(fill, 3)
                ab.need(pe, "b_tok", u)
                for b in ab2:
                    db.need(pe, f"invT0.{b}", u)
                    for i in range(4):
                        mm = pe.matmul(bank[4 + b][:, i * P:(i + 1) * P], invT[b][:, i, :], ident_r[:], start=True, stop=True)
                    pb.done(mm, f"inv0.{b}")
                ab.need(pe, "v_tok", u)
                for l in levels:
                    for b in ab2:
                        db.need(pe, f"inv{l - 1}.{b}", u)
                        if l == 1:
                            ab.need(pe, f"a_hi{b}", u)
                        for i in range(4):
                            mm = pe.matmul(bank[2 + b][:, i * P:(i + 1) * P], a_hi[b][:, i, :], inv[b][:, i, :], start=True, stop=True)
                        pb.done(mm, f"prod{l}.{b}")
                    _advance(fill, (1, 2, 2, 1, 1, 1)[l - 1])
                    for b in ab2:
                        db.need(pe, f"prod{l}.{b}", u)
                        if l > 1:
                            db.need(pe, f"invT{l - 1}.{b}", u)
                        low, high = bank[4 + 2 * b], bank[5 + 2 * b]
                        for i in range(4):
                            s = slice(i * P, (i + 1) * P)
                            pe.matmul(low[:, s], prod[b][:, i, :], invT[b][:, i, :], start=True, stop=True, skip_group_check=True)
                            mm = pe.matmul(high[:, s], invT[b][:, i, :], prod[b][:, i, :], start=True, stop=True, skip_group_check=True)
                        pb.done(mm, f"inv{l}.{b}")
                    _advance(fill, 1)
                for b in ab2:
                    db.need(pe, f"inv{LEVELS}.{b}", u)
                    gb.need(pe, f"a_lo{b}", u)
                    pe.matmul(bank[2 + b][:], minus_r[:], inv[b][:].rearrange("p i t -> p (i t)"), start=True, stop=False, skip_group_check=True)
                    for i in range(4):
                        s = slice(i * P, (i + 1) * P)
                        for q, (x, m) in enumerate(((ident_r[:], ident_r[:]), (a_hi[b][:, i, :], inv[b][:, i, :]), (a_lo[b][:, i, :], inv[b][:, i, :]))):
                            mm = pe.matmul(bank[2 + b][:, s], x, m, start=False, stop=q == 2, skip_group_check=True)
                    pb.done(mm, f"res{b}")
                _advance(fill, 1)
                for b in ab2:
                    ab.need(pe, f"res{b}", u)
                    db.need(pe, f"invT{LEVELS}.{b}", u)
                    pe.matmul(bank[4 + 2 * b][:], ident_r[:], invT[b][:].rearrange("p i t -> p (i t)"), start=True, stop=False, skip_group_check=True)
                    for i in range(4):
                        mm = pe.matmul(bank[4 + 2 * b][:, i * P:(i + 1) * P], prod[b][:, i, :], invT[b][:, i, :], start=False, stop=True, skip_group_check=True)
                    pb.done(mm, f"inverse{b}")
                _advance(fill, 1)
                db.need(pe, "inverse1", u)
                for c in range(NC):
                    s = slice(c * P, (c + 1) * P)
                    now = state[c % 2]
                    new = bank[(6, 3)[c % 2]]
                    for hd in range(2):
                        hs = slice(hd * HEAD, (hd + 1) * HEAD)
                        pe.matmul(bank[4][:, hs], scores[:, 2 * c + hd, 2, :], v_tok[:, c * P + hd * HEAD:c * P + (hd + 1) * HEAD],
                                  start=hd == 0, stop=False, skip_group_check=True)
                    pe.matmul(new[:, 0:P], k_tok[:, s], v_tok[:, s], start=True, stop=False)
                    _advance(fill, 1)
                    if c:
                        ab.need(pe, f"s{c - 1}", u)
                        db.need(pe, f"s{c - 1}", u)
                    else:
                        db.need(pe, "start1", u)
                    pb.done(pe.matmul(bank[4][:, 0:P], ar[h][:, c, 0, :], now[:], start=False, stop=True, skip_group_check=True), f"z{c}")
                    pe.matmul(new[:, 0:P], ident[:], now[:], start=False, stop=False)
                    pe.matmul(bank[7][:, s], now[:], ar[h][:, c, 1, :], start=True, stop=False, skip_group_check=True)
                    _advance(fill, 1)
                    ab.need(pe, f"z{c}", u)
                    for hd in range(2):
                        hs = slice(hd * HEAD, (hd + 1) * HEAD)
                        mm = pe.matmul(bank[5][:, hs], inverseT[c // 2][:, 2 * (c % 2) + hd, :], z[:, hs], start=True, stop=True)
                    pb.done(mm, f"u{c}")
                    for hd in range(2):
                        hs = slice(hd * HEAD, (hd + 1) * HEAD)
                        pe.matmul(bank[7][hs, s], v_tok[:, c * P + hd * HEAD:c * P + (hd + 1) * HEAD], scores[:, 2 * c + hd, 3, :],
                                  start=False, stop=False, skip_group_check=True)
                    _advance(fill, 1 if c < 3 else 0)
                    db.need(pe, f"u{c}", u)
                    pb.done(pe.matmul(new[:, 0:P], b_tok[:, s], uu[:], start=False, stop=True), f"s{c}")
                    for hd in range(2):
                        hs = slice(hd * HEAD, (hd + 1) * HEAD)
                        mm = pe.matmul(bank[7][hs, s], uu[:, hs], scores[:, 2 * c + hd, 1, :], start=False, stop=True, skip_group_check=True)
                    pb.done(mm, f"y{c}")
                _advance(fill, 100)

            walk(pe, front, back)

        @block.gpsimd
        def _(pool):
            gf.start(pool)
            gb.start(pool)
            nc.gpsimd.memset(scores[:], 0.0).then_inc(scores_zeroed, 1)

            def front(p, h, norm_, next_=True):
                u = p * 2 + h
                if not next_:
                    return
                df.need(pool, "bonus", u, 1)
                for n, name in enumerate(PROJ):
                    af.need(pool, name, u)
                    gf.done(nc.gpsimd.tensor_tensor(diff[n][:], raw[n][:, h * HALF:(h + 1) * HALF],
                                                    raw[n][:, 1 + h * HALF:1 + (h + 1) * HALF], ALU.subtract), f"{name}_diff")
                    yield

            def back(p, h, fill):
                u = p * 2 + h
                pb.need(pool, "res1", u, 1)
                for b in ab2:
                    ab.need(pool, f"a_hi{b}", u)
                    db.need(pool, f"scores{4 * b + 3}", u)
                    gb.done(nc.gpsimd.tensor_tensor(a_lo[b][:], scores[:, 4 * b:4 * b + 4, 0, :], a_hi[b][:].bitcast(F32), ALU.subtract), f"a_lo{b}")
                _advance(fill, 100)

            walk(pool, front, back)

        @block.scalar
        def _(act):
            af.start(act)
            ab.start(act)
            an.start(act)
            A = nc.scalar.activation

            def front(p, h, norm_, next_=True):
                u = p * 2 + h
                sm = small[h]

                def var_log():
                    an.need(act, "var", u - 2)
                    an.done(A(ysq[:], ysq[:], ACT.Ln, bias=eps[:, 0:1]), "var_log")

                def rstd():
                    an.need(act, "var_log", u - 2)
                    an.done(A(ysq[:], ysq[:], ACT.Exp, scale=-0.5), "rstd")

                def square():
                    dn.need(act, "centred", u - 2)
                    dn.need(act, "n", u - 2, 1)
                    an.done(A(ysq[:], y[h][:], ACT.Square, scale=0.125), "y_sq")

                def variance():
                    pn.need(act, "var", u - 2)
                    an.done(A(ysq[:], bank[1][:], ACT.Copy), "var")
                if not next_:
                    square()
                    yield from (None,) * 4
                    variance()
                    var_log()
                    rstd()
                    return
                df.need(act, "bonus", u, 1)
                df.need(act, "half_par", u)
                pf.need(act, "w", u)
                af.done(A(log_w[:], bank[1][:], ACT.Tanh, scale=0.5, bias=half_par[:, 0:1]), "w")
                yield
                pf.need(act, "a", u)
                af.done(A(a[:], bank[1][:], ACT.Tanh, scale=0.5, bias=half_par[:, 1:2]), "a")
                yield
                if norm_:
                    square()
                yield

                def evac(name):
                    pf.need(act, name, u)
                    af.done(A(raw[PROJ.index(name)][:, 1 + h * HALF:1 + (h + 1) * HALF], bank[0][:], ACT.Copy), name)
                df.need(act, "from_mid", u)
                af.done(A(up[:], from_mid[:], ACT.Exp), "up")
                yield
                af.done(A(down[:], from_mid[:], ACT.Exp, scale=-1.0), "down")
                yield
                evac("k")
                yield
                df.need(act, "from_prev", u)
                af.done(A(prev[:], cum[:], ACT.Exp), "prev")
                yield
                if norm_:
                    variance()
                yield
                df.need(act, "k_mod", u)
                af.done(A(sq[:], kk[:], ACT.Square), "kk_sq")
                yield
                ab.need(act, f"s{NC - 1}", u, 2)
                af.done(A(sm[:, 2 * NC:3 * NC], sm[:, 0:NC], ACT.Exp), "mid")
                af.done(A(sm[:, 3 * NC:4 * NC], sm[:, NC:2 * NC], ACT.Exp), "decay")
                yield
                df.need(act, "norm_floor", u)
                af.done(A(norm[:], norm[:], ACT.Ln), "norm_log")
                if norm_:
                    var_log()
                yield
                af.need(act, "norm_log", u)
                af.done(A(norm[:], norm[:], ACT.Exp, scale=-0.5), "norm_inv")
                if norm_:
                    rstd()
                yield
                evac("r")
                yield
                evac("v")
                yield
                pf.need(act, "gate", u)
                dn.need(act, "out", u, 2)
                af.done(A(gate[h][:], bank[1][:], ACT.Copy), "gate")
                yield

            def back(p, h, fill):
                u = p * 2 + h
                for n, (out, name) in enumerate(((k_tok, "k_tok"), (b_tok, "b_tok"), (v_tok, "v_tok"))):
                    pb.need(act, name, u)
                    ab.done(A(out[:], bank[(4, 5, 7)[n]][:], ACT.Copy), name)
                gb.need(act, "a_lo1", u, 1)
                for b in ab2:
                    db.need(act, f"scores{4 * b + 3}", u)
                    ab.done(A(a_hi[b][:], scores[:, 4 * b:4 * b + 4, 0, :], ACT.Copy), f"a_hi{b}")
                _advance(fill, 1)
                for l in levels:
                    pb.need(act, f"inv{l}.0", u)
                    _advance(fill, (1, 1, 3, 1, 2, 2)[l - 1])
                for b in ab2:
                    pb.need(act, f"res{b}", u)
                    ab.done(A(prod[b][:].rearrange("p i t -> p (i t)"), bank[2 + b][:], ACT.Copy), f"res{b}")
                _advance(fill, 1)
                af.need(act, "decay", u)
                for c in range(NC):
                    pb.need(act, f"z{c}", u)
                    ab.done(A(z[:], bank[4][:, 0:P], ACT.Copy), f"z{c}")
                    _advance(fill, (1, 0, 0, 0)[c])
                    pb.need(act, f"s{c}", u)
                    ab.done(A(state[(c + 1) % 2][0:HEAD, 0:HEAD], bank[(6, 3)[c % 2]][0:HEAD, 0:HEAD], ACT.Copy,
                              scale=small[h][0:HEAD, 3 * NC + c:3 * NC + c + 1]), f"s{c}")
                pb.need(act, end, u)
                dn.need(act, "plus", u, 2)
                ab.done(A(y[h][:], bank[7][:], ACT.Copy), "y")
                _advance(fill, 100)

            walk(act, front, back)

        @block.vector
        def _(dve):
            V = nc.vector
            for x in stored:
                dve.sem_inc(x, 16)
            V.memset(eps[:], GN_EPS).then_inc(zeroed, 1)
            V.tensor_scalar(ident_r[:], ident[:], 1.0, None, ALU.mult).then_inc(zeroed, 1)
            V.tensor_scalar(minus_r[:], ident[:], -1.0, None, ALU.mult).then_inc(zeroed, 1)
            for x in raw:
                V.memset(x[:, 0:1], 0.0).then_inc(zeroed, 1)
            for x in state:
                V.memset(x[:], 0.0).then_inc(zeroed, 1)
            dve.wait_ge(zeroed, 8)
            dve.wait_ge(par_in, 16)
            df.start(dve)
            db.start(dve)
            dn.start(dve)
            ch = lambda x: x.rearrange("p (c t) -> p c t", c=NC)

            def front(p, h, norm_, next_=True):
                u = p * 2 + h
                par = lambda i: par_now[h][:, i:i + 1]

                def centre():
                    pn.need(dve, "mean", u - 2)
                    dn.done(V.scalar_tensor_tensor(y[h][:], bank[0][:], -1.0 / HEAD, y[h][:], ALU.mult, ALU.add), "centred")

                def norm_ends():
                    an.need(dve, "rstd", u - 2)
                    dn.done(V.tensor_tensor(y[h][:], y[h][:], ysq[:], ALU.mult), "n")
                    dn.need(dve, "n", u - 2)
                    dn.done(V.tensor_scalar(y[h][:], y[h][:], ln[h][:, 0:1], ln[h][:, 1:2], ALU.mult, ALU.add), "affine")
                    dn.need(dve, "affine", u - 2)
                    dn.done(V.tensor_tensor(y[h][:], y[h][:], bonus[h][:], ALU.add), "plus")
                    dn.need(dve, "plus", u - 2)
                    dve.wait_ge(stored[h], p * 16)
                    dn.done(V.tensor_tensor(y_out[h][:], y[h][:], gate[h][:], ALU.mult), "out")
                if not next_:
                    centre()
                    yield from (None,) * 8
                    norm_ends()
                    return
                pb.need(dve, end, u, 2)
                ab.need(dve, f"s{NC - 1}", u, 2)
                df.done(V.tensor_scalar(par_now[h][:], par_all[:, bass.ds(p, 1), :].rearrange("p o n -> p (o n)"), 1.0, None, ALU.mult), "par")
                af.need(dve, "a", u, 1)
                df.need(dve, "par", u)
                df.done(V.tensor_scalar(half_par[:], par_now[h][:, W0:A0 + 1], 0.5, None, ALU.mult), "half_par")
                yield
                if norm_:
                    centre()
                yield
                af.need(dve, "w", u)
                df.done(V.tensor_scalar(log_w[:], log_w[:], -0.5 * DECAY, -0.5 * DECAY, ALU.mult, ALU.add), "log_w")
                yield
                df.need(dve, "log_w", u)
                df.done(V.tensor_tensor_scan(cum[:], cst["restart"][:], log_w[:], 0.0, ALU.mult, ALU.add), "cum")
                yield
                pf.need(dve, "bonus", u, 1)
                _chunk_small(nc, dve, df, u, cum, from_mid, small[h])
                yield
                df.need(dve, "from_mid", u)
                df.done(V.tensor_tensor(cum[:], from_mid[:], log_w[:], ALU.subtract), "from_prev")
                yield
                af.need(dve, "a", u)
                df.done(V.tensor_scalar(a[:], a[:], 0.5, 0.5, ALU.mult, ALU.add), "a")
                df.need(dve, "a", u)
                df.done(V.tensor_scalar(gain[:], a[:], 1.0, par(K_A), ALU.subtract, ALU.mult), "k_gain")
                yield

                def shift(n, name, out):
                    gf.need(dve, f"{name}_diff", u)
                    df.done(V.scalar_tensor_tensor(out[:], diff[n][:], par((MU_K, MU_R, MU_V)[n]), raw[n][:, 1 + h * HALF:1 + (h + 1) * HALF],
                                                   ALU.mult, ALU.add), name)
                shift(0, "k", k)
                df.need(dve, "k", u)
                df.done(V.tensor_scalar(kk[:], k[:], par(K_K), None, ALU.mult), "kk")
                yield
                df.done(V.scalar_tensor_tensor(k[:], gain[:], 1.0, k[:], ALU.add, ALU.mult), "k_mod")
                yield
                af.need(dve, "down", u)
                df.need(dve, "k_mod", u)
                df.done(V.tensor_tensor(k_bar[h][:], k[:], down[:], ALU.mult), "k_bar")
                yield
                pf.need(dve, "norm", u)
                df.done(V.tensor_scalar(norm[:], bank[1][:], 1e-24, None, ALU.max), "norm_floor")
                yield
                af.need(dve, "norm_inv", u)
                df.done(V.tensor_tensor(kk[:], kk[:], norm[:], ALU.mult), "kk_unit")
                yield
                df.need(dve, "kk_unit", u)
                df.done(V.tensor_tensor(a[:], kk[:], a[:], ALU.mult), "b")
                df.need(dve, "b", u)
                df.done(V.tensor_tensor(b_bar[h][:], a[:], down[:], ALU.mult), "b_bar")
                yield
                if norm_:
                    norm_ends()
                yield
                af.need(dve, "prev", u)
                df.done(V.scalar_tensor_tensor(ar[h][:, :, 0, :], ch(kk[:]), -1.0, ch(prev[:]), ALU.mult, ALU.mult), "a_prev")
                yield
                shift(1, "r", r)
                yield
                df.need(dve, "r", u)
                af.need(dve, "up", u)
                df.done(V.tensor_tensor(ar[h][:, :, 1, :], ch(r[:]), ch(up[:]), ALU.mult), "r_up")
                yield
                df.done(V.scalar_tensor_tensor(rk[:], r[:], par(R_K), k[:], ALU.mult, ALU.mult), "rk")
                yield
                shift(2, "v", v[h])
                yield

            def back(p, h, fill):
                u = p * 2 + h
                level = lambda l: _over(cst["level_mask"][:, l, :], 4)
                tiled = lambda x: x.rearrange("p (i t) -> p i t", i=4)
                gb.need(dve, "a_lo1", u, 1)
                dve.wait_ge(scores_zeroed, 1)
                for j in range(2 * NC):
                    pb.need(dve, f"scores{j}", u)
                    V.memset(touch[:, j:j + 1], 0.0)
                    db.done(V.copy_predicated(scores[:, j].rearrange("p k t -> p (k t)"), cst["score_mask"][:],
                                              bank[(2, 6, 3)[j % 3]][:]), f"scores{j}")
                    if j == 1:
                        df.need(dve, "v", u)
                        pf.need(dve, "bonus", u)
                        df.done(V.tensor_tensor(bonus[h][:], bank[0][:], v[h][:], ALU.mult), "bonus")
                        df.done(V.tensor_scalar(ln[h][:], par_now[h][:, LN_W:LN_B + 1], 1.0, None, ALU.mult), "ln")
                for b in ab2:
                    db.need(dve, f"scores{4 * b + 3}", u)
                    db.done(V.tensor_tensor(invT[b][:], scores[:, 4 * b:4 * b + 4, 0, :], level(0), ALU.mult), f"invT_mask{b}")
                    db.need(dve, f"invT_mask{b}", u)
                    db.done(V.tensor_tensor(invT[b][:], invT[b][:].bitcast(F32), _over(ident[:], 4), ALU.add), f"invT0.{b}")
                    if b == 0:
                        _advance(fill, 2)
                for b in ab2:
                    pb.need(dve, f"inv0.{b}", u)
                    db.done(V.tensor_copy(inv[b][:].rearrange("p i t -> p (i t)"), bank[4 + b][:]), f"inv0.{b}")
                for l in levels:
                    for b in ab2:
                        pb.need(dve, f"prod{l}.{b}", u)
                        db.done(V.tensor_tensor(prod[b][:], tiled(bank[2 + b][:]), level(l), ALU.mult), f"prod{l}.{b}")
                    _advance(fill, (2, 2, 1, 1, 2, 1)[l - 1])
                    for b in ab2:
                        pb.need(dve, f"inv{l}.{b}", u)
                        db.done(V.tensor_tensor(inv[b][:], tiled(bank[5 + 2 * b][:]), inv[b][:].bitcast(F32), ALU.add), f"inv{l}.{b}")
                    for b in ab2:
                        db.done(V.tensor_tensor(invT[b][:], tiled(bank[4 + 2 * b][:]), invT[b][:].bitcast(F32), ALU.add), f"invT{l}.{b}")
                for b in ab2:
                    pb.need(dve, f"inverse{b}", u)
                    db.done(V.tensor_copy(inverseT[b][:].rearrange("p i t -> p (i t)"), bank[4 + 2 * b][:]), f"inverse{b}")
                for hd in range(2):
                    hs = slice(hd * HEAD, (hd + 1) * HEAD)
                    if h == 0:
                        db.done(V.memset(state[0][hs, hs], 0.0), f"start{hd}")
                    else:
                        af.need(dve, "mid", u)
                        db.done(V.tensor_scalar(state[0][hs, hs], state[0][hs, hs], small[h][hs, 2 * NC:2 * NC + 1], None, ALU.mult), f"start{hd}")
                low = slice(HEAD, P)
                for c in range(NC):
                    pb.need(dve, f"u{c}", u)
                    db.done(V.tensor_copy(uu[:], bank[5][:, 0:P]), f"u{c}")
                    pb.need(dve, f"s{c}", u)
                    if c == 0:
                        af.need(dve, "decay", u)
                    db.done(V.tensor_scalar(state[(c + 1) % 2][low, low], bank[(6, 3)[c % 2]][low, low],
                                            small[h][low, 3 * NC + c:3 * NC + c + 1], None, ALU.mult), f"s{c}")
                    _advance(fill, (2, 2, 2, 1)[c])
                _advance(fill, 100)

            walk(dve, front, back)


def _merge(nc, sems, d, mixT, w_out, w_out_in):
    with ExitStack() as ctx:
        sb = lambda n, s, dt=F32: ctx.enter_context(nc.sbuf_tensor(n, s, dt))
        NAMES, SRC = ("ga", "gb", "gla", "rwkv"), (0, 0, 1, 2)
        STREAMS = ("h_spill", "y_gla", "y_rwkv")
        s_hi, s_lo = ([sb(f"m_{n}_{x}", [P, KT, HALF], F32R) for n in STREAMS] for x in ("hi", "lo"))
        w_hi, w_lo = ([sb(f"m_w_{x}{i}", [P, D], F32R) for i in range(2)] for x in ("hi", "lo"))
        w_raw = [sb(f"m_w_raw{i}", [P, D]) for i in range(2)]
        s_raw = [sb(f"m_s_raw{i}", [P, 2, HALF]) for i in range(3)]
        gate = [sb(f"m_g{x}", [P, HALF]) for x in range(2)]
        bank = [ctx.enter_context(nc.psum_tensor(f"m_ps{i}", [P, HALF], F32)) for i in range(4)]
        w_in = [sems.enter_context(nc.semaphore(f"m_w_in{i}")) for i in range(2)]
        s_in = [sems.enter_context(nc.semaphore(f"m_s_in{i}")) for i in range(3)]
        pe_s = Steps(nc, sems, "m_pe", NAMES)
        act_s = Steps(nc, sems, "m_act", ("ga", "gb"))
        dve_s = Steps(nc, sems, "m_dve", ("sa", "sb", "ma", "mb", "mix"))
        act_w, dve_w = (Steps(nc, sems, f"m_{x}_weights", NAMES) for x in ("act", "dve"))
        tiles = [f"{x}.{j}" for x in range(3) for j in range(4)]
        act_t, dve_t = (Steps(nc, sems, f"m_{x}_streams", tiles) for x in ("act", "dve"))
        block = ctx.enter_context(nc.Block())

        def walk(eng, begin, unit):
            begin()
            for half in range(2):
                u = half * KT
                unit(half, 0, u, (1, 2), True)
                with eng.Fori(1, KT - 1) as n:
                    unit(half, n, n + u, (None, None), True)
                unit(half, KT - 1, u + KT - 1, (None, 0 if half == 0 else None), half == 0)

        @block.sync
        def _(sp):
            def weight(q, u, n):
                (dve_w.need_before if q < 2 else dve_w.need)(sp, NAMES[q - 2], u)
                sp.dma_start(w_raw[q % 2][:], d["w_merge"][bass.ds(n * 4 + q, 1)].rearrange("o p k n -> p (o k n)")).then_inc(w_in[q % 2], 16)

            def stream(x, half):
                for j in range(4):
                    i = 4 * x + j
                    (dve_t.need_before if i < 3 else dve_t.need)(sp, tiles[i - 3], half)
                    sp.dma_start(s_raw[i % 3][:], d[STREAMS[x]][2 * j:2 * j + 2, :, half * HALF:(half + 1) * HALF].rearrange("k p t -> p k t")).then_inc(s_in[i % 3], 16)

            def begin():
                weight(0, 0, 0)
                stream(0, 0)
                weight(1, 0, 0)

            def unit(half, n, u, streams, next_):
                if streams[0] is not None:
                    stream(streams[0], half)
                weight(2, u, n)
                weight(3, u, n)
                if streams[1] is not None:
                    stream(streams[1], half if streams[1] else half + 1)
                if next_:
                    following = 0 if isinstance(n, int) and n == KT - 1 else n + 1
                    weight(0, u + 1, following)
                    weight(1, u + 1, following)
                if half == 1 and isinstance(n, int) and n == 0:
                    sp.dma_start(w_out[:], d["w_out"]).then_inc(w_out_in, 16)
            walk(sp, begin, unit)

        @block.tensor
        def _(pe):
            pe_s.start(pe)

            def unit(half, n, u, streams, next_):
                first = isinstance(n, int) and n == 0
                for q, name in enumerate(NAMES):
                    x = SRC[q]
                    dve_w.need(pe, name, u)
                    dve_s.need(pe, ("sa", "sb", "ma", "mb")[q], u, 1)
                    for k in range(KT):
                        if first and q != 1 and k % 2 == 0:
                            dve_t.need(pe, f"{x}.{k // 2}", half)
                        cols = slice(k * P, (k + 1) * P)
                        mm = _product(pe, bank[q][:], w_hi[q % 2][:, cols], w_lo[q % 2][:, cols], s_hi[x][:, k, :], s_lo[x][:, k, :],
                                      k == 0, k == KT - 1)
                    pe_s.done(mm, name)
            walk(pe, lambda: None, unit)

        def split_all(eng, weight, stream, gate_a, gate_b, end_a, end_b):
            def begin():
                weight(0, 0)
                stream(0, 0)
                weight(1, 0)

            def unit(half, n, u, streams, next_):
                if streams[0] is not None:
                    stream(streams[0], half)
                gate_a(u)
                weight(2, u)
                gate_b(u)
                weight(3, u)
                if streams[1] is not None:
                    stream(streams[1], half if streams[1] else half + 1)
                end_a(u)
                if next_:
                    weight(0, u + 1)
                end_b(half, n, u)
                if next_:
                    weight(1, u + 1)
            walk(eng, begin, unit)

        @block.scalar
        def _(act):
            act_s.start(act)
            act_w.start(act)
            act_t.start(act)

            def weight(q, u):
                pe_s.need(act, NAMES[q - 2], u, 1 if q < 2 else 0)
                act.wait_ge(w_in[q % 2], u * 32 + 16 * (q // 2 + 1))
                act_w.done(nc.scalar.activation(w_hi[q % 2][:], w_raw[q % 2][:], ACT.Copy), NAMES[q])

            def stream(x, half):
                if half:
                    pe_s.need(act, ("gb", "gla", "rwkv")[x], half * KT, 1)
                for j in range(4):
                    i = 4 * x + j
                    act.wait_ge(s_in[i % 3], 16 * (4 * half + i // 3 + 1))
                    act_t.done(nc.scalar.activation(s_hi[x][:, 2 * j:2 * j + 2, :], s_raw[i % 3][:], ACT.Copy), tiles[i])

            def gating(x):
                def tanh(u):
                    pe_s.need(act, NAMES[x], u)
                    dve_s.need(act, "mix", u, 1)
                    act_s.done(nc.scalar.activation(gate[x][:], bank[x][:], ACT.Tanh, scale=0.5), NAMES[x])
                return tanh
            split_all(act, weight, stream, gating(0), gating(1), lambda u: None, lambda *a: None)

        @block.vector
        def _(dve):
            V = nc.vector
            dve_s.start(dve)
            dve_w.start(dve)
            dve_t.start(dve)

            def weight(q, u):
                act_w.need(dve, NAMES[q], u)
                dve_w.done(V.tensor_tensor(w_lo[q % 2][:], w_raw[q % 2][:], w_hi[q % 2][:].bitcast(F32), ALU.subtract), NAMES[q])

            def stream(x, half):
                for j in range(4):
                    i, ks = 4 * x + j, slice(2 * j, 2 * j + 2)
                    act_t.need(dve, tiles[i], half)
                    dve_t.done(V.tensor_tensor(s_lo[x][:, ks, :], s_raw[i % 3][:], s_hi[x][:, ks, :].bitcast(F32), ALU.subtract), tiles[i])

            def gating(x):
                def half_(u):
                    act_s.need(dve, NAMES[x], u)
                    dve_s.done(V.tensor_scalar(gate[x][:], gate[x][:], 0.5, 0.5, ALU.mult, ALU.add), ("sa", "sb")[x])
                return half_

            def product(x, u):
                pe_s.need(dve, NAMES[2 + x], u)
                dve_s.need(dve, ("sa", "sb")[x], u)
                dve_s.done(V.tensor_tensor(gate[x][:], bank[2 + x][:], gate[x][:], ALU.mult), ("ma", "mb")[x])

            def mix(half, n, u):
                product(1, u)
                dve_s.need(dve, "mb", u)
                dve_s.done(V.tensor_tensor(mixT[:, bass.ds(n, 1), half * HALF:(half + 1) * HALF].rearrange("p o t -> p (o t)"),
                                           gate[0][:], gate[1][:], ALU.add), "mix")
            split_all(dve, weight, stream, gating(0), gating(1), lambda u: product(0, u), mix)
            dve_s.need(dve, "mix", 2 * KT - 1)


def _residual(nc, sems, d, mixT, w, w_in, x1, h2T_hi, h2T_lo, first_raw, raw_in, cst):
    ident = cst["ident"]
    with ExitStack() as ctx:
        sb = lambda n, s: ctx.enter_context(nc.sbuf_tensor(n, s, F32))
        h2 = sb("o_h2", [P, KT, D])
        ss, rs = sb("o_ss", [P, 8]), sb("o_rs", [P, 8])
        bank = [ctx.enter_context(nc.psum_tensor(f"o_ps{i}", [P, HALF], F32)) for i in range(8)]
        sem = lambda n: sems.enter_context(nc.semaphore(n))
        product, added, squares, mean_eps, root, rstd, scaled, turned, evacuated, high = map(
            sem, ("o_product", "o_added", "o_squares", "o_mean", "o_root", "o_rstd", "o_scaled", "o_turned", "o_evac", "o_high"))
        x_in = [sem(f"o_x_in{t}") for t in range(KT)]
        block = ctx.enter_context(nc.Block())

        @block.sync
        def _(sp):
            for t in range(KT):
                sp.dma_start(x1[:, t, :], d["x"][t * P:(t + 1) * P, :]).then_inc(x_in[t], 16)
            for i in range(2):
                sp.dma_start(first_raw[i][:], d["w_up"][i:i + 1].rearrange("o p k n -> p (o k n)")).then_inc(raw_in[2 + i], 16)

        @block.tensor
        def _(pe):
            def transposes(h):
                for k in range(KT):
                    n = h * KT + k
                    if k == 0:
                        pe.wait_ge(scaled, 4 * h + 4)
                    if n >= 4:
                        pe.wait_ge(evacuated, n - 3)
                    for j in range(4):
                        mm = pe.transpose(bank[4 + n % 4][:, j * P:(j + 1) * P], h2[:, 4 * h + j, k * P:(k + 1) * P], ident[:])
                    mm.then_inc(turned, 1)
            pe.wait_ge(w_in, 16)
            for t in range(KT):
                if t == 6:
                    transposes(0)
                for e in range(2):
                    n = 2 * t + e
                    if n >= 4:
                        pe.wait_ge(added, n - 3)
                    for k in range(KT):
                        mm = pe.matmul(bank[n % 4][:], mixT[:, k, t * P:(t + 1) * P], w[:, k, e * HALF:(e + 1) * HALF],
                                       start=k == 0, stop=k == KT - 1)
                    mm.then_inc(product, 1)
            transposes(1)

        @block.vector
        def _(dve):
            def low_parts(h):
                for k in range(KT):
                    n = h * KT + k
                    dve.wait_ge(high, n + 1)
                    s = slice(h * HALF, (h + 1) * HALF)
                    nc.vector.scalar_tensor_tensor(h2T_lo[:, k, s], bank[4 + n % 4][:], cst["norms"][:, 8 + k:9 + k],
                                                   h2T_hi[:, k, s].bitcast(F32), ALU.mult, ALU.subtract).then_inc(evacuated, 1)
            for t in range(KT):
                c = slice(t, t + 1)
                dve.wait_ge(x_in[t], 16)
                if t == 6:
                    low_parts(0)
                for e in range(2):
                    n = 2 * t + e
                    dve.wait_ge(product, n + 1)
                    s = slice(e * HALF, (e + 1) * HALF)
                    nc.vector.tensor_tensor(x1[:, t, s], bank[n % 4][:], x1[:, t, s], ALU.add).then_inc(added, 1)
                dve.wait_ge(squares, t + 1)
                nc.vector.tensor_scalar(ss[:, c], ss[:, c], 1.0 / D, NORM_EPS, ALU.mult, ALU.add).then_inc(mean_eps, 1)
                dve.wait_ge(root, t + 1)
                nc.vector.reciprocal(rs[:, c], rs[:, c]).then_inc(rstd, 1)
                dve.wait_ge(rstd, t + 1)
                nc.vector.tensor_scalar(h2[:, t, :], x1[:, t, :], rs[:, c], None, ALU.mult).then_inc(scaled, 1)
            low_parts(1)
            dve.wait_ge(evacuated, 2 * KT)

        @block.scalar
        def _(act):
            def high_parts(h):
                for k in range(KT):
                    n = h * KT + k
                    act.wait_ge(turned, n + 1)
                    nc.scalar.activation(h2T_hi[:, k, h * HALF:(h + 1) * HALF], bank[4 + n % 4][:], ACT.Copy,
                                         scale=cst["norms"][:, 8 + k:9 + k]).then_inc(high, 1)
            for t in range(KT):
                if t == 6:
                    high_parts(0)
                act.wait_ge(added, 2 * t + 2)
                nc.scalar.activation(h2[:, t, :], x1[:, t, :], ACT.Square, accum_out=ss[:, t:t + 1]).then_inc(squares, 1)
                act.wait_ge(mean_eps, t + 1)
                nc.scalar.activation(rs[:, t:t + 1], ss[:, t:t + 1], ACT.Sqrt).then_inc(root, 1)
            high_parts(1)


def _mlp(nc, sems, d, h2T_hi, h2T_lo, x1, first_raw, raw_in):
    with ExitStack() as ctx:
        sb = lambda n, s, dt=F32: ctx.enter_context(nc.sbuf_tensor(n, s, dt))
        raw = [sb(f"f_raw{i}", [P, D]) for i in range(2)] + first_raw
        up_hi, up_lo = ([sb(f"f_up_{x}{i}", [P, D], F32R) for i in range(2)] for x in ("hi", "lo"))
        down_hi, down_lo = (sb(f"f_down_{x}", [P, FF_TILES, D], F32R) for x in ("hi", "lo"))
        hid_hi, hid_lo = (sb(f"f_hid_{x}", [P, FF_TILES, SEQ], F32R) for x in ("hi", "lo"))
        relu = [sb(f"f_relu{i}", [P, HALF]) for i in range(2)]
        gain, ss, rs = sb("f_gain", [P, D]), sb("f_ss", [P, KT]), sb("f_rs", [P, KT])
        gain_in = sems.enter_context(nc.semaphore("f_gain_in"))
        norm_a = Steps(nc, sems, "f_act_norm", ["squares", "root"])
        norm_d = Steps(nc, sems, "f_dve_norm", ["mean", "rstd", "out"])
        stored = [sems.enter_context(nc.semaphore(f"f_stored{i}")) for i in range(2)]
        bank = [ctx.enter_context(nc.psum_tensor(f"f_ps{i}", [P, HALF], F32)) for i in range(8)]
        NU, ND, last = 2 * FF_TILES, 2 * KT, FF_GROUPS - 1
        after = [["u2", "d0"], ["u3", "d1"], ["d2", "d3"], []]
        slot = {"u2": (0, 0), "d0": (1, 0), "u3": (2, 1), "d1": (3, 1), "d2": (0, 1), "d3": (1, 1), "u0": (2, 0), "u1": (3, 0)}
        steps = lambda *x: [n for t in range(FF_TILES) for n in [f"{y}{2 * t + h}" for h in range(2) for y in x] + after[t]]
        pe_s = Steps(nc, sems, "f_pe", [f"up{n}" for n in range(NU)] + [f"down{n}" for n in range(ND)])
        act_s = Steps(nc, sems, "f_act", steps("relu", "hid"))
        dve_s = Steps(nc, sems, "f_dve", steps("sq", "hid") + [f"add{n}" for n in range(ND)])
        act_n = Steps(nc, sems, "f_act_next", ["u0", "u1"])
        dve_n = Steps(nc, sems, "f_dve_next", ["u0", "u1"])
        block = ctx.enter_context(nc.Block())

        def parts(name):
            i = int(name[1])
            return (up_hi[i % 2][:], up_lo[i % 2][:]) if name[0] == "u" else (down_hi[:, i, :], down_lo[:, i, :])

        def act_split(act, s, name, g):
            b, before = slot[name]
            act.wait_ge(raw_in[b], g * 32 + 16 * (before + 1))
            s.done(nc.scalar.activation(parts(name)[0], raw[b][:], ACT.Copy), name)

        def dve_split(dve, s, other, name, g):
            hi, lo = parts(name)
            other.need(dve, name, g)
            s.done(nc.vector.tensor_tensor(lo, raw[slot[name][0]][:], hi.bitcast(F32), ALU.subtract), name)

        @block.sync
        def _(sp):
            def load(name, g):
                i = int(name[1])
                src = d["w_up"][bass.ds(g * FF_TILES + i, 1)].rearrange("o p k n -> p (o k n)") if name[0] == "u" \
                    else d["w_down"][bass.ds(g * FF_TILES + i, 1)].rearrange("o p n -> p (o n)")
                b = slot[name][0]
                sp.dma_start(raw[b][:], src).then_inc(raw_in[b], 16)

            def group(g, next_):
                dve_s.need_before(sp, "d2", g)
                load("u2", g)
                dve_s.need_before(sp, "d3", g)
                load("d0", g)
                dve_n.need(sp, "u0", g)
                load("u3", g)
                dve_n.need(sp, "u1", g)
                load("d1", g)
                dve_s.need(sp, "u2", g)
                load("d2", g)
                dve_s.need(sp, "d0", g)
                load("d3", g)
                if next_:
                    dve_s.need(sp, "u3", g)
                    load("u0", g + 1)
                    dve_s.need(sp, "d1", g)
                    load("u1", g + 1)
            sp.dma_start(gain[:], d["norm_final"]).then_inc(gain_in, 16)
            with sp.Fori(0, last) as g:
                group(g, True)
            group(last, False)
            for t in range(KT):
                norm_d.need(sp, "out", t)
                sp.dma_start(d["out"][t * P:(t + 1) * P, :], raw[2 + t % 2][:]).then_inc(stored[t % 2], 16)
            for x in stored:
                sp.wait_ge(x, 16 * KT // 2)

        @block.tensor
        def _(pe):
            pe_s.start(pe)
            with pe.Fori(0, FF_GROUPS) as g:
                for n in range(NU):
                    t, h = n // 2, n % 2
                    tok = slice(h * HALF, (h + 1) * HALF)
                    if h == 0:
                        (dve_n if t < 2 else dve_s).need(pe, f"u{t}", g)
                    dve_s.need_before(pe, f"add{ND - 8 + n}", g)
                    for k in range(KT):
                        cols = slice(k * P, (k + 1) * P)
                        hi, lo = up_hi[t % 2][:, cols], up_lo[t % 2][:, cols]
                        mm = _product(pe, bank[n][:], hi, lo, h2T_hi[:, k, tok], h2T_lo[:, k, tok], k == 0, k == KT - 1)
                    pe_s.done(mm, f"up{n}")
                dve_s.need(pe, f"d{FF_TILES - 1}", g)
                for t in range(KT):
                    for e in range(2):
                        n = 2 * t + e
                        if n < 8:
                            act_s.need(pe, f"relu{n}", g)
                        else:
                            dve_s.need(pe, f"add{n - 8}", g)
                    for k in range(FF_TILES):
                        if t == 0 and k == FF_TILES - 1:
                            dve_s.need(pe, f"hid{NU - 1}", g)
                        hi, lo = hid_hi[:, k, t * P:(t + 1) * P], hid_lo[:, k, t * P:(t + 1) * P]
                        for e in range(2):
                            w = slice(e * HALF, (e + 1) * HALF)
                            mm = _product(pe, bank[(2 * t + e) % 8][:], hi, lo, down_hi[:, k, w], down_lo[:, k, w], k == 0, k == FF_TILES - 1)
                            if k == FF_TILES - 1:
                                pe_s.done(mm, f"down{2 * t + e}")

        @block.scalar
        def _(act):
            act_s.start(act)
            act_n.start(act)

            def first_tiles(g):
                for name in ("u0", "u1"):
                    act_split(act, act_n, name, g)

            def group(g):
                for n in range(NU):
                    t, h = n // 2, n % 2
                    pe_s.need(act, f"up{n}", g)
                    if n < 2:
                        dve_s.need_before(act, f"hid{NU - 2 + n}", g)
                    else:
                        dve_s.need(act, f"hid{n - 2}", g)
                    act_s.done(nc.scalar.activation(relu[n % 2][:], bank[n][:], ACT.Relu), f"relu{n}")
                    dve_s.need(act, f"sq{n}", g)
                    act_s.done(nc.scalar.activation(hid_hi[:, t, h * HALF:(h + 1) * HALF], relu[n % 2][:], ACT.Copy), f"hid{n}")
                    for name in after[t] if h else ():
                        act_split(act, act_s, name, g)
            first_tiles(0)
            with act.Fori(0, last) as g:
                group(g)
                first_tiles(g + 1)
            group(last)
            norm_a.start(act)
            for t in range(KT):
                dve_s.need(act, f"add{2 * t + 1}", last)
                if t == 0:
                    dve_s.need(act, "d3", last)
                else:
                    norm_a.need(act, "squares", t - 1)
                norm_a.done(nc.scalar.activation(raw[0][:], x1[:, t, :], ACT.Square, accum_out=ss[:, t:t + 1]), "squares")
                norm_d.need(act, "mean", t)
                norm_a.done(nc.scalar.activation(rs[:, t:t + 1], ss[:, t:t + 1], ACT.Sqrt), "root")

        @block.vector
        def _(dve):
            dve_s.start(dve)
            dve_n.start(dve)
            V = nc.vector

            def first_tiles(g):
                for name in ("u0", "u1"):
                    dve_split(dve, dve_n, act_n, name, g)

            def group(g, next_):
                for n in range(NU):
                    t, h = n // 2, n % 2
                    act_s.need(dve, f"relu{n}", g)
                    dve_s.done(V.tensor_tensor(relu[n % 2][:], relu[n % 2][:], relu[n % 2][:], ALU.mult), f"sq{n}")
                    act_s.need(dve, f"hid{n}", g)
                    dve_s.done(V.tensor_tensor(hid_lo[:, t, h * HALF:(h + 1) * HALF], relu[n % 2][:],
                                               hid_hi[:, t, h * HALF:(h + 1) * HALF].bitcast(F32), ALU.subtract), f"hid{n}")
                    for name in after[t] if h else ():
                        dve_split(dve, dve_s, act_s, name, g)
                for n in range(ND):
                    t, s = n // 2, slice((n % 2) * HALF, (n % 2 + 1) * HALF)
                    pe_s.need(dve, f"down{n}", g)
                    dve_s.done(V.tensor_tensor(x1[:, t, s], bank[n % 8][:], x1[:, t, s], ALU.add), f"add{n}")
                    if n == 3 and next_:
                        first_tiles(g + 1)
                    if n % 2 and not next_:
                        finish(t)

            def finish(t):
                norm_a.need(dve, "squares", t)
                c = slice(t, t + 1)
                norm_d.done(V.tensor_scalar(ss[:, c], ss[:, c], 1.0 / D, NORM_EPS, ALU.mult, ALU.add), "mean")
                norm_a.need(dve, "root", t)
                norm_d.done(V.reciprocal(rs[:, c], rs[:, c]), "rstd")
                norm_d.need(dve, "rstd", t)
                if t == 0:
                    dve.wait_ge(gain_in, 16)
                if t >= 2:
                    dve.wait_ge(stored[t % 2], 16 * (t // 2))
                norm_d.done(V.scalar_tensor_tensor(raw[2 + t % 2][:], x1[:, t, :], rs[:, c], gain[:], ALU.mult, ALU.mult), "out")
            norm_d.start(dve)
            first_tiles(0)
            with dve.Fori(0, last) as g:
                group(g, True)
            group(last, False)
            dve_s.need(dve, f"add{ND - 1}", last)


def build(nc, d):
    with ExitStack() as outer, ExitStack() as sems:
        sb = lambda ctx, n, s, dt=F32: ctx.enter_context(nc.sbuf_tensor(n, s, dt))
        cst = {n: sb(outer, f"c_{n}", s) for n, s in (("ident", [P, P]), ("ones", [P, P]), ("norms", [P, 18]))}
        far = lambda ctx, n, dt=F32: ctx.enter_context(nc.sbuf_tensor(n, [P, KT, SEQ], dt, side="right"))
        mix_stream = ExitStack()
        with ExitStack() as mixers:
            cst.update({n: sb(mixers, f"c_{n}", s) for n, s in (("block_ones", [P, P]), ("level_mask", [P, 7, P]), ("restart", [P, HALF]))})
            cst["score_mask"] = sb(mixers, "c_score_mask", [P, 4 * P], U32)
            lora_wa, lora_g = sb(mixers, "lora_wa", [P, SEQ]), sb(mixers, "lora_g", [P, SEQ])
            with ExitStack() as low:
                hT_hi, hT_lo = (sb(low, f"hT_{x}", [P, KT, SEQ], F32R) for x in ("hi", "lo"))
                gla_al = sb(low, "gla_al", [RANK, SEQ])
                with ExitStack() as lora_ctx:
                    w_hi, w_lo = (sb(lora_ctx, f"lora_w_{x}", [P, KT, 272], F32R) for x in ("hi", "lo"))
                    _prepare(nc, sems, d, hT_hi, hT_lo, w_hi, w_lo, cst)
                    _low_rank(nc, sems, hT_hi, hT_lo, w_hi, w_lo, lora_wa, lora_g, gla_al, cst["norms"])
                _gla(nc, sems, d, hT_hi, hT_lo, gla_al, d["y_gla"], cst)
                hT = far(mix_stream, "hT")
                _whole(nc, sems, hT_hi, hT_lo, hT)
            _rwkv(nc, sems, d, hT, lora_wa, lora_g, d["y_rwkv"], cst)
        mix_stream.close()
        with ExitStack() as mlp_stream:
            with ExitStack() as ctx:
                mixT, w_out = sb(ctx, "mixT", [P, KT, SEQ]), sb(ctx, "w_out", [P, KT, D])
                w_out_in = sems.enter_context(nc.semaphore("w_out_in"))
                _merge(nc, sems, d, mixT, w_out, w_out_in)
                x1 = mlp_stream.enter_context(nc.sbuf_tensor("x1", [P, KT, D], F32, side="right"))
                h2_hi, h2_lo = (far(mlp_stream, n, F32R) for n in ("h2_hi", "h2_lo"))
                first_raw = [mlp_stream.enter_context(nc.sbuf_tensor(f"f_raw{i}", [P, D], F32, side="right")) for i in (2, 3)]
                raw_in = [sems.enter_context(nc.semaphore(f"f_raw_in{i}")) for i in range(4)]
                _residual(nc, sems, d, mixT, w_out, w_out_in, x1, h2_hi, h2_lo, first_raw, raw_in, cst)
            _mlp(nc, sems, d, h2_hi, h2_lo, x1, first_raw, raw_in)


def _tiles(np, w, width):
    r, c = w.shape
    return np.ascontiguousarray(w.reshape(r // P, P, c // width, width).transpose(2, 1, 0, 3))


def kernel(**inputs):
    import numpy as np
    import concourse.bacc as bacc
    from concourse.bass_utils import run_bass_kernel_spmd

    a = {k: np.asarray(v) for k, v in inputs.items()}
    w_in = a["w_in"][0]
    cols = lambda lo, n: w_in[:, lo:lo + n]
    gq, gk, gv, gog, gal = 0, 512, 1024, 2048, 3072
    rr = 3088
    rk, rv, rwl, rgl = rr + 1024, rr + 2048, rr + 3072, rr + 3200
    ga, gb = rr + 3328, rr + 4352
    group = lambda n, parts: np.concatenate([np.concatenate([cols(o + i * s, s) for o, s in parts], 1) for i in range(n)], 1)
    per_channel = lambda v: np.ascontiguousarray(v.reshape(-1, P).T)
    mu = a["rwkv_mu"][0]
    pair = np.stack([v.reshape(-1, P) for v in (mu[0:1024], mu[1024:2048], mu[2048:3072], a["rwkv_w0"][0], a["rwkv_a0"][0],
                                                a["rwkv_k_k"][0], a["rwkv_k_a"][0], a["rwkv_r_k"][0].reshape(-1),
                                                a["rwkv_ln_w"][0], a["rwkv_ln_b"][0])], -1)
    wa2 = np.concatenate([a["rwkv_w_w2"][0], a["rwkv_a_w2"][0]], 0).reshape(P, 8, P).transpose(1, 0, 2)
    g2 = a["rwkv_g_w2"][0].reshape(P, 8, P).transpose(1, 0, 2)
    i, j = np.arange(P)[:, None], np.arange(P)[None, :]
    strict, incl = (j > i), (j >= i)
    levels = [(j % 2 == 1) & (i == j - 1)] + [((i >> l) % 2 == 1) & ((j >> l) == (i >> l) - 1) for l in range(1, 7)]
    merge = np.stack([_tiles(np, m, P) for m in (cols(ga, 1024), cols(gb, 1024), a["w_branch_gla"][0], a["w_branch_rwkv"][0])], 1)
    arrays = {
        "x": a["x"][0],
        "w_gla": _tiles(np, group(4, ((gk, 128), (gq, 128), (gog, 256))), P),
        "w_gla_v": _tiles(np, cols(gv, 1024), GLA_DV),
        "w_rwkv": _tiles(np, group(8, ((rk, 128), (rr, 128), (rv, 128))), P),
        "w_lora": _tiles(np, np.concatenate([cols(rwl, 256), cols(gal, 16)], 1), 272)[0],
        "w_merge": merge.reshape(32, P, KT, P),
        "w_out": _tiles(np, a["w_out"][0], D)[0],
        "w_up": _tiles(np, a["w_up"][0], P),
        "w_down": a["w_down"][0].reshape(-1, P, D),
        "gla_a_w2": np.ascontiguousarray(a["gla_a_w2"][0].reshape(RANK, 4, P).transpose(1, 0, 2)),
        "gla_par": np.ascontiguousarray(np.concatenate([a["gla_a_b"][0].reshape(4, P, 1),
                                                        np.broadcast_to(per_channel(a["gla_norm"][0]), (4, P, 2))], 2).transpose(1, 0, 2)),
        "rwkv_lora2": np.ascontiguousarray(wa2),
        "rwkv_g2": np.ascontiguousarray(g2),
        "rwkv_par": np.ascontiguousarray(pair.transpose(1, 0, 2)),
        "norms": np.concatenate([per_channel(a["norm_mix"][0]), per_channel(a["norm_mlp"][0]), per_channel(mu[3072:3328])], 1),
        "norm_final": np.ascontiguousarray(np.broadcast_to(a["norm_final"], (P, D))),
        "ident": np.eye(P, dtype=np.float32),
        "ones": np.ones((P, P), np.float32),
        "block_ones": (i // HEAD == j // HEAD).astype(np.float32),
        "level_mask": np.ascontiguousarray(np.stack(levels, 1).astype(np.float32)),
        "score_mask": np.concatenate([strict, incl, strict, incl], 1).astype(np.uint32),
        "restart": np.ascontiguousarray(np.broadcast_to((np.arange(HALF) % CHUNK != 0).astype(np.float32), (P, HALF))),
    }
    nc = bacc.Bacc("TRN2", target_bir_lowering=False, num_devices=1)
    d = {n: nc.dram_tensor(f"in_{n}", v.shape, mybir.dt.from_np(v.dtype), kind="ExternalInput").ap() for n, v in arrays.items()}
    d["out"] = nc.dram_tensor("out", (SEQ, D), F32, kind="ExternalOutput").ap()
    d["y_gla"] = nc.dram_tensor("y_gla", (KT, P, SEQ), F32, kind="Internal").ap()
    d["h_spill"] = nc.dram_tensor("h_spill", (KT, P, SEQ), F32, kind="Internal").ap()
    d["y_rwkv"] = nc.dram_tensor("y_rwkv", (RWKV_PAIRS, P, SEQ), F32, kind="Internal").ap()
    build(nc, d)
    r = run_bass_kernel_spmd(nc, [{f"in_{n}": v for n, v in arrays.items()}], core_ids=[0])
    return r.results[0]["out"].reshape(1, SEQ, D)
```
